# Optimizing a Trainium2 kernel written in Bass

```python
import jax, jax.numpy as jnp
from jax import lax
import numpy as np

D_MODEL = 1024
BATCH = 1
SEQ = 1024
DEPTH = 1

N_HEADS = 8
HEAD_DIM = 64
ATTN_WIDTH = N_HEADS * HEAD_DIM
DILATED_PATTERNS = ((128, 1), (512, 4), (2048, 16))
ATTN_BLOCK = 128
POOL_WINDOWS = (2, 4, 8, 16)
N_POOL_GROUPS = len(POOL_WINDOWS)
POOL_GROUP_DIM = 128
POOL_WIDTH = N_POOL_GROUPS * POOL_GROUP_DIM
N_BRANCHES = 2
IN_PROJ_WIDTH = 3 * ATTN_WIDTH + POOL_WIDTH + N_BRANCHES * D_MODEL
N_EXPERT_GROUPS = 4
EXPERTS_PER_GROUP = 8
N_EXPERTS = N_EXPERT_GROUPS * EXPERTS_PER_GROUP
TOP_K = 2
EXPERT_HIDDEN = 512
MOE_BLOCK = 128
RMS_EPS = 1e-6
NEG_INF = -1e30

kernel_name = "hybrid_dilated_attn_pool_hmoe"

def _rmsnorm(x, g):
    xf = x.astype(jnp.float32)
    y = xf * lax.rsqrt(jnp.mean(xf * xf, axis=-1, keepdims=True) + RMS_EPS)
    return (y * g.astype(jnp.float32)).astype(x.dtype)

def _dilated_branch(q, k, v, window, dilation):
    b_, h_, s_, e_ = q.shape
    steps = window // dilation
    span = dilation * ATTN_BLOCK
    s_pad = -(-s_ // span) * span
    n_strided = s_pad // dilation
    n_blk = n_strided // ATTN_BLOCK

    def to_blocks(t):
        t = jnp.pad(t, ((0, 0), (0, 0), (0, s_pad - s_), (0, 0)))
        t = t.reshape(b_, h_, n_strided, dilation, e_).transpose(0, 1, 3, 2, 4)
        return t.reshape(b_, h_, dilation, n_blk, ATTN_BLOCK, e_)

    def with_prev(t):
        prev = jnp.pad(t, ((0, 0), (0, 0), (0, 0), (1, 0), (0, 0), (0, 0)))[:, :, :, :-1]
        return jnp.concatenate([prev, t], axis=4)

    qb = to_blocks(q)
    kk = with_prev(to_blocks(k))
    vv = with_prev(to_blocks(v))
    s = jnp.einsum('bhcnqe,bhcnke->bhcnqk', qb, kk) * (HEAD_DIM ** -0.5)
    qi = jnp.arange(ATTN_BLOCK)[:, None]
    kj = jnp.arange(2 * ATTN_BLOCK)[None, :]
    dist = ATTN_BLOCK + qi - kj
    blk = jnp.arange(n_blk)[:, None, None]
    valid = (dist >= 0) & (dist <= steps) & (blk * ATTN_BLOCK - ATTN_BLOCK + kj >= 0)
    s = jnp.where(valid, s, NEG_INF)
    lse = jax.nn.logsumexp(s, axis=-1)
    p = jnp.exp(s - lse[..., None])
    o = jnp.einsum('bhcnqk,bhcnke->bhcnqe', p, vv)
    o = o.reshape(b_, h_, dilation, n_strided, e_).transpose(0, 1, 3, 2, 4).reshape(b_, h_, s_pad, e_)
    lse = lse.reshape(b_, h_, dilation, n_strided).transpose(0, 1, 3, 2).reshape(b_, h_, s_pad)
    return o[:, :, :s_], lse[:, :, :s_]

def _dilated_attention(q, k, v):
    outs, lses = [], []
    for window, dilation in DILATED_PATTERNS:
        o, l = _dilated_branch(q, k, v, window, dilation)
        outs.append(o)
        lses.append(l)
    wts = jax.nn.softmax(jnp.stack(lses, axis=0), axis=0)
    return jnp.einsum('gbhs,gbhse->bhse', wts, jnp.stack(outs, axis=0))

def _pool_mixer(u, w_mix, scale):
    b_, s_, _ = u.shape
    ug = u.reshape(b_, s_, N_POOL_GROUPS, POOL_GROUP_DIM).astype(jnp.float32)
    cs = jnp.cumsum(ug, axis=1)
    pos = jnp.arange(s_)
    outs = []
    for gi, w in enumerate(POOL_WINDOWS):
        c = cs[:, :, gi]
        lower = jnp.pad(c, ((0, 0), (w, 0), (0, 0)))[:, :s_]
        cnt = jnp.minimum(pos + 1, w).astype(jnp.float32)[None, :, None]
        outs.append((c - lower) / cnt - ug[:, :, gi])
    pooled = jnp.stack(outs, axis=2)
    mixed = jnp.einsum('bsgc,gcd->bsgd', pooled, w_mix.astype(jnp.float32))
    return (mixed.reshape(b_, s_, POOL_WIDTH) * scale.astype(jnp.float32)).astype(u.dtype)

def _hier_moe(h, w_rg, b_rg, w_re, b_re, w_gate, w_up, w_down):
    b_, s_, d_ = h.shape
    n_tok = b_ * s_
    hf = h.reshape(n_tok, d_)
    g_logits = jnp.dot(hf, w_rg).astype(jnp.float32) + b_rg.astype(jnp.float32)
    g_prob = jax.nn.softmax(g_logits, axis=-1)
    g_sel = jnp.argmax(g_logits, axis=-1).astype(jnp.int32)
    g_gate = jnp.take_along_axis(g_prob, g_sel[:, None], axis=1)[:, 0]
    e_logits_all = jnp.einsum('nd,gde->nge', hf, w_re).astype(jnp.float32) + b_re.astype(jnp.float32)
    e_logits = jnp.take_along_axis(e_logits_all, g_sel[:, None, None], axis=1)[:, 0]
    e_prob = jax.nn.softmax(e_logits, axis=-1)
    top_p, top_i = lax.top_k(e_prob, TOP_K)
    top_p = top_p / jnp.sum(top_p, axis=-1, keepdims=True)
    gate = g_gate[:, None] * top_p
    expert_id = g_sel[:, None] * EXPERTS_PER_GROUP + top_i.astype(jnp.int32)

    n_assign = n_tok * TOP_K
    e_flat = expert_id.reshape(n_assign)
    tok_flat = jnp.repeat(jnp.arange(n_tok, dtype=jnp.int32), TOP_K)
    w_flat = gate.reshape(n_assign)
    order = jnp.argsort(e_flat)
    e_s, tok_s, w_s = e_flat[order], tok_flat[order], w_flat[order]
    counts = jnp.bincount(e_flat, length=N_EXPERTS).astype(jnp.int32)
    start = jnp.cumsum(counts) - counts
    padded = (counts + MOE_BLOCK - 1) // MOE_BLOCK * MOE_BLOCK
    pend = jnp.cumsum(padded)
    pstart = pend - padded
    dest = pstart[e_s] + (jnp.arange(n_assign, dtype=jnp.int32) - start[e_s])
    buf_len = n_assign + N_EXPERTS * MOE_BLOCK
    n_blocks = buf_len // MOE_BLOCK
    buf_tok = jnp.full((buf_len,), n_tok, jnp.int32).at[dest].set(tok_s)
    buf_w = jnp.zeros((buf_len,), jnp.float32).at[dest].set(w_s)
    block_start = jnp.arange(n_blocks, dtype=jnp.int32) * MOE_BLOCK
    block_expert = jnp.minimum(jnp.searchsorted(pend, block_start, side='right'), N_EXPERTS - 1).astype(jnp.int32)
    x_rows = jnp.concatenate([hf, jnp.zeros((1, d_), hf.dtype)], axis=0)[buf_tok]
    x_rows = x_rows.reshape(n_blocks, MOE_BLOCK, d_)

    def expert_block(args):
        xb, e = args
        a = xb @ w_gate[e]
        bb = xb @ w_up[e]
        return (jax.nn.silu(a) * bb) @ w_down[e]

    y_rows = lax.map(expert_block, (x_rows, block_expert)).reshape(buf_len, d_)
    y = jnp.zeros((n_tok + 1, d_), jnp.float32).at[buf_tok].add(y_rows.astype(jnp.float32) * buf_w[:, None])
    return y[:n_tok].reshape(b_, s_, d_).astype(h.dtype)

def setup_inputs(seed: int = 0) -> dict:
    key = jax.random.key(seed)
    ks = jax.random.split(key, 18)
    f32 = jnp.float32
    nrm = lambda k, shape, scale: (jax.random.normal(k, shape, f32) * scale)
    return {
        "x": jax.random.normal(ks[0], (BATCH, SEQ, D_MODEL), f32),
        "norm1_g": 1.0 + nrm(ks[1], (DEPTH, D_MODEL), 0.02),
        "w_in": nrm(ks[2], (DEPTH, D_MODEL, IN_PROJ_WIDTH), D_MODEL ** -0.5),
        "q_norm_g": 1.0 + nrm(ks[3], (DEPTH, HEAD_DIM), 0.02),
        "k_norm_g": 1.0 + nrm(ks[4], (DEPTH, HEAD_DIM), 0.02),
        "w_attn_out": nrm(ks[5], (DEPTH, ATTN_WIDTH, D_MODEL), ATTN_WIDTH ** -0.5),
        "w_pool_mix": nrm(ks[6], (DEPTH, N_POOL_GROUPS, POOL_GROUP_DIM, POOL_GROUP_DIM), POOL_GROUP_DIM ** -0.5),
        "pool_scale": 1.0 + nrm(ks[7], (DEPTH, POOL_WIDTH), 0.1),
        "w_pool_out": nrm(ks[8], (DEPTH, POOL_WIDTH, D_MODEL), POOL_WIDTH ** -0.5),
        "w_o": nrm(ks[9], (DEPTH, D_MODEL, D_MODEL), D_MODEL ** -0.5),
        "norm2_g": 1.0 + nrm(ks[10], (DEPTH, D_MODEL), 0.02),
        "w_router_group": nrm(ks[11], (DEPTH, D_MODEL, N_EXPERT_GROUPS), D_MODEL ** -0.5),
        "b_router_group": nrm(ks[12], (DEPTH, N_EXPERT_GROUPS), 0.01),
        "w_router_expert": nrm(ks[13], (DEPTH, N_EXPERT_GROUPS, D_MODEL, EXPERTS_PER_GROUP), D_MODEL ** -0.5),
        "b_router_expert": nrm(ks[14], (DEPTH, N_EXPERT_GROUPS, EXPERTS_PER_GROUP), 0.01),
        "w_exp_gate": nrm(ks[15], (DEPTH, N_EXPERTS, D_MODEL, EXPERT_HIDDEN), D_MODEL ** -0.5),
        "w_exp_up": nrm(ks[16], (DEPTH, N_EXPERTS, D_MODEL, EXPERT_HIDDEN), D_MODEL ** -0.5),
        "w_exp_down": nrm(ks[17], (DEPTH, N_EXPERTS, EXPERT_HIDDEN, D_MODEL), EXPERT_HIDDEN ** -0.5),
    }

def reference(x, norm1_g, w_in, q_norm_g, k_norm_g, w_attn_out, w_pool_mix, pool_scale, w_pool_out,
              w_o, norm2_g, w_router_group, b_router_group, w_router_expert, b_router_expert,
              w_exp_gate, w_exp_up, w_exp_down):
    b_, s_, d_ = x.shape
    splits = [ATTN_WIDTH, 2 * ATTN_WIDTH, 3 * ATTN_WIDTH, 3 * ATTN_WIDTH + POOL_WIDTH,
              3 * ATTN_WIDTH + POOL_WIDTH + D_MODEL]
    for layer in range(DEPTH):
        h = _rmsnorm(x, norm1_g[layer])
        proj = h @ w_in[layer]
        q, k, v, u, gate_a, gate_p = jnp.split(proj, splits, axis=-1)
        q = _rmsnorm(q.reshape(b_, s_, N_HEADS, HEAD_DIM), q_norm_g[layer])
        k = _rmsnorm(k.reshape(b_, s_, N_HEADS, HEAD_DIM), k_norm_g[layer])
        v = v.reshape(b_, s_, N_HEADS, HEAD_DIM)
        q, k, v = (t.transpose(0, 2, 1, 3).astype(jnp.float32) for t in (q, k, v))
        attn = _dilated_attention(q, k, v).transpose(0, 2, 1, 3).reshape(b_, s_, ATTN_WIDTH).astype(x.dtype)
        y_a = attn @ w_attn_out[layer]
        y_p = _pool_mixer(u, w_pool_mix[layer], pool_scale[layer]) @ w_pool_out[layer]
        merged = jax.nn.sigmoid(gate_a) * y_a + jax.nn.sigmoid(gate_p) * y_p
        x = x + merged @ w_o[layer]
        h2 = _rmsnorm(x, norm2_g[layer])
        x = x + _hier_moe(h2, w_router_group[layer], b_router_group[layer], w_router_expert[layer],
                          b_router_expert[layer], w_exp_gate[layer], w_exp_up[layer], w_exp_down[layer])
    return x


_drawn_inputs = setup_inputs


def setup_inputs(seed=0):
    import zlib

    import numpy as np

    out = dict(_drawn_inputs(seed))
    spreads = {}
    factors = {'q_norm_g': 8.0, 'k_norm_g': 8.0, 'b_router_group': 7.117, 'b_router_expert': 3.977}
    for name, (base, spread) in spreads.items():
        noise = np.random.default_rng([zlib.crc32(name.encode()), seed]).standard_normal(out[name].shape)
        drawn = base * np.exp(spread * noise) if base else spread * noise
        out[name] = __import__('jax').numpy.asarray(drawn.astype(out[name].dtype))
    for name, factor in factors.items():
        out[name] = (out[name] * factor).astype(out[name].dtype)
    return out
```

```python
from contextlib import ExitStack

import numpy as np

import concourse.bass as bass
from concourse import mybir

P = 128
ALU = mybir.AluOpType
ACT = mybir.ActivationFunctionType
AX_X = mybir.AxisListType.X
F32 = mybir.dt.float32
F32R = mybir.dt.float32r
I32 = mybir.dt.int32
U32 = mybir.dt.uint32

D = 1024
S = 1024
KC = D // P
TT = S // P
HD = 64
NH = 8
AW = NH * HD
PG = 4
WIN = (2, 4, 8, 16)
NW = 512
DILATED = ((128, 1), (512, 4), (2048, 16))
NG, NE = 4, 8
E = NG * NE
FH = 512
FC = FH // P
NR = NG + E
EPS = 1e-6
MASKED = -1e30
MOST = 16
NB = E + MOST
PAD = max(WIN)

C_ID, C_TRI, C_ONE = 0, P, 2 * P
C_CNT = 3 * P
C_D4 = C_CNT + PG * PAD
C_D8 = C_D4 + NG
C_EID = C_D8 + NE
C_TH = C_EID + E
C_TOK = C_TH + MOST
C_LOG = C_TOK + TT
C_ALL = C_LOG + S


def shape_constants():
    c = np.zeros((P, C_ALL), np.float32)
    r = np.arange(P)
    c[:, C_ID:C_ID + P] = np.eye(P)
    c[:, C_TRI:C_TRI + P] = r[:, None] < r[None, :]
    c[:, C_ONE:C_ONE + P] = 1
    for g, w in enumerate(WIN):
        c[:, C_CNT + g * PAD:C_CNT + (g + 1) * PAD] = w / np.minimum(np.arange(PAD) + 1, w)
    c[:, C_D4:C_D4 + NG] = NG - np.arange(NG)
    c[:, C_D8:C_D8 + NE] = NE - np.arange(NE)
    c[:, C_EID:C_EID + E] = np.arange(E)
    c[:, C_TH:C_TH + MOST] = np.arange(MOST)
    c[:, C_TOK:C_TOK + TT] = np.arange(TT)[None, :] * P + r[:, None]
    dist = r[:, None] + (S - P) - np.arange(S)[None, :]
    held = sum(((dist >= 0) & (dist <= w) & (dist % d == 0)).astype(np.int64) for w, d in DILATED)
    c[:, C_LOG:C_LOG + S] = np.where(held > 0, np.log(np.maximum(held, 1)), MASKED)
    return c


def wait(eng, sem, value):
    if not isinstance(value, int) or value > 0:
        eng.wait_ge(sem, value)


def held_value(eng, value):
    return value if isinstance(value, int) else eng.to_reg(value)


class Chain:

    def __init__(self, eng, sem, base=0):
        self.eng, self.sem, self.n = eng, sem, base

    def __call__(self, ins):
        self.n = self.n + 1
        ins.then_inc(self.sem, 1)
        self.eng.wait_ge(self.sem, self.n)


def three_passes(nc, out, a_hi, a_lo, b_hi, b_lo, first, last):
    nc.tensor.matmul(out, a_hi, b_hi, start=first, stop=False)
    nc.tensor.matmul(out, a_lo, b_hi, start=False, stop=False)
    return nc.tensor.matmul(out, a_hi, b_lo, start=False, stop=last)


class Scope:

    def __init__(self, nc, ctx, stage):
        self.nc, self.ctx, self.stage = nc, ctx, stage

    def sb(self, name, shape, dt=F32):
        return self.ctx.enter_context(self.nc.sbuf_tensor(f"{self.stage}_{name}", shape, dt))

    def ps(self, name, shape, dt=F32):
        return self.ctx.enter_context(self.nc.psum_tensor(f"{self.stage}_{name}_ps", shape, dt))

    def sem(self, name):
        return self.ctx.enter_context(self.nc.semaphore(f"{self.stage}_{name}"))

    def sems(self, name, n):
        return [self.sem(f"{name}{i}") for i in range(n)]


def norm_and_transpose(nc, x, norm1_g, consts, h_hi, h_lo):
    with ExitStack() as ctx:
        m = Scope(nc, ctx, "norm")
        xs = m.sb("x", [P, TT, D])
        g = m.sb("g", [P, D])
        ident = m.sb("ident", [P, P])
        squares = m.sb("squares", [P, D])
        ssq = m.sb("ssq", [P, TT])
        var = m.sb("var", [P, TT])
        dev = m.sb("dev", [P, TT])
        rstd = m.sb("rstd", [P, TT])
        h = m.sb("h", [P, 2, D])
        turned = [m.ps(f"turned{b}", [P, KC, P]) for b in range(2)]
        x_loaded = m.sems("x_loaded", TT)
        g_loaded, id_loaded = m.sem("g_loaded"), m.sem("id_loaded")
        summed, var_done, dev_done = m.sem("summed"), m.sem("var_done"), m.sem("dev_done")
        rstd_done, scaled = m.sem("rstd_done"), m.sem("scaled")
        transposed, hi_done, lo_done = m.sem("transposed"), m.sem("hi_done"), m.sem("lo_done")
        half = TT // 2
        block = ctx.enter_context(nc.Block())

        @block.sync
        def _(sp):
            for t in range(TT):
                sp.dma_start(xs[:, t, :], x[0, t * P:(t + 1) * P, :]).then_inc(x_loaded[t], 16)
                if t == 0:
                    sp.dma_start(ident[:], consts[:, C_ID:C_ID + P]).then_inc(id_loaded, 16)
                    sp.dma_start(g[:], norm1_g[0:1, :].to_broadcast([P, D])).then_inc(g_loaded, 16)

        @block.scalar
        def _(act):
            def sums(b):
                for t in range(b * half, (b + 1) * half):
                    act.wait_ge(x_loaded[t], 16)
                    wait(act, summed, t)
                    nc.scalar.activation(squares[:], xs[:, t, :], ACT.Square,
                                         accum_out=ssq[:, t:t + 1]).then_inc(summed, 1)

            def root(b):
                act.wait_ge(var_done, b + 1)
                nc.scalar.activation(dev[:, b * half:(b + 1) * half], var[:, b * half:(b + 1) * half],
                                     ACT.Sqrt).then_inc(dev_done, 1)

            def upper(t):
                act.wait_ge(transposed, t + 1)
                nc.scalar.copy(h_hi[:, :, t * P:(t + 1) * P], turned[t % 2][:]).then_inc(hi_done, 1)

            sums(0)
            root(0)
            sums(1)
            root(1)
            for t in range(TT):
                upper(t)

        @block.vector
        def _(dve):
            def scale(b):
                r = slice(b * half, (b + 1) * half)
                dve.wait_ge(summed, (b + 1) * half)
                nc.vector.tensor_scalar(var[:, r], ssq[:, r], 1.0 / D, EPS, ALU.mult, ALU.add).then_inc(var_done, 1)
                dve.wait_ge(dev_done, b + 1)
                nc.vector.reciprocal(rstd[:, r], dev[:, r]).then_inc(rstd_done, 1)
                dve.wait_ge(rstd_done, b + 1)

            def apply(t):
                wait(dve, transposed, t - 1)
                nc.vector.scalar_tensor_tensor(out=h[:, t % 2, :], in0=xs[:, t, :], scalar=rstd[:, t:t + 1],
                                               in1=g[:], op0=ALU.mult, op1=ALU.mult).then_inc(scaled, 1)

            def lower(t):
                dve.wait_ge(hi_done, t + 1)
                nc.vector.tensor_tensor(h_lo[:, :, t * P:(t + 1) * P], turned[t % 2][:],
                                        h_hi[:, :, t * P:(t + 1) * P].bitcast(F32),
                                        ALU.subtract).then_inc(lo_done, 1)

            scale(0)
            dve.wait_ge(g_loaded, 16)
            for t in range(TT):
                apply(t)
                if t == 1:
                    scale(1)
                if t >= 1:
                    lower(t - 1)
            lower(TT - 1)

        @block.tensor
        def _(pe):
            pe.wait_ge(id_loaded, 16)
            for t in range(TT):
                pe.wait_ge(scaled, t + 1)
                wait(pe, lo_done, t - 1)
                for k in range(KC):
                    last = nc.tensor.transpose(turned[t % 2][:, k, :], h[:, t % 2, k * P:(k + 1) * P], ident[:])
                last.then_inc(transposed, 1)


def project(nc, w_in, h_hi, h_lo, qkv, rqk, u_dram, gates_dram, y_dram):
    with ExitStack() as ctx:
        m = Scope(nc, ctx, "proj")
        CH = 8
        QT, SL = 4, KC // 4
        raw = m.sb("raw", [P, 2, SL, NW])
        w_hi = m.sb("w_hi", [P, 2, KC, NW], F32R)
        w_lo = m.sb("w_lo", [P, 2, KC, NW], F32R)
        staged = m.sb("staged", [P, 2, NW])
        sq = m.sb("sq", [P, 4 * AW])
        ssq = m.sb("ssq", [P, 2 * TT * NH])
        var = m.sb("var", [P, 2 * TT * NH])
        dev = m.sb("dev", [P, 2 * TT * NH])
        acc = [m.ps(f"acc{b}", [P, NW]) for b in range(4)]
        raw_loaded = m.sems("raw_loaded", 2)
        hi_done, lo_done = m.sem("hi_done"), m.sem("lo_done")
        projected, evacuated = m.sem("projected"), m.sem("evacuated")
        stored = m.sems("stored", 2)
        var_done, dev_done, chain = m.sem("var_done"), m.sem("dev_done"), m.sem("chain")
        zeros = m.sb("zeros", [P, D // 2])
        zeroed, filled = m.sem("zeroed"), m.sem("filled")
        w_rows = w_in[0].rearrange("(k p) n -> p k n", p=P)
        block = ctx.enter_context(nc.Block())

        @block.sync
        def _(sp):
            def load(c, col):
                for q in range(QT):
                    wait(sp, lo_done, c * QT + q - 1)
                    sp.dma_start(raw[:, q % 2], w_rows[:, q * SL:(q + 1) * SL, bass.ds(col, NW)]
                                 ).then_inc(raw_loaded[q % 2], 16)

            load(0, 3 * AW)
            with sp.Fori(1, 4) as c:
                load(c, c * NW - NW)
            with sp.Fori(4, CH) as c:
                load(c, c * NW)

        @block.gpsimd
        def _(pool):
            nc.gpsimd.memset(zeros[:], 0.0).then_inc(zeroed, 1)
            pool.wait_ge(zeroed, 1)
            with pool.Fori(E, NB) as b:
                for half in range(2):
                    pool.dma_start(y_dram[bass.ds(b * P, P), half * (D // 2):(half + 1) * (D // 2)],
                                   zeros[:]).then_inc(filled, 16)
            pool.wait_ge(filled, 16 * 2 * MOST)

        @block.scalar
        def _(act):
            def upper(c, q):
                act.wait_ge(raw_loaded[q % 2], c * 32 + 16 * (q // 2 + 1))
                if not isinstance(c, int) or c >= 2:
                    act.wait_ge(projected, c * 8 - 8)
                nc.scalar.copy(w_hi[:, c % 2, q * SL:(q + 1) * SL, :], raw[:, q % 2]).then_inc(hi_done, 1)

            def to_dram(c, t, dst, func, n):
                act.wait_ge(projected, c * 8 + t + 1)
                wait(act, stored[t % 2], n * 16)
                nc.scalar.activation(staged[:, t % 2, :], acc[t % 4][:], func).then_inc(evacuated, 1)
                act.wait_ge(evacuated, c * 8 + t + 1)
                act.dma_start(dst, staged[:, t % 2, :]).then_inc(stored[t % 2], 16)

            def split_next(c, t):
                if t % 2:
                    upper(c + 1, t // 2)

            def gate_chunk(c, more):
                for t in range(TT):
                    to_dram(c, t, gates_dram[t * P:(t + 1) * P, bass.ds(c * NW - 4 * NW, NW)],
                            ACT.Sigmoid, c * 4 - 12 + t // 2)
                    if more:
                        split_next(c, t)

            for q in range(QT):
                upper(0, q)
            for t in range(TT):
                g, half = divmod(t, 2)
                to_dram(0, t, u_dram[g, :, half * NW:(half + 1) * NW], ACT.Copy, t // 2)
                if t % 2:
                    upper(1, t // 2)
            with act.Fori(1, 4) as c:
                for t in range(TT):
                    act.wait_ge(projected, c * 8 + t + 1)
                    nc.scalar.copy(qkv[:, c - 1, t, :], acc[t % 4][:]).then_inc(evacuated, 1)
                    split_next(c, t)
            with act.Fori(4, CH - 1) as c:
                gate_chunk(c, True)
            gate_chunk(CH - 1, False)
            act.wait_ge(var_done, 1)
            nc.scalar.activation(dev[:], var[:], ACT.Sqrt).then_inc(dev_done, 1)
            for b in range(2):
                act.wait_ge(stored[b], 16 * (4 + 16))

        @block.vector
        def _(dve):
            link = Chain(dve, chain)

            def lower(c, q):
                dve.wait_ge(hi_done, c * QT + q + 1)
                nc.vector.tensor_tensor(w_lo[:, c % 2, q * SL:(q + 1) * SL, :], raw[:, q % 2],
                                        w_hi[:, c % 2, q * SL:(q + 1) * SL, :].bitcast(F32),
                                        ALU.subtract).then_inc(lo_done, 1)

            for q in range(QT):
                lower(0, q)
            with dve.Fori(1, 5) as c:
                for q in range(QT):
                    lower(c, q)
            dve.wait_ge(evacuated, 8 * 3)
            for s in range(2):
                for b in range(2):
                    half = qkv[:, s, b * 4:(b + 1) * 4, :].rearrange("p t n -> p (t n)")
                    link(nc.vector.tensor_tensor(sq[:], half, half, ALU.mult))
                    at = (s * 2 + b) * 4 * NH
                    link(nc.vector.tensor_reduce(ssq[:, at:at + 4 * NH], sq[:].rearrange("p (a e) -> p a e", e=HD),
                                                 AX_X, ALU.add))
            nc.vector.tensor_scalar(var[:], ssq[:], 1.0 / HD, EPS, ALU.mult, ALU.add).then_inc(var_done, 1)
            with dve.Fori(5, CH) as c:
                for q in range(QT):
                    lower(c, q)
            dve.wait_ge(dev_done, 1)
            link(nc.vector.reciprocal(rqk[:].rearrange("p a b c -> p (a b c)"), dev[:]))

        @block.tensor
        def _(pe):
            def columns_first():
                for t in range(8):
                    g, half = divmod(t, 2)
                    wait(pe, evacuated, t - 3)
                    for k in range(KC):
                        if t == 0 and k % SL == 0:
                            pe.wait_ge(lo_done, k // SL + 1)
                        cols, toks = slice(g * P, (g + 1) * P), slice(half * NW, (half + 1) * NW)
                        last = three_passes(nc, acc[t % 4][:], w_hi[:, 0, k, cols], w_lo[:, 0, k, cols],
                                            h_hi[:, k, toks], h_lo[:, k, toks], k == 0, k == KC - 1)
                    last.then_inc(projected, 1)

            def tokens_first(c):
                for t in range(TT):
                    pe.wait_ge(evacuated, c * 8 + t - 3)
                    toks = slice(t * P, (t + 1) * P)
                    for k in range(KC):
                        if t == 0 and k % SL == 0:
                            pe.wait_ge(lo_done, c * QT + k // SL + 1)
                        last = three_passes(nc, acc[t % 4][:], h_hi[:, k, toks], h_lo[:, k, toks],
                                            w_hi[:, c % 2, k, :], w_lo[:, c % 2, k, :], k == 0, k == KC - 1)
                    last.then_inc(projected, 1)

            columns_first()
            with pe.Fori(1, CH) as c:
                tokens_first(c)


def attend(nc, consts, q_norm_g, k_norm_g, w_pool_mix, pool_scale, u_dram, qkv, rqk,
           attn_hi, attn_lo, pool_hi, pool_lo):
    with ExitStack() as ctx:
        m = Scope(nc, ctx, "attn")
        PAIRS, IT = NH // 2, 2 * TT
        ident = m.sb("ident", [P, P])
        log_held = m.sb("log_held", [P, S])
        ratio = m.sb("ratio", [P, PG, PAD])
        norm_g = m.sb("norm_g", [P, 2])
        scale_g = m.sb("scale_g", [P, 2])
        qk_st = m.sb("qk_st", [P, 2, TT, P])
        v_st = m.sb("v_st", [P, TT, P])
        qk_t = m.sb("qk_t", [P, 2, S])
        masked = m.sb("masked", [P, 2, S])
        negmax = m.sb("negmax", [P, 2])
        prob = m.sb("prob", [P, 2, S])
        den = m.sb("den", [P, 2])
        rden = m.sb("rden", [P, 2])
        prob_t = m.sb("prob_t", [P, 2, TT, P])
        u = m.sb("u", [P, PG, PAD + S])
        run = m.sb("run", [P, 2, PAD + S])
        wsum = m.sb("wsum", [P, PG, S])
        mix = m.sb("mix", [P, PG, P])
        pscale = m.sb("pscale", [P, PG])
        score = [m.ps(f"score{b}", [P, S]) for b in range(2)]
        turned = m.ps("turned", [P, TT, P])
        out_t = [m.ps(f"out_t{b}", [P, NW]) for b in range(2)]
        c_loaded, g_loaded, u_loaded, mix_loaded = (m.sem("c_loaded"), m.sem("g_loaded"), m.sem("u_loaded"),
                                                    m.sem("mix_loaded"))
        g_scaled, qk_staged, v_staged = m.sem("g_scaled"), m.sem("qk_staged"), m.sem("v_staged")
        qk_turned, qk_copied = m.sem("qk_turned"), m.sem("qk_copied")
        scored, maxed, exped, normed = m.sem("scored"), m.sem("maxed"), m.sem("exped"), m.sem("normed")
        rden_done, p_turned, p_copied = m.sem("rden_done"), m.sem("p_turned"), m.sem("p_copied")
        summed, hi_done, lo_done = m.sem("summed"), m.sem("hi_done"), m.sem("lo_done")
        padded, pool_chain, windows_done = m.sem("padded"), m.sem("pool_chain"), m.sem("windows_done")
        pooled, pool_link, mixed = m.sem("pooled"), m.sem("pool_link"), m.sem("mixed")
        mix_hi, mix_lo = m.sem("mix_hi"), m.sem("mix_lo")
        block = ctx.enter_context(nc.Block())

        @block.sync
        def _(sp):
            sp.dma_start(ident[:], consts[:, C_ID:C_ID + P]).then_inc(c_loaded, 16)
            sp.dma_start(log_held[:], consts[:, C_LOG:C_LOG + S]).then_inc(c_loaded, 16)
            sp.dma_start(ratio[:].rearrange("p g w -> p (g w)"), consts[:, C_CNT:C_CNT + PG * PAD]
                         ).then_inc(c_loaded, 16)
            for i, g in enumerate((q_norm_g, k_norm_g)):
                for a in range(2):
                    sp.dma_start(norm_g[a * HD:(a + 1) * HD, i:i + 1], g[0].unsqueeze(1)).then_inc(g_loaded, 16)
            sp.wait_ge(padded, 1)
            sp.dma_start(u[:, :, PAD:], u_dram.rearrange("g p s -> p g s")).then_inc(u_loaded, 16)
            sp.dma_start(mix[:], w_pool_mix[0].rearrange("g c d -> c g d")).then_inc(mix_loaded, 16)
            for g in range(PG):
                sp.dma_start(pscale[:, g:g + 1], pool_scale[0, g * P:(g + 1) * P].unsqueeze(1)).then_inc(mix_loaded, 16)

        @block.gpsimd
        def _(pool):
            link = Chain(pool, pool_chain)
            nc.gpsimd.memset(u[:], 0.0).then_inc(padded, 1)
            link(nc.gpsimd.memset(run[:], 0.0))

            def stage_v(hp):
                wait(pool, summed, hp * IT)
                nc.gpsimd.tensor_copy(v_st[:], qkv[:, 2, :, bass.ds(hp * P, P)]).then_inc(v_staged, 1)

            stage_v(0)
            pool.wait_ge(u_loaded, 16)
            for g, w in enumerate(WIN):
                src = u[:, g]
                for step in range(g + 1):
                    s = 1 << step
                    dst = wsum[:, g] if step == g else run[:, step % 2, PAD:]
                    link(nc.gpsimd.tensor_tensor(dst, src[:, PAD:], src[:, PAD - s:PAD + S - s], ALU.add))
                    src = run[:, step % 2]
                ins = nc.gpsimd.tensor_tensor(wsum[:, g, 0:PAD], wsum[:, g, 0:PAD], ratio[:, g], ALU.mult)
                ins.then_inc(windows_done, 1)
            with pool.Fori(1, PAIRS) as hp:
                stage_v(hp)

        @block.vector
        def _(dve):
            dve.wait_ge(g_loaded, 64)
            nc.vector.tensor_scalar(scale_g[:, 0:1], norm_g[:, 0:1], HD ** -0.5, None, ALU.mult).then_inc(g_scaled, 1)
            nc.vector.tensor_copy(scale_g[:, 1:2], norm_g[:, 1:2]).then_inc(g_scaled, 1)

            def stage_qk(hp):
                wait(dve, qk_turned, hp * 2)
                for s in range(2):
                    nc.vector.tensor_tensor(
                        qk_st[:, s].rearrange("p t (a e) -> p t a e", a=2),
                        qkv[:, s, :, bass.ds(hp * P, P)].rearrange("p t (a e) -> p t a e", a=2),
                        rqk[:, s, :, bass.ds(hp * 2, 2)].unsqueeze(3).to_broadcast([P, TT, 2, HD]),
                        ALU.mult).then_inc(qk_staged, 1)

            def mask_and_max(hp, i):
                b, n = i % 2, (i // 2 + 1) * P
                scores_due, exps_due = held_value(dve, hp * IT + i + 1), held_value(dve, hp * IT + max(i - 1, 0))
                dve.wait_ge(c_loaded, 48)
                dve.wait_ge(scored, scores_due)
                wait(dve, exped, exps_due)
                nc.vector.tensor_tensor_reduce(
                    out=masked[:, b, 0:n], in0=score[b][:, 0:n], in1=log_held[:, S - n:S], scale=-1.0,
                    scalar=3e38, op0=ALU.add, op1=ALU.min, accum_out=negmax[:, b:b + 1]).then_inc(maxed, 1)

            def normalise(hp, i):
                b, n = i % 2, (i // 2 + 1) * P
                dve.wait_ge(exped, hp * IT + i + 1)
                nc.vector.reciprocal(rden[:, b:b + 1], den[:, b:b + 1]).then_inc(rden_done, 1)
                dve.wait_ge(rden_done, hp * IT + i + 1)
                nc.vector.tensor_scalar(prob[:, b, 0:n], prob[:, b, 0:n], rden[:, b:b + 1], None,
                                        ALU.mult).then_inc(normed, 1)

            def lower(hp, t):
                dve.wait_ge(hi_done, hp * TT + t + 1)
                at = (slice(None), hp, slice(t * P, (t + 1) * P))
                nc.vector.tensor_tensor(attn_lo[at], out_t[t % 2][:, 0:P], attn_hi[at].bitcast(F32),
                                        ALU.subtract).then_inc(lo_done, 1)

            def pair(hp, more):
                for i in range(IT):
                    mask_and_max(hp, i)
                    if i >= 1:
                        normalise(hp, i - 1)
                    if i >= 4 and i % 2 == 0:
                        lower(hp, i // 2 - 2)
                    if i == 8 and more:
                        stage_qk(hp + 1)
                normalise(hp, IT - 1)
                lower(hp, TT - 2)
                lower(hp, TT - 1)

            stage_qk(0)
            dve.wait_ge(c_loaded, 48)
            pair(0, True)
            with dve.Fori(1, PAIRS - 1) as hp:
                pair(hp, True)
            pair(PAIRS - 1, False)
            for g, w in enumerate(WIN):
                dve.wait_ge(windows_done, g + 1)
                nc.vector.scalar_tensor_tensor(out=wsum[:, g], in0=wsum[:, g], scalar=1.0 / w, in1=u[:, g, PAD:],
                                               op0=ALU.mult, op1=ALU.subtract).then_inc(pooled, 1)
            for n in range(2 * PG):
                g, half = divmod(n, 2)
                dst = (slice(None), g, slice(half * NW, (half + 1) * NW))
                dve.wait_ge(mix_hi, n + 1)
                nc.vector.scalar_tensor_tensor(out=pool_lo[dst], in0=score[half][:, 0:NW], scalar=pscale[:, g:g + 1],
                                               in1=pool_hi[dst].bitcast(F32), op0=ALU.mult,
                                               op1=ALU.subtract).then_inc(mix_lo, 1)

        @block.scalar
        def _(act):
            def copy_qk(hp, s):
                act.wait_ge(qk_turned, hp * 2 + s + 1)
                nc.scalar.activation(qk_t[:, s, :], score[s][:], ACT.Copy,
                                     scale=scale_g[:, s:s + 1]).then_inc(qk_copied, 1)

            def exponent(hp, i):
                b, n = i % 2, (i // 2 + 1) * P
                act.wait_ge(maxed, hp * IT + i + 1)
                wait(act, p_turned, hp * IT + max(i - 1, 0))
                nc.scalar.activation(prob[:, b, 0:n], masked[:, b, 0:n], ACT.Exp, bias=negmax[:, b:b + 1], scale=-1.0,
                                     accum_out=den[:, b:b + 1]).then_inc(exped, 1)

            def copy_prob(hp, i):
                b, j = i % 2, i // 2 + 1
                act.wait_ge(p_turned, hp * IT + i + 1)
                wait(act, summed, hp * IT + max(i - 1, 0))
                nc.scalar.copy(prob_t[:, b, 0:j, :], turned[:, 0:j, :]).then_inc(p_copied, 1)

            def upper(hp, t):
                act.wait_ge(summed, hp * IT + 2 * t + 2)
                nc.scalar.copy(attn_hi[:, hp, t * P:(t + 1) * P], out_t[t % 2][:, 0:P]).then_inc(hi_done, 1)

            def pair(hp, more):
                for i in range(IT):
                    exponent(hp, i)
                    if i >= 1:
                        copy_prob(hp, i - 1)
                    if i >= 4 and i % 2 == 0:
                        upper(hp, i // 2 - 2)
                if more:
                    copy_qk(hp + 1, 0)
                copy_prob(hp, IT - 1)
                upper(hp, TT - 2)
                if more:
                    copy_qk(hp + 1, 1)
                upper(hp, TT - 1)

            act.wait_ge(g_scaled, 2)
            copy_qk(0, 0)
            copy_qk(0, 1)
            pair(0, True)
            with act.Fori(1, PAIRS - 1) as hp:
                pair(hp, True)
            pair(PAIRS - 1, False)
            act.wait_ge(mix_loaded, 80)
            for n in range(2 * PG):
                g, half = divmod(n, 2)
                act.wait_ge(mixed, n + 1)
                nc.scalar.activation(pool_hi[:, g, half * NW:(half + 1) * NW], score[half][:, 0:NW], ACT.Copy,
                                     scale=pscale[:, g:g + 1]).then_inc(mix_hi, 1)

        @block.tensor
        def _(pe):
            def turn_qk(hp, s):
                pe.wait_ge(qk_staged, hp * 2 + s + 1)
                wait(pe, maxed, hp * IT - 1 + s if not isinstance(hp, int) or hp else 0)
                for t in range(TT):
                    last = nc.tensor.transpose(score[s][:, t * P:(t + 1) * P], qk_st[:, s, t, :], ident[:])
                last.then_inc(qk_turned, 1)

            def scores(hp, i):
                t, a = divmod(i, 2)
                n, h = (t + 1) * P, slice(a * HD, (a + 1) * HD)
                if i < 2:
                    pe.wait_ge(qk_copied, hp * 2 + 2)
                else:
                    pe.wait_ge(maxed, hp * IT + i - 1)
                for c in range(0, n, NW):
                    w = min(NW, n - c)
                    last = nc.tensor.matmul(score[i % 2][:, c:c + w], qk_t[h, 0, t * P:(t + 1) * P],
                                            qk_t[h, 1, c:c + w], start=True, stop=True)
                last.then_inc(scored, 1)

            def turn_prob(hp, i):
                pe.wait_ge(normed, hp * IT + i + 1)
                wait(pe, p_copied, hp * IT + i)
                for j in range(i // 2 + 1):
                    last = nc.tensor.transpose(turned[:, j, :], prob[:, i % 2, j * P:(j + 1) * P], ident[:])
                last.then_inc(p_turned, 1)

            def weigh(hp, i):
                t, a = divmod(i, 2)
                h = slice(a * HD, (a + 1) * HD)
                pe.wait_ge(p_copied, hp * IT + i + 1)
                if a == 0:
                    wait(pe, lo_done, hp * TT + max(t - 1, 0))
                if i == 0:
                    pe.wait_ge(v_staged, hp + 1)
                for j in range(t + 1):
                    last = nc.tensor.matmul(out_t[t % 2][h, 0:P], v_st[:, j, h], prob_t[:, i % 2, j, :],
                                            start=(j == 0), stop=(j == t))
                last.then_inc(summed, 1)

            def pair(hp, more):
                for i in range(IT + 3):
                    if i < IT:
                        scores(hp, i)
                    if 2 <= i < IT + 2:
                        turn_prob(hp, i - 2)
                    if i >= 3:
                        weigh(hp, i - 3)
                    if more and i == IT:
                        turn_qk(hp + 1, 0)
                    if more and i == IT + 1:
                        turn_qk(hp + 1, 1)

            pe.wait_ge(c_loaded, 48)
            turn_qk(0, 0)
            turn_qk(0, 1)
            pair(0, True)
            with pe.Fori(1, PAIRS - 1) as hp:
                pair(hp, True)
            pair(PAIRS - 1, False)
            pe.wait_ge(mix_loaded, 80)
            for n in range(2 * PG):
                g, half = divmod(n, 2)
                pe.wait_ge(pooled, g + 1)
                pe.wait_ge(maxed, PAIRS * IT)
                wait(pe, mix_lo, n - 1)
                nc.tensor.matmul(score[half][:, 0:NW], mix[:, g, :], wsum[:, g, half * NW:(half + 1) * NW],
                                 start=True, stop=True).then_inc(mixed, 1)


def merge(nc, consts, gates_dram, w_attn_out, w_pool_out, attn_hi, attn_lo, pool_hi, pool_lo, mt_hi, mt_lo):
    with ExitStack() as ctx:
        m = Scope(nc, ctx, "merge")
        QT, SL, BK = 4, 2, AW // P
        ident = m.sb("ident", [P, P])
        raw = m.sb("raw", [P, 2, SL, NW])
        w_hi = m.sb("w_hi", [P, 2 * BK, NW], F32R)
        w_lo = m.sb("w_lo", [P, 2 * BK, NW], F32R)
        gate = m.sb("gate", [P, 2, 2, NW])
        part = m.sb("part", [P, 2, NW])
        merged = m.sb("merged", [P, 2, NW])
        acc = [[m.ps(f"acc{b}{s}", [P, NW]) for s in range(2)] for b in range(2)]
        turned = [m.ps(f"turned{b}", [P, NW // P, P]) for b in range(2)]
        id_loaded = m.sem("id_loaded")
        raw_loaded, gate_loaded = m.sems("raw_loaded", 2), m.sems("gate_loaded", 2)
        w_hi_done, w_lo_done = m.sem("w_hi_done"), m.sem("w_lo_done")
        attn_done, pool_done, gated, added = m.sem("attn_done"), m.sem("pool_done"), m.sem("gated"), m.sem("added")
        transposed, hi_done, lo_done = m.sem("transposed"), m.sem("hi_done"), m.sem("lo_done")
        rows = [w[0].rearrange("(k p) n -> p k n", p=P) for w in (w_attn_out, w_pool_out)]
        block = ctx.enter_context(nc.Block())

        @block.sync
        def _(sp):
            sp.dma_start(ident[:], consts[:, C_ID:C_ID + P]).then_inc(id_loaded, 16)

            def weights(c, quarters):
                for q in quarters:
                    wait(sp, w_lo_done, c * QT + q - 1)
                    sp.dma_start(raw[:, q % 2], rows[q // 2][:, (q % 2) * SL:(q % 2 + 1) * SL, c * NW:(c + 1) * NW]
                                 ).then_inc(raw_loaded[q % 2], 16)

            def gates(n):
                c, t = divmod(n, TT)
                wait(sp, added, n - 1)
                for s in range(2):
                    col = s * D + c * NW
                    sp.dma_start(gate[:, n % 2, s, :], gates_dram[t * P:(t + 1) * P, col:col + NW]
                                 ).then_inc(gate_loaded[n % 2], 16)

            weights(0, range(QT))
            for n in range(2 * TT):
                gates(n)
                if n == 3:
                    weights(1, range(QT // 2))
                if n == TT:
                    weights(1, range(QT // 2, QT))

        @block.scalar
        def _(act):
            def w_upper(c, q):
                act.wait_ge(raw_loaded[q % 2], 16 * (c * 2 + q // 2 + 1))
                if c:
                    act.wait_ge((attn_done, pool_done)[q // 2], TT)
                nc.scalar.copy(w_hi[:, q * SL:(q + 1) * SL, :], raw[:, q % 2]).then_inc(w_hi_done, 1)

            def upper(n):
                c, t = divmod(n, TT)
                act.wait_ge(transposed, n + 1)
                nc.scalar.copy(mt_hi[:, c * BK:(c + 1) * BK, t * P:(t + 1) * P], turned[n % 2][:]).then_inc(hi_done, 1)

            for c in range(2):
                for q in range(QT):
                    w_upper(c, q)
                for t in range(TT):
                    if c * TT + t >= 1:
                        upper(c * TT + t - 1)
            upper(2 * TT - 1)

        @block.vector
        def _(dve):
            def w_lower(c, q):
                dve.wait_ge(w_hi_done, c * QT + q + 1)
                nc.vector.tensor_tensor(w_lo[:, q * SL:(q + 1) * SL, :], raw[:, q % 2],
                                        w_hi[:, q * SL:(q + 1) * SL, :].bitcast(F32), ALU.subtract
                                        ).then_inc(w_lo_done, 1)

            def combine(n):
                b = n % 2
                dve.wait_ge(gate_loaded[b], 32 * (n // 2 + 1))
                dve.wait_ge(attn_done, n + 1)
                nc.vector.tensor_tensor(part[:, 0, :], acc[b][0][:], gate[:, b, 0, :], ALU.mult).then_inc(gated, 1)
                dve.wait_ge(pool_done, n + 1)
                nc.vector.tensor_tensor(part[:, 1, :], acc[b][1][:], gate[:, b, 1, :], ALU.mult).then_inc(gated, 1)
                dve.wait_ge(gated, 2 * n + 2)
                wait(dve, transposed, n - 1)
                nc.vector.tensor_tensor(merged[:, b, :], part[:, 0, :], part[:, 1, :], ALU.add).then_inc(added, 1)
                dve.wait_ge(added, n + 1)

            def lower(n):
                c, t = divmod(n, TT)
                dve.wait_ge(hi_done, n + 1)
                at = (slice(None), slice(c * BK, (c + 1) * BK), slice(t * P, (t + 1) * P))
                nc.vector.tensor_tensor(mt_lo[at], turned[n % 2][:], mt_hi[at].bitcast(F32),
                                        ALU.subtract).then_inc(lo_done, 1)

            for c in range(2):
                for q in range(QT):
                    w_lower(c, q)
                for t in range(TT):
                    n = c * TT + t
                    combine(n)
                    if n >= 1:
                        lower(n - 1)
            lower(2 * TT - 1)

        @block.tensor
        def _(pe):
            def branch(n, s, hi, lo, done):
                c, t = divmod(n, TT)
                toks = slice(t * P, (t + 1) * P)
                for k in range(BK):
                    q = (s * BK + k) // SL
                    if t == 0 and k % SL == 0:
                        pe.wait_ge(w_lo_done, c * QT + q + 1)
                    last = three_passes(nc, acc[n % 2][s][:], hi[:, k, toks], lo[:, k, toks],
                                        w_hi[:, s * BK + k, :], w_lo[:, s * BK + k, :], k == 0, k == BK - 1)
                last.then_inc(done, 1)
                return last

            def turn(n):
                pe.wait_ge(added, n + 1)
                wait(pe, lo_done, n - 1)
                for j in range(BK):
                    last = nc.tensor.transpose(turned[n % 2][:, j, :], merged[:, n % 2, j * P:(j + 1) * P], ident[:])
                last.then_inc(transposed, 1)

            pe.wait_ge(id_loaded, 16)
            for n in range(2 * TT):
                wait(pe, added, n - 1)
                branch(n, 0, attn_hi, attn_lo, attn_done)
                branch(n, 1, pool_hi, pool_lo, pool_done)
                if n >= 1:
                    turn(n - 1)
            turn(2 * TT - 1)


def output_and_norm(nc, consts, x, w_o, norm2_g, w_rg, w_re, mt_hi, mt_lo, logits_t, x1_dram, h2_dram):
    with ExitStack() as ctx:
        m = Scope(nc, ctx, "out")
        QT, SL = 4, KC // 4
        ident = m.sb("ident", [P, P])
        raw = m.sb("raw", [P, 2, SL, NW])
        w_hi = m.sb("w_hi", [P, 2, KC, NW], F32R)
        w_lo = m.sb("w_lo", [P, 2, KC, NW], F32R)
        xin = m.sb("xin", [P, 2, NW])
        x1 = m.sb("x1", [P, TT, D])
        g = m.sb("g", [P, D])
        squares = m.sb("squares", [P, D])
        ssq, var = m.sb("ssq", [P, TT]), m.sb("var", [P, TT])
        dev, rstd = m.sb("dev", [P, TT]), m.sb("rstd", [P, TT])
        h2 = m.sb("h2", [P, 2, D])
        h2t = m.sb("h2t", [P, 2, KC, P])
        router = m.sb("router", [P, KC, NR])
        acc = [m.ps(f"acc{b}", [P, NW]) for b in range(4)]
        turned = m.ps("turned", [P, KC, P])
        logit = m.ps("logit", [NR, NW])
        c_loaded, r_loaded = m.sem("c_loaded"), m.sem("r_loaded")
        raw_loaded, x_loaded = m.sems("raw_loaded", 2), m.sems("x_loaded", 2)
        w_hi_done, w_lo_done = m.sem("w_hi_done"), m.sem("w_lo_done")
        projected, added, squared = m.sem("projected"), m.sem("added"), m.sem("squared")
        var_done, dev_done, rstd_done, normed = m.sem("var_done"), m.sem("dev_done"), m.sem("rstd_done"), m.sem("normed")
        x1_stored, h2_stored = m.sem("x1_stored"), m.sems("h2_stored", 2)
        transposed, t_copied, routed, l_copied = m.sem("transposed"), m.sem("t_copied"), m.sem("routed"), m.sem("l_copied")
        rows = w_o[0].rearrange("(k p) n -> p k n", p=P)
        block = ctx.enter_context(nc.Block())

        @block.sync
        def _(sp):
            def weights(c, quarters):
                for q in quarters:
                    wait(sp, w_lo_done, c * QT + q - 1)
                    sp.dma_start(raw[:, q % 2], rows[:, q * SL:(q + 1) * SL, c * NW:(c + 1) * NW]
                                 ).then_inc(raw_loaded[q % 2], 16)

            def store(t):
                sp.wait_ge(added, TT + t + 1)
                sp.dma_start(x1_dram[t * P:(t + 1) * P, :], x1[:, t, :]).then_inc(x1_stored, 16)
                sp.wait_ge(normed, t + 1)
                sp.dma_start(h2_dram[t * P:(t + 1) * P, :], h2[:, t % 2, :]).then_inc(h2_stored[t % 2], 16)

            weights(0, range(QT))
            for n in range(2 * TT):
                c, t = divmod(n, TT)
                wait(sp, added, n - 1)
                sp.dma_start(xin[:, n % 2, :], x[0, t * P:(t + 1) * P, c * NW:(c + 1) * NW]
                             ).then_inc(x_loaded[n % 2], 16)
                if n == 0:
                    sp.dma_start(ident[:], consts[:, C_ID:C_ID + P]).then_inc(c_loaded, 16)
                    sp.dma_start(g[:], norm2_g[0:1, :].to_broadcast([P, D])).then_inc(c_loaded, 16)
                    sp.dma_start(router[:, :, 0:NG], w_rg[0].rearrange("(p c) e -> p c e", c=KC)).then_inc(r_loaded, 16)
                    for e in range(NG):
                        sp.dma_start(router[:, :, NG + e * NE:NG + (e + 1) * NE],
                                     w_re[0, e].rearrange("(p c) e -> p c e", c=KC)).then_inc(r_loaded, 16)
                if n % 2 and n < TT:
                    weights(1, (n // 2,))
                if c == 1 and t >= 3:
                    store(t - 3)
            for t in range(TT - 3, TT):
                store(t)
            sp.wait_ge(x1_stored, 16 * TT)
            for b in range(2):
                sp.wait_ge(h2_stored[b], 16 * TT // 2)

        @block.scalar
        def _(act):
            def square(t):
                act.wait_ge(added, TT + t + 1)
                wait(act, squared, t)
                nc.scalar.activation(squares[:], x1[:, t, :], ACT.Square, accum_out=ssq[:, t:t + 1]).then_inc(squared, 1)

            def root(t):
                act.wait_ge(var_done, t + 1)
                nc.scalar.activation(dev[:, t:t + 1], var[:, t:t + 1], ACT.Sqrt).then_inc(dev_done, 1)

            def copy_turned(t):
                act.wait_ge(transposed, t + 1)
                wait(act, routed, t - 1)
                nc.scalar.copy(h2t[:, t % 2], turned[:]).then_inc(t_copied, 1)

            def copy_logits(t):
                act.wait_ge(routed, t + 1)
                nc.scalar.copy(logits_t[0:NR, t * P:(t + 1) * P], logit[:, 0:P]).then_inc(l_copied, 1)

            for c in range(2):
                for q in range(QT):
                    act.wait_ge(raw_loaded[q % 2], 16 * (c * 2 + q // 2 + 1))
                    nc.scalar.copy(w_hi[:, c, q * SL:(q + 1) * SL, :], raw[:, q % 2]).then_inc(w_hi_done, 1)
            for t in range(TT + 3):
                if t < TT:
                    square(t)
                if 1 <= t <= TT:
                    root(t - 1)
                if 2 <= t < TT + 2:
                    copy_turned(t - 2)
                if t >= 3:
                    copy_logits(t - 3)

        @block.vector
        def _(dve):
            def w_lower(c, q):
                dve.wait_ge(w_hi_done, c * QT + q + 1)
                nc.vector.tensor_tensor(w_lo[:, c, q * SL:(q + 1) * SL, :], raw[:, q % 2],
                                        w_hi[:, c, q * SL:(q + 1) * SL, :].bitcast(F32), ALU.subtract
                                        ).then_inc(w_lo_done, 1)

            def add(n):
                c, t = divmod(n, TT)
                dve.wait_ge(x_loaded[n % 2], 16 * (n // 2 + 1))
                dve.wait_ge(projected, n + 1)
                nc.vector.tensor_tensor(x1[:, t, c * NW:(c + 1) * NW], acc[n % 4][:], xin[:, n % 2, :],
                                        ALU.add).then_inc(added, 1)

            def norm(t):
                at = slice(t, t + 1)
                dve.wait_ge(squared, t + 1)
                nc.vector.tensor_scalar(var[:, at], ssq[:, at], 1.0 / D, EPS, ALU.mult, ALU.add).then_inc(var_done, 1)
                dve.wait_ge(dev_done, t + 1)
                nc.vector.reciprocal(rstd[:, at], dev[:, at]).then_inc(rstd_done, 1)
                dve.wait_ge(rstd_done, t + 1)
                wait(dve, transposed, t - 1)
                wait(dve, h2_stored[t % 2], 16 * (t // 2))
                nc.vector.scalar_tensor_tensor(
                    out=h2[:, t % 2, :].rearrange("q (c p) -> q p c", c=KC), in0=x1[:, t, :].rearrange("q (p c) -> q p c", c=KC),
                    scalar=rstd[:, at], in1=g[:].rearrange("q (p c) -> q p c", c=KC), op0=ALU.mult, op1=ALU.mult
                ).then_inc(normed, 1)

            for q in range(QT):
                w_lower(0, q)
            dve.wait_ge(c_loaded, 32)
            for n in range(2 * TT):
                add(n)
                if n % 2 and n < TT:
                    w_lower(1, n // 2)
                if n > TT:
                    norm(n - TT - 1)
            norm(TT - 1)

        @block.tensor
        def _(pe):
            def products(n):
                c, t = divmod(n, TT)
                toks = slice(t * P, (t + 1) * P)
                wait(pe, added, n - 3)
                for k in range(KC):
                    if t == 0 and k % SL == 0:
                        pe.wait_ge(w_lo_done, c * QT + k // SL + 1)
                    last = three_passes(nc, acc[n % 4][:], mt_hi[:, k, toks], mt_lo[:, k, toks],
                                        w_hi[:, c, k, :], w_lo[:, c, k, :], k == 0, k == KC - 1)
                last.then_inc(projected, 1)

            def turn(t):
                pe.wait_ge(normed, t + 1)
                wait(pe, t_copied, t)
                for k in range(KC):
                    last = nc.tensor.transpose(turned[:, k, :], h2[:, t % 2, k * P:(k + 1) * P], ident[:])
                last.then_inc(transposed, 1)

            def route(t):
                pe.wait_ge(t_copied, t + 1)
                wait(pe, l_copied, t)
                for k in range(KC):
                    last = nc.tensor.matmul(logit[:, 0:P], router[:, k, :], h2t[:, t % 2, k, :],
                                            start=(k == 0), stop=(k == KC - 1))
                last.then_inc(routed, 1)

            for n in range(2 * TT + 3):
                t = n - TT
                if n < 2 * TT:
                    products(n)
                if n == TT:
                    pe.wait_ge(c_loaded, 32)
                    pe.wait_ge(r_loaded, 16 * (1 + NG))
                if 2 <= t < TT + 2:
                    turn(t - 2)
                if t >= 3:
                    route(t - 3)


class ExpertBlocks:

    HALF = D * FH // P // 2

    def __init__(self, nc, m, w_gate, w_up, w_down, h2_dram, y_dram, idx, idx_ready, ident, slots, psum):
        self.nc, self.slots, self.idx, self.idx_ready, self.ident = nc, slots, idx, idx_ready, ident
        self.h2_dram, self.y_dram = h2_dram, y_dram
        self.w = (w_gate, w_up, w_down)
        self.raw = m.sb("raw", [P, 6, self.HALF])
        self.w_hi = m.sb("w_hi", [P, 6, self.HALF], F32R)
        self.w_lo = m.sb("w_lo", [P, 6, self.HALF], F32R)
        self.rows = m.sb("rows", [P, slots, D])
        self.row_of = [m.sb(f"row_of{b}", [P, 1], U32) for b in range(slots)]
        self.xt_hi = m.sb("xt_hi", [P, slots, KC, P], F32R)
        self.xt_lo = m.sb("xt_lo", [P, slots, KC, P], F32R)
        self.act = m.sb("act", [P, FH])
        self.hid = m.sb("hid", [P, FH])
        self.ht_hi = m.sb("ht_hi", [P, FC, P], F32R)
        self.ht_lo = m.sb("ht_lo", [P, FC, P], F32R)
        self.y = m.sb("y", [P, slots, D])
        self.xt_ps, self.gate_ps, self.up_ps, self.ht_ps, self.y_ps = psum
        self.loaded = m.sems("loaded", 6)
        self.w_hi_done = m.sems("w_hi_done", 6)
        self.w_lo_done = m.sems("w_lo_done", 6)
        self.used = m.sems("used", 6)
        self.row_ready = m.sem("row_ready")
        self.gathered = m.sems("gathered", slots)
        self.stored = m.sems("stored", slots)
        self.x_turned, self.x_hi_done, self.x_lo_done = m.sem("x_turned"), m.sem("x_hi_done"), m.sem("x_lo_done")
        self.act_done, self.hid_done = m.sem("act_done"), m.sem("hid_done")
        self.h_turned, self.h_hi_done, self.h_lo_done = m.sem("h_turned"), m.sem("h_hi_done"), m.sem("h_lo_done")
        self.y_copied = m.sem("y_copied")

    def counts_of_blocks(self):
        return [*self.w_hi_done, *self.w_lo_done, *self.used, self.row_ready, self.x_turned, self.x_hi_done,
                self.x_lo_done, self.act_done, self.hid_done, self.h_turned, self.h_hi_done, self.h_lo_done,
                self.y_copied]

    def counts_of_dmas(self):
        return [*self.loaded, *self.gathered, *self.stored]


    def load(self, sp, i, expert, mats):
        for h in [2 * w + j for w in mats for j in range(2)]:
            src = self.w[h // 2][0, expert].rearrange("(p c) n -> p (c n)", p=P)
            wait(sp, self.w_lo_done[h], i)
            sp.dma_start(self.raw[:, h, :], src[:, (h % 2) * self.HALF:(h % 2 + 1) * self.HALF]
                         ).then_inc(self.loaded[h], 16)

    def gather(self, pool, i, b, n, column):
        wait(pool, self.x_turned, i + 1 - self.slots if not isinstance(i, int) or i >= self.slots else 0)
        self.nc.gpsimd.tensor_copy(self.row_of[b][:], self.idx[:, bass.ds(column, 1)]).then_inc(self.row_ready, 1)
        rows_due = held_value(pool, i + 1)
        pool.wait_ge(self.idx_ready, 16)
        pool.wait_ge(self.row_ready, rows_due)
        pool.indirect_dma_start(out=self.rows[:, b, :], out_offset=None, in_=self.h2_dram,
                                in_offset=bass.IndirectOffsetOnAxis(ap=self.row_of[b][:, 0:1], axis=0)
                                ).then_inc(self.gathered[b], 16)

    def turn_x(self, pe, i, b, n):
        pe.wait_ge(self.gathered[b], n * 16 + 16)
        wait(pe, self.x_lo_done, i)
        for k in range(KC):
            last = self.nc.tensor.transpose(self.xt_ps[:, k, :], self.rows[:, b, k * P:(k + 1) * P], self.ident[:])
        last.then_inc(self.x_turned, 1)

    def x_upper(self, act, i, b):
        act.wait_ge(self.x_turned, i + 1)
        wait(act, self.used[3], i + 1 - self.slots if not isinstance(i, int) or i >= self.slots else 0)
        self.nc.scalar.copy(self.xt_hi[:, b], self.xt_ps[:]).then_inc(self.x_hi_done, 1)

    def x_lower(self, dve, i, b):
        dve.wait_ge(self.x_hi_done, i + 1)
        self.nc.vector.tensor_tensor(self.xt_lo[:, b], self.xt_ps[:], self.xt_hi[:, b].bitcast(F32),
                                     ALU.subtract).then_inc(self.x_lo_done, 1)

    def w_upper(self, act, i, h):
        act.wait_ge(self.loaded[h], i * 16 + 16)
        wait(act, self.used[h], i)
        self.nc.scalar.copy(self.w_hi[:, h, :], self.raw[:, h, :]).then_inc(self.w_hi_done[h], 1)

    def w_lower(self, dve, i, h):
        dve.wait_ge(self.w_hi_done[h], i + 1)
        self.nc.vector.tensor_tensor(self.w_lo[:, h, :], self.raw[:, h, :], self.w_hi[:, h, :].bitcast(F32),
                                     ALU.subtract).then_inc(self.w_lo_done[h], 1)

    def into_hidden(self, pe, i, b, mat, half):
        if half == 0:
            if mat == 0:
                pe.wait_ge(self.x_lo_done, i + 1)
            wait(pe, (self.act_done, self.hid_done)[mat], i)
        h = 2 * mat + half
        pe.wait_ge(self.w_lo_done[h], i + 1)
        for j in range(KC // 2):
            k = half * (KC // 2) + j
            cols = slice(j * FH, (j + 1) * FH)
            last = three_passes(self.nc, (self.gate_ps, self.up_ps)[mat][:], self.xt_hi[:, b, k], self.xt_lo[:, b, k],
                                self.w_hi[:, h, cols], self.w_lo[:, h, cols], k == 0, k == KC - 1)
        last.then_inc(self.used[h], 1)

    def silu(self, act, i):
        act.wait_ge(self.used[1], i + 1)
        wait(act, self.hid_done, i)
        self.nc.scalar.activation(self.act[:], self.gate_ps[:], ACT.Silu).then_inc(self.act_done, 1)

    def hidden(self, dve, i):
        dve.wait_ge(self.act_done, i + 1)
        dve.wait_ge(self.used[3], i + 1)
        wait(dve, self.h_turned, i)
        self.nc.vector.tensor_tensor(self.hid[:].rearrange("q (c p) -> q p c", c=FC),
                                     self.up_ps[:].rearrange("q (p c) -> q p c", c=FC),
                                     self.act[:].rearrange("q (p c) -> q p c", c=FC), ALU.mult
                                     ).then_inc(self.hid_done, 1)

    def turn_h(self, pe, i):
        pe.wait_ge(self.hid_done, i + 1)
        wait(pe, self.h_lo_done, i)
        for k in range(FC):
            last = self.nc.tensor.transpose(self.ht_ps[:, k, :], self.hid[:, k * P:(k + 1) * P], self.ident[:])
        last.then_inc(self.h_turned, 1)

    def h_upper(self, act, i):
        act.wait_ge(self.h_turned, i + 1)
        wait(act, self.used[5], i)
        self.nc.scalar.copy(self.ht_hi[:], self.ht_ps[:]).then_inc(self.h_hi_done, 1)

    def h_lower(self, dve, i):
        dve.wait_ge(self.h_hi_done, i + 1)
        self.nc.vector.tensor_tensor(self.ht_lo[:], self.ht_ps[:], self.ht_hi[:].bitcast(F32),
                                     ALU.subtract).then_inc(self.h_lo_done, 1)

    def down(self, pe, i):
        pe.wait_ge(self.h_lo_done, i + 1)
        wait(pe, self.y_copied, i)
        for half in range(2):
            h = 4 + half
            pe.wait_ge(self.w_lo_done[h], i + 1)
            for j in range(FC // 2):
                k = half * (FC // 2) + j
                for c in range(D // NW):
                    cols = slice(j * D + c * NW, j * D + (c + 1) * NW)
                    last = three_passes(self.nc, self.y_ps[:, c, :], self.ht_hi[:, k], self.ht_lo[:, k],
                                        self.w_hi[:, h, cols], self.w_lo[:, h, cols], k == 0, k == FC - 1)
            last.then_inc(self.used[h], 1)

    def copy_y(self, act, i, b, n, block):
        act.wait_ge(self.used[5], i + 1)
        wait(act, self.stored[b], n * 16)
        self.nc.scalar.copy(self.y[:, b, :], self.y_ps[:].rearrange("p c n -> p (c n)")).then_inc(self.y_copied, 1)
        act.wait_ge(self.y_copied, i + 1)
        act.dma_start(self.y_dram[bass.ds(block * P, P), :], self.y[:, b, :]).then_inc(self.stored[b], 16)


def psum_of_experts(m):
    return (m.ps("xt", [P, KC, P]), m.ps("gate", [P, FH]), m.ps("up", [P, FH]), m.ps("ht", [P, FC, P]),
            m.ps("y", [P, D // NW, NW]))


def route_and_experts(nc, consts, b_rg, b_re, w_gate, w_up, w_down, logits_t, idx, slot_of, gates, over,
                      h2_dram, y_dram, idx_dram):
    with ExitStack() as ctx:
        m = Scope(nc, ctx, "moe")
        ident, tri, ones = m.sb("ident", [P, P]), m.sb("tri", [P, P]), m.sb("ones", [P, P])
        small = m.sb("small", [P, C_LOG - C_D4])
        bias = m.sb("bias", [P, NR])
        logits = m.sb("logits", [P, TT, NR])
        g_max, g_sum, g_gate, g_key = (m.sb(n, [P, TT]) for n in ("g_max", "g_sum", "g_gate", "g_key"))
        g_one, g_exp = m.sb("g_one", [P, TT, NG]), m.sb("g_exp", [P, TT, NG])
        e_all = m.sb("e_all", [P, TT, NG, NE])
        e_logit = m.sb("e_logit", [P, 2, TT, NE])
        e_max, e_key = m.sb("e_max", [P, 2, TT]), m.sb("e_key", [P, 2, TT])
        e_one = m.sb("e_one", [P, 2, TT, NE])
        ratio, total = m.sb("ratio", [P, TT]), m.sb("total", [P, TT])
        chosen = m.sb("chosen", [P, 2, TT, E])
        both = m.sb("both", [P, TT, E])
        before = m.sb("before", [P, TT + 1, E])
        rank_all = m.sb("rank_all", [P, TT, E])
        pick = m.sb("pick", [P, 2, TT, E])
        rank, eid, base, beyond, many = (m.sb(n, [P, 2, TT]) for n in ("rank", "eid", "base", "beyond", "many"))
        column, slot_f, at_f = (m.sb(n, [P, 2, TT]) for n in ("column", "slot_f", "at_f"))
        at = m.sb("at", [P, 2, TT], U32)
        count, more, end, begin = (m.sb(n, [P, E]) for n in ("count", "more", "end", "begin"))
        ended = m.sb("ended", [P, MOST, E])
        over_f = m.sb("over_f", [P, 1 + MOST])
        tok = m.sb("tok", [P, TT], I32)
        zeros = m.sb("zeros", [P, NB], I32)
        psum = psum_of_experts(m)
        by_token = psum[3][:].rearrange("p a b -> p (a b)").rearrange("p (t e) -> p t e", t=TT)
        rank_ps = psum[1][:, 0:TT * E].rearrange("p (t e) -> p t e", t=TT)
        count_ps = psum[2][:, 0:E]
        c_loaded, b_loaded = m.sem("c_loaded"), m.sem("b_loaded")
        l_turned, near, exp_done = m.sem("l_turned"), m.sem("near"), m.sem("exp_done")
        link_sem, chosen_done, ranked = m.sem("link"), m.sem("chosen_done"), m.sem("ranked")
        at_done, zeroed, cleared, scattered, idx_loaded = (m.sem("at_done"), m.sem("zeroed"), m.sem("cleared"),
                                                           m.sem("scattered"), m.sem("idx_loaded"))
        x = ExpertBlocks(nc, m, w_gate, w_up, w_down, h2_dram, y_dram, idx, idx_loaded, ident, 2, psum)
        o = -C_D4
        d4, d8 = small[:, C_D4 + o:C_D8 + o], small[:, C_D8 + o:C_EID + o]
        eids, th, toks = small[:, C_EID + o:C_TH + o], small[:, C_TH + o:C_TOK + o], small[:, C_TOK + o:C_LOG + o]
        block = ctx.enter_context(nc.Block())

        @block.sync
        def _(sp):
            x.load(sp, 0, 0, (0, 1))
            sp.dma_start(ident[:], consts[:, C_ID:C_ID + P]).then_inc(c_loaded, 16)
            sp.dma_start(tri[:], consts[:, C_TRI:C_TRI + P]).then_inc(c_loaded, 16)
            sp.dma_start(ones[:], consts[:, C_ONE:C_ONE + P]).then_inc(c_loaded, 16)
            sp.dma_start(small[:], consts[:, C_D4:C_LOG]).then_inc(c_loaded, 16)
            sp.dma_start(bias[:, 0:NG], b_rg[0:1, :].to_broadcast([P, NG])).then_inc(b_loaded, 16)
            sp.dma_start(bias[:, NG:NR], b_re.rearrange("a g e -> a (g e)").to_broadcast([P, E])).then_inc(b_loaded, 16)
            def further(i):
                x.load(sp, i, i, (0,))
                x.load(sp, i - 1, i - 1, (2,))
                x.load(sp, i, i, (1,))

            further(1)
            with sp.Fori(2, E) as i:
                further(i)
            x.load(sp, E - 1, E - 1, (2,))

        @block.gpsimd
        def _(pool):
            nc.gpsimd.memset(zeros[:], 0).then_inc(zeroed, 1)
            pool.wait_ge(zeroed, 1)
            pool.dma_start(idx_dram.rearrange("(p b) a -> p (b a)", p=P), zeros[:]).then_inc(cleared, 16)
            pool.wait_ge(cleared, 16)
            pool.wait_ge(at_done, 1)
            for k in range(2):
                for t in range(TT):
                    pool.indirect_dma_start(
                        out=idx_dram, out_offset=bass.IndirectOffsetOnAxis(ap=at[:, k, t:t + 1], axis=0),
                        in_=tok[:, t:t + 1], in_offset=None).then_inc(scattered, 16)
            pool.wait_ge(scattered, 16 * 2 * TT)
            pool.dma_start(idx[:], idx_dram.rearrange("(p b) a -> p (b a)", p=P)).then_inc(idx_loaded, 16)
            pool.wait_ge(idx_loaded, 16)
            x.gather(pool, 0, 0, 0, 0)
            x.gather(pool, 1, 1, 0, 1)
            with pool.Fori(1, E // 2) as j:
                x.gather(pool, j * 2, 0, j, j * 2)
                x.gather(pool, j * 2 + 1, 1, j, j * 2 + 1)

        @block.scalar
        def _(act):
            def step(i, b, n, first=False, last=False):
                before_1, after_1 = (n, n + 1) if b else (n - 1, n)
                if not first:
                    x.w_upper(act, i - 1, 4)
                    x.h_upper(act, i - 1)
                    x.w_upper(act, i - 1, 5)
                x.w_upper(act, i, 2)
                x.silu(act, i)
                x.w_upper(act, i, 3)
                if not last:
                    x.w_upper(act, i + 1, 0)
                if not first:
                    x.copy_y(act, i - 1, 1 - b, before_1, i - 1)
                if not last:
                    x.x_upper(act, i + 1, 1 - b)
                    x.w_upper(act, i + 1, 1)

            act.wait_ge(near, 1)
            nc.scalar.activation(g_exp[:], g_exp[:], ACT.Exp).then_inc(exp_done, 1)
            act.wait_ge(near, 2)
            nc.scalar.activation(ratio[:], ratio[:], ACT.Exp).then_inc(exp_done, 1)
            x.w_upper(act, 0, 0)
            x.w_upper(act, 0, 1)
            x.x_upper(act, 0, 0)
            step(0, 0, 0, first=True)
            step(1, 1, 0)
            step(2, 0, 1)
            with act.Fori(1, E // 2 - 1) as j:
                step(j * 2 + 1, 1, j)
                step(j * 2 + 2, 0, j + 1)
            step(E - 1, 1, E // 2 - 1, last=True)
            x.w_upper(act, E - 1, 4)
            x.h_upper(act, E - 1)
            x.w_upper(act, E - 1, 5)
            x.copy_y(act, E - 1, 1, E // 2 - 1, E - 1)
            for b in range(2):
                act.wait_ge(x.stored[b], 16 * E // 2)

        @block.vector
        def _(dve):
            v = nc.vector
            link = Chain(dve, link_sem)

            def wide(a, n):
                return a.unsqueeze(len(a.shape)).to_broadcast([*a.shape, n])

            def rows(a, *shape):
                for _ in range(len(shape) - 1):
                    a = a.unsqueeze(1)
                return a.to_broadcast([P, *shape])

            def first_of(values, most, key, one, order):
                n = values.shape[-1]
                link(v.tensor_reduce(most, values, AX_X, ALU.max))
                link(v.tensor_tensor(one, values, wide(most, n), ALU.is_equal))
                link(v.tensor_tensor(one, one, rows(order, TT, n), ALU.mult))
                link(v.tensor_reduce(key, one, AX_X, ALU.max))
                link(v.tensor_tensor(one, one, wide(key, n), ALU.is_equal))

            dve.wait_ge(c_loaded, 64)
            dve.wait_ge(b_loaded, 32)
            dve.wait_ge(l_turned, 1)
            link(v.tensor_tensor(logits[:], by_token[:, :, 0:NR], rows(bias[:], TT, NR), ALU.add))
            gl = logits[:, :, 0:NG]
            first_of(gl, g_max[:], g_key[:], g_one[:], d4)
            v.tensor_tensor(g_exp[:], gl, wide(g_max[:], NG), ALU.subtract).then_inc(near, 1)
            link(v.tensor_tensor(e_all[:], logits[:, :, NG:NR].rearrange("p t (g e) -> p t g e", g=NG),
                                 wide(g_one[:], NE), ALU.mult))
            link(v.tensor_reduce(e_logit[:, 0], e_all[:].rearrange("p t g e -> p t e g"), AX_X, ALU.add))
            first_of(e_logit[:, 0], e_max[:, 0], e_key[:, 0], e_one[:, 0], d8)
            link(v.scalar_tensor_tensor(out=e_logit[:, 1], in0=e_one[:, 0], scalar=-3e38, in1=e_logit[:, 0],
                                        op0=ALU.mult, op1=ALU.add))
            first_of(e_logit[:, 1], e_max[:, 1], e_key[:, 1], e_one[:, 1], d8)
            v.tensor_tensor(ratio[:], e_max[:, 1], e_max[:, 0], ALU.subtract).then_inc(near, 1)
            for k in range(2):
                for g in range(NG):
                    ins = v.tensor_tensor(chosen[:, k, :, g * NE:(g + 1) * NE], e_one[:, k],
                                          wide(g_one[:, :, g], NE), ALU.mult)
                    if (k, g) == (1, NG - 1):
                        link(ins)
            link(v.tensor_tensor(both[:], chosen[:, 0], chosen[:, 1], ALU.add))
            link(v.memset(before[:, 0, :], 0.0))
            for t in range(TT):
                link(v.tensor_tensor(before[:, t + 1, :], before[:, t, :], both[:, t, :], ALU.add))
            v.engine_nop().then_inc(chosen_done, 1)
            dve.wait_ge(exp_done, 2)
            link(v.tensor_reduce(g_sum[:], g_exp[:], AX_X, ALU.add))
            link(v.reciprocal(g_gate[:], g_sum[:]))
            link(v.tensor_scalar(total[:], ratio[:], 1.0, None, ALU.add))
            link(v.reciprocal(total[:], total[:]))
            link(v.tensor_tensor(gates[:, 0, :], g_gate[:], total[:], ALU.mult))
            link(v.tensor_tensor(gates[:, 1, :], gates[:, 0, :], ratio[:], ALU.mult))
            dve.wait_ge(ranked, 1)
            link(v.tensor_copy(count[:], count_ps))
            link(v.tensor_copy(rank_all[:], rank_ps))
            link(v.tensor_scalar(more[:], count[:], float(P), None, ALU.is_gt))
            for k in range(2, TT):
                link(v.scalar_tensor_tensor(out=more[:], in0=count[:], scalar=float(k * P), in1=more[:],
                                            op0=ALU.is_gt, op1=ALU.add))
            link(v.tensor_tensor_scan(end[:], ones[:, 0:E], more[:], 0.0, ALU.mult, ALU.add))
            link(v.tensor_tensor(begin[:], end[:], more[:], ALU.subtract))
            for values, result in ((rank_all, rank), (eids, eid), (begin, base)):
                for k in range(2):
                    ap = values[:] if values is rank_all else rows(values[:] if values is begin else values, TT, E)
                    link(v.tensor_tensor(pick[:, k], chosen[:, k], ap, ALU.mult))
                link(v.tensor_reduce(result[:].rearrange("p k t -> p (k t)"), pick[:].rearrange("p k t e -> p (k t) e"),
                                     AX_X, ALU.add))
            link(v.tensor_scalar(beyond[:], rank[:], float(P), None, ALU.is_ge))
            for k in range(2, TT):
                link(v.scalar_tensor_tensor(out=beyond[:], in0=rank[:], scalar=float(k * P), in1=beyond[:],
                                            op0=ALU.is_ge, op1=ALU.add))
            link(v.tensor_scalar(many[:], beyond[:], 1.0, None, ALU.min))
            link(v.scalar_tensor_tensor(out=column[:], in0=base[:], scalar=float(E - 1), in1=beyond[:],
                                        op0=ALU.add, op1=ALU.add))
            link(v.tensor_tensor(column[:], column[:], eid[:], ALU.subtract))
            link(v.tensor_tensor(column[:], column[:], many[:], ALU.mult))
            link(v.tensor_tensor(column[:], column[:], eid[:], ALU.add))
            link(v.scalar_tensor_tensor(out=rank[:], in0=beyond[:], scalar=-float(P), in1=rank[:],
                                        op0=ALU.mult, op1=ALU.add))
            link(v.scalar_tensor_tensor(out=slot_f[:], in0=column[:], scalar=float(P), in1=rank[:],
                                        op0=ALU.mult, op1=ALU.add))
            link(v.scalar_tensor_tensor(out=at_f[:], in0=rank[:], scalar=float(NB), in1=column[:],
                                        op0=ALU.mult, op1=ALU.add))
            link(v.tensor_copy(slot_of[:], slot_f[:]))
            link(v.tensor_copy(tok[:], toks))
            v.tensor_copy(at[:], at_f[:]).then_inc(at_done, 1)
            link(v.tensor_tensor(ended[:], rows(end[:], MOST, E), wide(th, E), ALU.is_le))
            link(v.tensor_copy(over_f[:, 0:1], end[:, E - 1:E]))
            link(v.tensor_reduce(over_f[:, 1:], ended[:], AX_X, ALU.add))
            link(v.tensor_scalar(over_f[:, 1:], over_f[:, 1:], float(E - 1), None, ALU.min))
            link(v.tensor_copy(over[:], over_f[:]))

            def step(i, first=False, last=False):
                b = None
                if not first:
                    x.hidden(dve, i - 1)
                    x.w_lower(dve, i - 1, 4)
                    x.h_lower(dve, i - 1)
                    x.w_lower(dve, i - 1, 5)
                x.w_lower(dve, i, 2)
                x.w_lower(dve, i, 3)

            def ahead(i, b):
                x.w_lower(dve, i, 0)
                x.x_lower(dve, i, b)
                x.w_lower(dve, i, 1)

            x.w_lower(dve, 0, 0)
            x.w_lower(dve, 0, 1)
            x.x_lower(dve, 0, 0)
            step(0, first=True)
            ahead(1, 1)
            step(1)
            ahead(2, 0)
            step(2)
            ahead(3, 1)
            with dve.Fori(1, E // 2 - 1) as j:
                step(j * 2 + 1)
                ahead(j * 2 + 2, 0)
                step(j * 2 + 2)
                ahead(j * 2 + 3, 1)
            step(E - 1)
            x.hidden(dve, E - 1)
            x.w_lower(dve, E - 1, 4)
            x.h_lower(dve, E - 1)
            x.w_lower(dve, E - 1, 5)

        @block.tensor
        def _(pe):
            pe.wait_ge(c_loaded, 64)
            for t in range(TT):
                last = nc.tensor.transpose(by_token[:, t, 0:NR], logits_t[0:NR, t * P:(t + 1) * P],
                                           ident[0:NR, 0:NR])
            last.then_inc(l_turned, 1)
            pe.wait_ge(chosen_done, 1)
            nc.tensor.matmul(psum[1][:, 0:TT * E], tri[:], both[:].rearrange("p t e -> p (t e)"), start=True, stop=False)
            nc.tensor.matmul(psum[1][:, 0:TT * E], ones[:], before[:, 0:TT, :].rearrange("p t e -> p (t e)"),
                             start=False, stop=True)
            nc.tensor.matmul(count_ps, ones[:], before[:, TT, :], start=True, stop=True).then_inc(ranked, 1)

            def step(i, b, n, first=False, last=False):
                x.into_hidden(pe, i, b, 0, 0)
                if not first:
                    x.turn_h(pe, i - 1)
                x.into_hidden(pe, i, b, 0, 1)
                if not first:
                    x.down(pe, i - 1)
                if not last:
                    x.turn_x(pe, i + 1, 1 - b, n + 1 if b else n)
                x.into_hidden(pe, i, b, 1, 0)
                x.into_hidden(pe, i, b, 1, 1)

            x.turn_x(pe, 0, 0, 0)
            pe.wait_ge(at_done, 1)
            step(0, 0, 0, first=True)
            step(1, 1, 0)
            step(2, 0, 1)
            with pe.Fori(1, E // 2 - 1) as j:
                step(j * 2 + 1, 1, j)
                step(j * 2 + 2, 0, j + 1)
            step(E - 1, 1, E // 2 - 1, last=True)
            x.turn_h(pe, E - 1)
            x.down(pe, E - 1)


def blocks_beyond(nc, consts, w_gate, w_up, w_down, idx, over, h2_dram, y_dram):
    with ExitStack() as ctx:
        m = Scope(nc, ctx, "beyond")
        ident = m.sb("ident", [P, P])
        id_loaded, started = m.sem("id_loaded"), m.sem("started")
        x = ExpertBlocks(nc, m, w_gate, w_up, w_down, h2_dram, y_dram, idx, id_loaded, ident, 1, psum_of_experts(m))
        block = ctx.enter_context(nc.Block())

        def each(eng, body):
            n = eng.value_load(over[0:1, 0:1], min_val=0, max_val=MOST - 1)
            with eng.If(n > 0):
                if eng is nc.gpsimd:
                    for s in x.counts_of_blocks():
                        eng.sem_inc(s, 1)
                    for s in x.counts_of_dmas():
                        eng.sem_inc(s, 16)
                    eng.sem_inc(started, 1)
                eng.wait_ge(started, 1)
                with eng.Fori(1, n + 1) as i:
                    body(i)

        @block.sync
        def _(sp):
            sp.dma_start(ident[:], consts[:, C_ID:C_ID + P]).then_inc(id_loaded, 16)

            def body(i):
                expert = sp.value_load(over[0:1, bass.ds(i, 1)], min_val=0, max_val=E - 1)
                x.load(sp, i, expert, (0, 1, 2))

            each(sp, body)

        @block.gpsimd
        def _(pool):
            each(pool, lambda i: x.gather(pool, i, 0, i, i + E - 1))

        @block.scalar
        def _(act):
            def body(i):
                x.x_upper(act, i, 0)
                for h in range(4):
                    x.w_upper(act, i, h)
                x.silu(act, i)
                x.w_upper(act, i, 4)
                x.w_upper(act, i, 5)
                x.h_upper(act, i)
                x.copy_y(act, i, 0, i, i + E - 1)
                act.wait_ge(x.stored[0], i * 16 + 16)

            each(act, body)

        @block.vector
        def _(dve):
            def body(i):
                x.x_lower(dve, i, 0)
                for h in range(4):
                    x.w_lower(dve, i, h)
                x.w_lower(dve, i, 4)
                x.w_lower(dve, i, 5)
                x.hidden(dve, i)
                x.h_lower(dve, i)

            each(dve, body)

        @block.tensor
        def _(pe):
            pe.wait_ge(id_loaded, 16)

            def body(i):
                x.turn_x(pe, i, 0, i)
                for mat in range(2):
                    for half in range(2):
                        x.into_hidden(pe, i, 0, mat, half)
                x.turn_h(pe, i)
                x.down(pe, i)

            each(pe, body)


def clear_released_semaphores(nc):
    ids = sorted(nc.released_uncleared_semaphores)
    first = [i for i in ids if i - 1 not in ids]
    last = [i for i in ids if i + 1 not in ids]
    with nc.Block() as block:
        @block.gpsimd
        def _(pool):
            for a, b in zip(first, last):
                pool.sem_clear(range(a, b + 1))


def combine(nc, slot_of, gates, x1_dram, y_dram, out):
    with ExitStack() as ctx:
        m = Scope(nc, ctx, "sum")
        NS = 4
        x1 = m.sb("x1", [P, NS, D])
        y = m.sb("y", [P, NS, 2, D])
        x_loaded, y_loaded = m.sems("x_loaded", NS), m.sems("y_loaded", NS)
        first, added, stored = m.sem("first"), m.sem("added"), m.sems("stored", NS)
        block = ctx.enter_context(nc.Block())

        @block.sync
        def _(sp):
            for t in range(TT):
                if t >= NS:
                    sp.wait_ge(stored[t % NS], 16 * (t // NS))
                sp.dma_start(x1[:, t % NS, :], x1_dram[t * P:(t + 1) * P, :]).then_inc(x_loaded[t % NS], 16)

        @block.gpsimd
        def _(pool):
            for t in range(TT):
                wait(pool, added, t - NS + 1)
                for k in range(2):
                    pool.indirect_dma_start(
                        out=y[:, t % NS, k, :], out_offset=None, in_=y_dram,
                        in_offset=bass.IndirectOffsetOnAxis(ap=slot_of[:, k, t:t + 1], axis=0)
                    ).then_inc(y_loaded[t % NS], 16)

        @block.vector
        def _(dve):
            for t in range(TT):
                s = t % NS
                dve.wait_ge(x_loaded[s], 16 * (t // NS + 1))
                dve.wait_ge(y_loaded[s], 32 * (t // NS + 1))
                for k, done in ((0, first), (1, added)):
                    nc.vector.scalar_tensor_tensor(out=x1[:, s, :], in0=y[:, s, k, :], scalar=gates[:, k, t:t + 1],
                                                   in1=x1[:, s, :], op0=ALU.mult, op1=ALU.add).then_inc(done, 1)
                    if k == 0:
                        dve.wait_ge(first, t + 1)

        @block.scalar
        def _(act):
            for t in range(TT):
                act.wait_ge(added, t + 1)
                act.dma_start(out[0, t * P:(t + 1) * P, :], x1[:, t % NS, :]).then_inc(stored[t % NS], 16)
            for s in range(NS):
                act.wait_ge(stored[s], 16 * TT // NS)


def decoder_layer(nc, x, norm1_g, w_in, q_norm_g, k_norm_g, w_attn_out, w_pool_mix, pool_scale, w_pool_out, w_o,
                  norm2_g, w_rg, b_rg, w_re, b_re, w_gate, w_up, w_down, consts, out):
    def dram(name, shape, dt=F32):
        return nc.dram_tensor(name, shape, dt).ap()

    u_dram = dram("u_scratch", [PG, P, S])
    gates_dram = dram("gates_scratch", [S, 2 * D])
    x1_dram = dram("x1_scratch", [S, D])
    h2_dram = dram("h2_scratch", [S, D])
    y_dram = dram("y_scratch", [NB * P, D])
    idx_dram = dram("idx_scratch", [P * NB, 1], I32)

    def held(ctx, side, *tensors):
        return [ctx.enter_context(nc.sbuf_tensor(n, s, d, side=side)) for n, s, d in tensors]

    heads, merged, branches, qkv_held = ExitStack(), ExitStack(), ExitStack(), ExitStack()
    with ExitStack() as small:
        h_hi, h_lo = held(heads, "left", ("h_hi", [P, KC, S], F32R), ("h_lo", [P, KC, S], F32R))
        norm_and_transpose(nc, x, norm1_g, consts, h_hi, h_lo)
        qkv, rqk = held(qkv_held, "right", ("qkv", [P, 3, TT, AW], F32), ("rqk", [P, 2, TT, NH], F32))
        project(nc, w_in, h_hi, h_lo, qkv, rqk, u_dram, gates_dram, y_dram)
        heads.close()
        attn_hi, attn_lo, pool_hi, pool_lo = held(
            branches, "left", *((n, [P, AW // P, S], F32R) for n in ("attn_hi", "attn_lo", "pool_hi", "pool_lo")))
        attend(nc, consts, q_norm_g, k_norm_g, w_pool_mix, pool_scale, u_dram, qkv, rqk,
               attn_hi, attn_lo, pool_hi, pool_lo)
        qkv_held.close()
        mt_hi, mt_lo = held(merged, "right", ("mt_hi", [P, KC, S], F32R), ("mt_lo", [P, KC, S], F32R))
        merge(nc, consts, gates_dram, w_attn_out, w_pool_out, attn_hi, attn_lo, pool_hi, pool_lo, mt_hi, mt_lo)
        branches.close()
        logits_t, idx, slot_of, gates, over = held(
            small, "left", ("logits_t", [P, S], F32), ("idx", [P, NB], I32), ("slot_of", [P, 2, TT], U32),
            ("gates", [P, 2, TT], F32), ("over", [P, 1 + MOST], I32))
        output_and_norm(nc, consts, x, w_o, norm2_g, w_rg, w_re, mt_hi, mt_lo, logits_t, x1_dram, h2_dram)
        merged.close()
        route_and_experts(nc, consts, b_rg, b_re, w_gate, w_up, w_down, logits_t, idx, slot_of, gates, over,
                          h2_dram, y_dram, idx_dram)
        clear_released_semaphores(nc)
        blocks_beyond(nc, consts, w_gate, w_up, w_down, idx, over, h2_dram, y_dram)
        combine(nc, slot_of, gates, x1_dram, y_dram, out)


_INS = ["x", "norm1_g", "w_in", "q_norm_g", "k_norm_g", "w_attn_out", "w_pool_mix", "pool_scale", "w_pool_out", "w_o",
        "norm2_g", "w_router_group", "b_router_group", "w_router_expert", "b_router_expert", "w_exp_gate",
        "w_exp_up", "w_exp_down"]
_OUTS = [((1, S, D), "float32")]


def kernel(**inputs):
    import numpy as _np
    import concourse.bacc as _bacc
    from concourse import mybir as _mybir
    from concourse.bass_utils import run_bass_kernel_spmd as _run

    nc = _bacc.Bacc("TRN2", target_bir_lowering=False, num_devices=1)
    arrays, args = {}, []
    for name, a in [(n, _np.ascontiguousarray(inputs[n])) for n in _INS] + [("shape_constants", shape_constants())]:
        arrays[f"in_{name}_dram"] = a
        args.append(nc.dram_tensor(f"in_{name}_dram", a.shape, _mybir.dt.from_np(a.dtype), kind="ExternalInput").ap())
    for i, (shape, dtype) in enumerate(_OUTS):
        dt = _mybir.dt.from_np(_np.dtype(dtype))
        args.append(nc.dram_tensor(f"out_{i}_dram", shape, dt, kind="ExternalOutput").ap())
    decoder_layer(nc, *args)
    r = _run(nc, [arrays], core_ids=[0])
    return r.results[0]["out_0_dram"]
```

```python
from contextlib import ExitStack

import numpy as np

import concourse.bass as bass
from concourse import mybir

P = 128
ALU = mybir.AluOpType
ACT = mybir.ActivationFunctionType
AX_X = mybir.AxisListType.X
F32 = mybir.dt.float32
F32R = mybir.dt.float32r
I32 = mybir.dt.int32
U32 = mybir.dt.uint32

D = 1024
S = 1024
KC = D // P
TT = S // P
HD = 64
NH = 8
AW = NH * HD
PG = 4
WIN = (2, 4, 8, 16)
NW = 512
DILATED = ((128, 1), (512, 4), (2048, 16))
NG, NE = 4, 8
E = NG * NE
FH = 512
FC = FH // P
NR = NG + E
EPS = 1e-6
MASKED = -1e30
MOST = 16
NB = E + MOST
PAD = max(WIN)

C_ID, C_TRI, C_ONE = 0, P, 2 * P
C_CNT = 3 * P
C_D4 = C_CNT + PG * PAD
C_D8 = C_D4 + NG
C_EID = C_D8 + NE
C_TH = C_EID + E
C_TOK = C_TH + MOST
C_LOG = C_TOK + TT
C_IOTA = C_LOG + S
C_ALL = C_IOTA + P


def shape_constants():
    c = np.zeros((P, C_ALL), np.float32)
    r = np.arange(P)
    c[:, C_ID:C_ID + P] = np.eye(P)
    c[:, C_TRI:C_TRI + P] = r[:, None] < r[None, :]
    c[:, C_ONE:C_ONE + P] = 1
    for g, w in enumerate(WIN):
        c[:, C_CNT + g * PAD:C_CNT + (g + 1) * PAD] = w / np.minimum(np.arange(PAD) + 1, w)
    c[:, C_D4:C_D4 + NG] = NG - np.arange(NG)
    c[:, C_D8:C_D8 + NE] = NE - np.arange(NE)
    c[:, C_EID:C_EID + E] = np.arange(E)
    c[:, C_TH:C_TH + MOST] = np.arange(MOST)
    c[:, C_TOK:C_TOK + TT] = np.arange(TT)[None, :] * P + r[:, None]
    dist = r[:, None] + (S - P) - np.arange(S)[None, :]
    held = sum(((dist >= 0) & (dist <= w) & (dist % d == 0)).astype(np.int64) for w, d in DILATED)
    c[:, C_IOTA:C_ALL] = np.arange(P)
    c[:, C_LOG:C_LOG + S] = np.where(held > 0, np.log(np.maximum(held, 1)), MASKED)
    return c


def wait(eng, sem, value):
    if not isinstance(value, int) or value > 0:
        eng.wait_ge(sem, value)


def held_value(eng, value):
    return value if isinstance(value, int) else eng.to_reg(value)


class Chain:

    def __init__(self, eng, sem, base=0):
        self.eng, self.sem, self.n = eng, sem, base

    def __call__(self, ins):
        self.n = self.n + 1
        ins.then_inc(self.sem, 1)
        self.eng.wait_ge(self.sem, self.n)


def three_passes(nc, out, a_hi, a_lo, b_hi, b_lo, first, last):
    nc.tensor.matmul(out, a_hi, b_hi, start=first, stop=False)
    nc.tensor.matmul(out, a_lo, b_hi, start=False, stop=False)
    return nc.tensor.matmul(out, a_hi, b_lo, start=False, stop=last)


class Scope:

    def __init__(self, nc, ctx, stage):
        self.nc, self.ctx, self.stage = nc, ctx, stage

    def sb(self, name, shape, dt=F32):
        return self.ctx.enter_context(self.nc.sbuf_tensor(f"{self.stage}_{name}", shape, dt))

    def ps(self, name, shape, dt=F32):
        return self.ctx.enter_context(self.nc.psum_tensor(f"{self.stage}_{name}_ps", shape, dt))

    def sem(self, name):
        return self.ctx.enter_context(self.nc.semaphore(f"{self.stage}_{name}"))

    def sems(self, name, n):
        return [self.sem(f"{name}{i}") for i in range(n)]


def norm_and_transpose(nc, x, norm1_g, consts, h_hi, h_lo):
    with ExitStack() as ctx:
        m = Scope(nc, ctx, "norm")
        xs = m.sb("x", [P, TT, D])
        g = m.sb("g", [P, D])
        ident = m.sb("ident", [P, P])
        squares = m.sb("squares", [P, D])
        ssq = m.sb("ssq", [P, TT])
        var = m.sb("var", [P, TT])
        dev = m.sb("dev", [P, TT])
        rstd = m.sb("rstd", [P, TT])
        h = m.sb("h", [P, 2, D])
        turned = [m.ps(f"turned{b}", [P, KC, P]) for b in range(2)]
        x_loaded = m.sems("x_loaded", TT)
        g_loaded, id_loaded = m.sem("g_loaded"), m.sem("id_loaded")
        summed, var_done, dev_done = m.sem("summed"), m.sem("var_done"), m.sem("dev_done")
        rstd_done, scaled = m.sem("rstd_done"), m.sem("scaled")
        transposed, hi_done, lo_done = m.sem("transposed"), m.sem("hi_done"), m.sem("lo_done")
        half = TT // 2
        block = ctx.enter_context(nc.Block())

        @block.sync
        def _(sp):
            for t in range(TT):
                sp.dma_start(xs[:, t, :], x[0, t * P:(t + 1) * P, :]).then_inc(x_loaded[t], 16)
                if t == 0:
                    sp.dma_start(ident[:], consts[:, C_ID:C_ID + P]).then_inc(id_loaded, 16)
                    sp.dma_start(g[:], norm1_g[0:1, :].to_broadcast([P, D])).then_inc(g_loaded, 16)

        @block.scalar
        def _(act):
            def sums(b):
                for t in range(b * half, (b + 1) * half):
                    act.wait_ge(x_loaded[t], 16)
                    wait(act, summed, t)
                    nc.scalar.activation(squares[:], xs[:, t, :], ACT.Square,
                                         accum_out=ssq[:, t:t + 1]).then_inc(summed, 1)

            def root(b):
                act.wait_ge(var_done, b + 1)
                nc.scalar.activation(dev[:, b * half:(b + 1) * half], var[:, b * half:(b + 1) * half],
                                     ACT.Sqrt).then_inc(dev_done, 1)

            def upper(t):
                act.wait_ge(transposed, t + 1)
                nc.scalar.copy(h_hi[:, :, t * P:(t + 1) * P], turned[t % 2][:]).then_inc(hi_done, 1)

            sums(0)
            root(0)
            sums(1)
            root(1)
            for t in range(TT):
                upper(t)

        @block.vector
        def _(dve):
            def scale(b):
                r = slice(b * half, (b + 1) * half)
                dve.wait_ge(summed, (b + 1) * half)
                nc.vector.tensor_scalar(var[:, r], ssq[:, r], 1.0 / D, EPS, ALU.mult, ALU.add).then_inc(var_done, 1)
                dve.wait_ge(dev_done, b + 1)
                nc.vector.reciprocal(rstd[:, r], dev[:, r]).then_inc(rstd_done, 1)
                dve.wait_ge(rstd_done, b + 1)

            def apply(t):
                wait(dve, transposed, t - 1)
                nc.vector.scalar_tensor_tensor(out=h[:, t % 2, :], in0=xs[:, t, :], scalar=rstd[:, t:t + 1],
                                               in1=g[:], op0=ALU.mult, op1=ALU.mult).then_inc(scaled, 1)

            def lower(t):
                dve.wait_ge(hi_done, t + 1)
                nc.vector.tensor_tensor(h_lo[:, :, t * P:(t + 1) * P], turned[t % 2][:],
                                        h_hi[:, :, t * P:(t + 1) * P].bitcast(F32),
                                        ALU.subtract).then_inc(lo_done, 1)

            scale(0)
            dve.wait_ge(g_loaded, 16)
            for t in range(TT):
                apply(t)
                if t == 1:
                    scale(1)
                if t >= 1:
                    lower(t - 1)
            lower(TT - 1)

        @block.tensor
        def _(pe):
            pe.wait_ge(id_loaded, 16)
            for t in range(TT):
                pe.wait_ge(scaled, t + 1)
                wait(pe, lo_done, t - 1)
                for k in range(KC):
                    last = nc.tensor.transpose(turned[t % 2][:, k, :], h[:, t % 2, k * P:(k + 1) * P], ident[:])
                last.then_inc(transposed, 1)


def project(nc, w_in, h_hi, h_lo, qkv, rqk, u_dram, gates_dram):
    with ExitStack() as ctx:
        m = Scope(nc, ctx, "proj")
        CH = 8
        QT, SL = 4, KC // 4
        raw = m.sb("raw", [P, 2, SL, NW])
        w_hi = m.sb("w_hi", [P, 2, KC, NW], F32R)
        w_lo = m.sb("w_lo", [P, 2, KC, NW], F32R)
        staged = m.sb("staged", [P, 2, NW])
        sq = m.sb("sq", [P, 4 * AW])
        ssq = m.sb("ssq", [P, 2 * TT * NH])
        var = m.sb("var", [P, 2 * TT * NH])
        dev = m.sb("dev", [P, 2 * TT * NH])
        acc = [m.ps(f"acc{b}", [P, NW]) for b in range(4)]
        raw_loaded = m.sems("raw_loaded", 2)
        hi_done, lo_done = m.sem("hi_done"), m.sem("lo_done")
        projected, evacuated = m.sem("projected"), m.sem("evacuated")
        stored = m.sems("stored", 2)
        var_done, dev_done, chain = m.sem("var_done"), m.sem("dev_done"), m.sem("chain")
        w_rows = w_in[0].rearrange("(k p) n -> p k n", p=P)
        block = ctx.enter_context(nc.Block())

        @block.sync
        def _(sp):
            def load(c, col):
                for q in range(QT):
                    wait(sp, lo_done, c * QT + q - 1)
                    sp.dma_start(raw[:, q % 2], w_rows[:, q * SL:(q + 1) * SL, bass.ds(col, NW)]
                                 ).then_inc(raw_loaded[q % 2], 16)

            load(0, 3 * AW)
            with sp.Fori(1, 4) as c:
                load(c, c * NW - NW)
            with sp.Fori(4, CH) as c:
                load(c, c * NW)

        @block.scalar
        def _(act):
            def upper(c, q):
                act.wait_ge(raw_loaded[q % 2], c * 32 + 16 * (q // 2 + 1))
                if not isinstance(c, int) or c >= 2:
                    act.wait_ge(projected, c * 8 - 8)
                nc.scalar.copy(w_hi[:, c % 2, q * SL:(q + 1) * SL, :], raw[:, q % 2]).then_inc(hi_done, 1)

            def to_dram(c, t, dst, func, n):
                act.wait_ge(projected, c * 8 + t + 1)
                wait(act, stored[t % 2], n * 16)
                nc.scalar.activation(staged[:, t % 2, :], acc[t % 4][:], func).then_inc(evacuated, 1)
                act.wait_ge(evacuated, c * 8 + t + 1)
                act.dma_start(dst, staged[:, t % 2, :]).then_inc(stored[t % 2], 16)

            def split_next(c, t):
                if t % 2:
                    upper(c + 1, t // 2)

            def gate_chunk(c, more):
                for t in range(TT):
                    to_dram(c, t, gates_dram[t * P:(t + 1) * P, bass.ds(c * NW - 4 * NW, NW)],
                            ACT.Sigmoid, c * 4 - 12 + t // 2)
                    if more:
                        split_next(c, t)

            for q in range(QT):
                upper(0, q)
            for t in range(TT):
                g, half = divmod(t, 2)
                to_dram(0, t, u_dram[g, :, half * NW:(half + 1) * NW], ACT.Copy, t // 2)
                if t % 2:
                    upper(1, t // 2)
            with act.Fori(1, 4) as c:
                for t in range(TT):
                    act.wait_ge(projected, c * 8 + t + 1)
                    nc.scalar.copy(qkv[:, c - 1, t, :], acc[t % 4][:]).then_inc(evacuated, 1)
                    split_next(c, t)
            with act.Fori(4, CH - 1) as c:
                gate_chunk(c, True)
            gate_chunk(CH - 1, False)
            act.wait_ge(var_done, 1)
            nc.scalar.activation(dev[:], var[:], ACT.Sqrt).then_inc(dev_done, 1)
            for b in range(2):
                act.wait_ge(stored[b], 16 * (4 + 16))

        @block.vector
        def _(dve):
            link = Chain(dve, chain)

            def lower(c, q):
                dve.wait_ge(hi_done, c * QT + q + 1)
                nc.vector.tensor_tensor(w_lo[:, c % 2, q * SL:(q + 1) * SL, :], raw[:, q % 2],
                                        w_hi[:, c % 2, q * SL:(q + 1) * SL, :].bitcast(F32),
                                        ALU.subtract).then_inc(lo_done, 1)

            for q in range(QT):
                lower(0, q)
            with dve.Fori(1, 5) as c:
                for q in range(QT):
                    lower(c, q)
            dve.wait_ge(evacuated, 8 * 3)
            for s in range(2):
                for b in range(2):
                    half = qkv[:, s, b * 4:(b + 1) * 4, :].rearrange("p t n -> p (t n)")
                    link(nc.vector.tensor_tensor(sq[:], half, half, ALU.mult))
                    at = (s * 2 + b) * 4 * NH
                    link(nc.vector.tensor_reduce(ssq[:, at:at + 4 * NH], sq[:].rearrange("p (a e) -> p a e", e=HD),
                                                 AX_X, ALU.add))
            nc.vector.tensor_scalar(var[:], ssq[:], 1.0 / HD, EPS, ALU.mult, ALU.add).then_inc(var_done, 1)
            with dve.Fori(5, CH) as c:
                for q in range(QT):
                    lower(c, q)
            dve.wait_ge(dev_done, 1)
            link(nc.vector.reciprocal(rqk[:].rearrange("p a b c -> p (a b c)"), dev[:]))

        @block.tensor
        def _(pe):
            def columns_first():
                for t in range(8):
                    g, half = divmod(t, 2)
                    wait(pe, evacuated, t - 3)
                    for k in range(KC):
                        if t == 0 and k % SL == 0:
                            pe.wait_ge(lo_done, k // SL + 1)
                        cols, toks = slice(g * P, (g + 1) * P), slice(half * NW, (half + 1) * NW)
                        last = three_passes(nc, acc[t % 4][:], w_hi[:, 0, k, cols], w_lo[:, 0, k, cols],
                                            h_hi[:, k, toks], h_lo[:, k, toks], k == 0, k == KC - 1)
                    last.then_inc(projected, 1)

            def tokens_first(c):
                for t in range(TT):
                    pe.wait_ge(evacuated, c * 8 + t - 3)
                    toks = slice(t * P, (t + 1) * P)
                    for k in range(KC):
                        if t == 0 and k % SL == 0:
                            pe.wait_ge(lo_done, c * QT + k // SL + 1)
                        last = three_passes(nc, acc[t % 4][:], h_hi[:, k, toks], h_lo[:, k, toks],
                                            w_hi[:, c % 2, k, :], w_lo[:, c % 2, k, :], k == 0, k == KC - 1)
                    last.then_inc(projected, 1)

            columns_first()
            with pe.Fori(1, CH) as c:
                tokens_first(c)


def attend(nc, consts, q_norm_g, k_norm_g, u_dram, qkv, rqk, attn_hi, attn_lo, pooled):
    with ExitStack() as ctx:
        m = Scope(nc, ctx, "attn")
        PAIRS, IT = NH // 2, 2 * TT
        TURNS = {IT: [(0, 0)], IT + 1: [(0, 1), (1, 0)], IT + 2: [(1, 1)]}
        ident = m.sb("ident", [P, P])
        log_held = m.sb("log_held", [P, S])
        ratio = m.sb("ratio", [P, PG, PAD])
        norm_g = m.sb("norm_g", [P, 2])
        scale_g = m.sb("scale_g", [P, 2])
        qk_st = m.sb("qk_st", [P, 2, TT, 2, 2, HD])
        v_st = m.sb("v_st", [P, TT, P])
        q_split = m.sb("q_split", [P, 2, S], F32R)
        k_hi = m.sb("k_hi", [P, 2, S], F32R)
        k_lo = m.sb("k_lo", [P, 2, S], F32R)
        masked = m.sb("masked", [P, 2, S])
        negmax = m.sb("negmax", [P, 2])
        prob = m.sb("prob", [P, 2, S])
        den = m.sb("den", [P, 2, 2])
        rden = m.sb("rden", [P, 2, 2])
        heads_out = m.sb("heads_out", [P, 2, P])
        prob_t = m.sb("prob_t", [P, 2, TT, P])
        u = m.sb("u", [P, PG, PAD + S])
        run = m.sb("run", [P, 2, PAD + S])
        score = [m.ps(f"score{b}", [P, S]) for b in range(2)]
        turned = m.ps("turned", [P, TT, P])
        out = [m.ps(f"out{b}", [P, 2, NW // 2]) for b in range(2)]
        c_loaded, g_loaded, u_loaded = m.sem("c_loaded"), m.sem("g_loaded"), m.sem("u_loaded")
        g_scaled, qk_staged, v_staged = m.sem("g_scaled"), m.sem("qk_staged"), m.sem("v_staged")
        qk_turned, qk_hi_done, qk_lo_done = m.sem("qk_turned"), m.sem("qk_hi_done"), m.sem("qk_lo_done")
        scored, maxed, exped = m.sem("scored"), m.sem("maxed"), m.sem("exped")
        p_turned, p_copied = m.sem("p_turned"), m.sem("p_copied")
        rden_done, normed, out_turned = m.sem("rden_done"), m.sem("normed"), m.sem("out_turned")
        summed, hi_done, lo_done = m.sem("summed"), m.sem("hi_done"), m.sem("lo_done")
        padded, pool_chain, windows_done = m.sem("padded"), m.sem("pool_chain"), m.sem("windows_done")
        averaged = m.sem("averaged")
        block = ctx.enter_context(nc.Block())

        @block.sync
        def _(sp):
            sp.dma_start(ident[:], consts[:, C_ID:C_ID + P]).then_inc(c_loaded, 16)
            sp.dma_start(log_held[:], consts[:, C_LOG:C_LOG + S]).then_inc(c_loaded, 16)
            sp.dma_start(ratio[:].rearrange("p g w -> p (g w)"), consts[:, C_CNT:C_CNT + PG * PAD]
                         ).then_inc(c_loaded, 16)
            for i, g in enumerate((q_norm_g, k_norm_g)):
                for a in range(2):
                    sp.dma_start(norm_g[a * HD:(a + 1) * HD, i:i + 1], g[0].unsqueeze(1)).then_inc(g_loaded, 16)
            sp.wait_ge(padded, 1)
            sp.dma_start(u[:, :, PAD:], u_dram.rearrange("g p s -> p g s")).then_inc(u_loaded, 16)

        @block.gpsimd
        def _(pool):
            link = Chain(pool, pool_chain)
            nc.gpsimd.memset(u[:], 0.0).then_inc(padded, 1)
            link(nc.gpsimd.memset(run[:], 0.0))

            def stage_v(hp):
                wait(pool, summed, hp * IT)
                nc.gpsimd.tensor_copy(v_st[:], qkv[:, 2, :, bass.ds(hp * P, P)]).then_inc(v_staged, 1)

            stage_v(0)
            pool.wait_ge(u_loaded, 16)
            for g, w in enumerate(WIN):
                src = u[:, g]
                for step in range(g + 1):
                    s = 1 << step
                    dst = pooled[:, g] if step == g else run[:, step % 2, PAD:]
                    link(nc.gpsimd.tensor_tensor(dst, src[:, PAD:], src[:, PAD - s:PAD + S - s], ALU.add))
                    src = run[:, step % 2]
                ins = nc.gpsimd.tensor_tensor(pooled[:, g, 0:PAD], pooled[:, g, 0:PAD], ratio[:, g], ALU.mult)
                ins.then_inc(windows_done, 1)
            with pool.Fori(1, PAIRS) as hp:
                stage_v(hp)

        @block.vector
        def _(dve):
            dve.wait_ge(g_loaded, 64)
            nc.vector.tensor_scalar(scale_g[:, 0:1], norm_g[:, 0:1], HD ** -0.5, None, ALU.mult).then_inc(g_scaled, 1)
            nc.vector.tensor_copy(scale_g[:, 1:2], norm_g[:, 1:2]).then_inc(g_scaled, 1)

            def stage_qk(hp):
                wait(dve, qk_turned, hp * 4)
                for s in range(2):
                    for twice in range(2):
                        nc.vector.tensor_tensor(
                            qk_st[:, s, :, :, twice],
                            qkv[:, s, :, bass.ds(hp * P, P)].rearrange("p t (a e) -> p t a e", a=2),
                            rqk[:, s, :, bass.ds(hp * 2, 2)].unsqueeze(3).to_broadcast([P, TT, 2, HD]),
                            ALU.mult).then_inc(qk_staged, 1)

            def qk_lower(hp, a, s):
                dve.wait_ge(qk_hi_done, hp * 4 + a * 2 + s + 1)
                low = slice(HD, P) if s == 0 else slice(0, P)
                hi, lo = (q_split, q_split) if s == 0 else (k_hi, k_lo)
                nc.vector.scalar_tensor_tensor(
                    out=lo[low, a, :], in0=score[s][low, :], scalar=scale_g[low, s:s + 1],
                    in1=hi[low, a, :].bitcast(F32), op0=ALU.mult, op1=ALU.subtract).then_inc(qk_lo_done, 1)

            def mask_and_max(hp, i):
                b, n = i % 2, (i // 2 + 1) * P
                scores_due, exps_due = held_value(dve, hp * IT + i + 1), held_value(dve, hp * IT + max(i - 1, 0))
                dve.wait_ge(c_loaded, 48)
                dve.wait_ge(scored, scores_due)
                wait(dve, exped, exps_due)
                nc.vector.tensor_tensor_reduce(
                    out=masked[:, b, 0:n], in0=score[b][:, 0:n], in1=log_held[:, S - n:S], scale=-1.0,
                    scalar=3e38, op0=ALU.add, op1=ALU.min, accum_out=negmax[:, b:b + 1]).then_inc(maxed, 1)

            def invert(hp, t):
                dve.wait_ge(exped, hp * IT + 2 * t + 2)
                wait(dve, normed, hp * TT + max(t - 1, 0))
                nc.vector.reciprocal(rden[:, t % 2], den[:, t % 2]).then_inc(rden_done, 1)

            def normalise(hp, t):
                dve.wait_ge(rden_done, hp * TT + t + 1)
                dve.wait_ge(summed, hp * IT + 2 * t + 2)
                wait(dve, out_turned, hp * TT + max(t - 1, 0))
                nc.vector.tensor_tensor(
                    heads_out[:, t % 2, :].rearrange("p (a e) -> p a e", a=2),
                    out[t % 2][:, 0, 0:P].rearrange("p (a e) -> p a e", a=2),
                    rden[:, t % 2].unsqueeze(2).to_broadcast([P, 2, HD]), ALU.mult).then_inc(normed, 1)

            def lower(hp, t):
                dve.wait_ge(hi_done, hp * TT + t + 1)
                at = (slice(None), hp, slice(t * P, (t + 1) * P))
                nc.vector.tensor_tensor(attn_lo[at], out[t % 2][:, 1, 0:P], attn_hi[at].bitcast(F32),
                                        ALU.subtract).then_inc(lo_done, 1)

            def pair(hp, more):
                for i in range(IT + 3):
                    if i < IT:
                        mask_and_max(hp, i)
                    if i % 2 == 0 and 2 <= i <= IT:
                        invert(hp, i // 2 - 1)
                    if i % 2 == 0 and i >= 6:
                        lower(hp, i // 2 - 3)
                    if i % 2 == 0 and i >= 4:
                        normalise(hp, i // 2 - 2)
                    if i == 8 and more:
                        stage_qk(hp + 1)
                    if more:
                        for a, s in TURNS.get(i, []):
                            qk_lower(hp + 1, a, s)
                lower(hp, TT - 1)

            stage_qk(0)
            dve.wait_ge(c_loaded, 48)
            for a in range(2):
                for s in range(2):
                    qk_lower(0, a, s)
            pair(0, True)
            with dve.Fori(1, PAIRS - 1) as hp:
                pair(hp, True)
            for g, w in enumerate(WIN):
                dve.wait_ge(windows_done, g + 1)
                nc.vector.scalar_tensor_tensor(out=pooled[:, g], in0=pooled[:, g], scalar=1.0 / w, in1=u[:, g, PAD:],
                                               op0=ALU.mult, op1=ALU.subtract).then_inc(averaged, 1)
            pair(PAIRS - 1, False)

        @block.scalar
        def _(act):
            def qk_upper(hp, a, s):
                act.wait_ge(qk_turned, hp * 4 + a * 2 + s + 1)
                nc.scalar.activation((q_split, k_hi)[s][:, a, :], score[s][:], ACT.Copy,
                                     scale=scale_g[:, s:s + 1]).then_inc(qk_hi_done, 1)

            def exponent(hp, i):
                b, n = i % 2, (i // 2 + 1) * P
                act.wait_ge(maxed, hp * IT + i + 1)
                wait(act, p_turned, hp * IT + max(i - 1, 0))
                nc.scalar.activation(prob[:, b, 0:n], masked[:, b, 0:n], ACT.Exp, bias=negmax[:, b:b + 1], scale=-1.0,
                                     accum_out=den[:, i // 2 % 2, b:b + 1]).then_inc(exped, 1)

            def copy_prob(hp, i):
                b, j = i % 2, i // 2 + 1
                act.wait_ge(p_turned, hp * IT + i + 1)
                wait(act, summed, hp * IT + max(i - 1, 0))
                nc.scalar.copy(prob_t[:, b, 0:j, :], turned[:, 0:j, :]).then_inc(p_copied, 1)

            def upper(hp, t):
                act.wait_ge(out_turned, hp * TT + t + 1)
                nc.scalar.copy(attn_hi[:, hp, t * P:(t + 1) * P], out[t % 2][:, 1, 0:P]).then_inc(hi_done, 1)

            def pair(hp, more):
                for i in range(IT + 3):
                    if i < IT:
                        exponent(hp, i)
                    if i % 2 and i >= 5:
                        upper(hp, (i - 5) // 2)
                    if 1 <= i <= IT:
                        copy_prob(hp, i - 1)
                    if more:
                        for a, s in TURNS.get(i, []):
                            qk_upper(hp + 1, a, s)
                upper(hp, TT - 1)

            act.wait_ge(g_scaled, 2)
            for a in range(2):
                for s in range(2):
                    qk_upper(0, a, s)
            pair(0, True)
            with act.Fori(1, PAIRS - 1) as hp:
                pair(hp, True)
            pair(PAIRS - 1, False)

        @block.tensor
        def _(pe):
            def turn_qk(hp, a, s):
                pe.wait_ge(qk_staged, hp * 4 + s * 2 + 2)
                if a:
                    pe.wait_ge(qk_lo_done, hp * 4 + s + 1)
                else:
                    wait(pe, maxed, hp * IT - 1 + s if not isinstance(hp, int) or hp else 0)
                for t in range(TT):
                    last = nc.tensor.transpose(score[s][:, t * P:(t + 1) * P],
                                               qk_st[:, s, t, a].rearrange("p two e -> p (two e)"), ident[:])
                last.then_inc(qk_turned, 1)

            def scores(hp, i):
                t, a = divmod(i, 2)
                n = (t + 1) * P
                if i < 2:
                    pe.wait_ge(qk_lo_done, hp * 4 + i + 3)
                else:
                    pe.wait_ge(maxed, hp * IT + i - 1)
                for c in range(0, n, NW):
                    w = min(NW, n - c)
                    for k, first in ((k_hi, True), (k_lo, False)):
                        last = nc.tensor.matmul(score[i % 2][:, c:c + w], q_split[:, a, t * P:(t + 1) * P],
                                                k[:, a, c:c + w], start=first, stop=not first)
                last.then_inc(scored, 1)

            def turn_prob(hp, i):
                pe.wait_ge(exped, hp * IT + i + 1)
                wait(pe, p_copied, hp * IT + i)
                for j in range(i // 2 + 1):
                    last = nc.tensor.transpose(turned[:, j, :], prob[:, i % 2, j * P:(j + 1) * P], ident[:])
                last.then_inc(p_turned, 1)

            def weigh(hp, i):
                t, a = divmod(i, 2)
                h = slice(a * HD, (a + 1) * HD)
                pe.wait_ge(p_copied, hp * IT + i + 1)
                if a == 0:
                    wait(pe, lo_done, hp * TT + max(t - 1, 0))
                if i == 0:
                    pe.wait_ge(v_staged, hp + 1)
                for j in range(t + 1):
                    last = nc.tensor.matmul(out[t % 2][:, 0, h], prob_t[:, i % 2, j, :], v_st[:, j, h],
                                            start=(j == 0), stop=(j == t))
                last.then_inc(summed, 1)

            def turn_out(hp, t):
                pe.wait_ge(normed, hp * TT + t + 1)
                nc.tensor.transpose(out[t % 2][:, 1, 0:P], heads_out[:, t % 2, :], ident[:]).then_inc(out_turned, 1)

            def pair(hp, more):
                for i in range(IT + 3):
                    if i < IT:
                        scores(hp, i)
                    if 2 <= i < IT + 2:
                        turn_prob(hp, i - 2)
                    if i % 2 and i >= 5:
                        turn_out(hp, (i - 5) // 2)
                    if i >= 3:
                        weigh(hp, i - 3)
                    if more:
                        for a, s in TURNS.get(i, []):
                            turn_qk(hp + 1, a, s)
                turn_out(hp, TT - 1)

            pe.wait_ge(c_loaded, 48)
            for a in range(2):
                for s in range(2):
                    turn_qk(0, a, s)
            pair(0, True)
            with pe.Fori(1, PAIRS - 1) as hp:
                pair(hp, True)
            pair(PAIRS - 1, False)


def merge(nc, consts, gates_dram, w_attn_out, w_pool_mix, pool_scale, w_pool_out, attn_hi, attn_lo, pooled,
          pool_hi, pool_lo, mt_hi, mt_lo):
    with ExitStack() as ctx:
        m = Scope(nc, ctx, "merge")
        QT, SL, BK = 4, 2, AW // P
        ident = m.sb("ident", [P, P])
        raw = m.sb("raw", [P, 2, SL, NW])
        w_hi = m.sb("w_hi", [P, 2 * BK, NW], F32R)
        w_lo = m.sb("w_lo", [P, 2 * BK, NW], F32R)
        gate = m.sb("gate", [P, 2, 2, NW])
        part = m.sb("part", [P, 2, NW])
        merged = m.sb("merged", [P, 2, NW])
        acc = [[m.ps(f"acc{b}{s}", [P, NW]) for s in range(2)] for b in range(2)]
        turned = [m.ps(f"turned{b}", [P, NW // P, P]) for b in range(2)]
        mix = m.sb("mix", [P, PG, P])
        pscale = m.sb("pscale", [P, PG])
        mixed_ps = [m.ps(f"mixed{b}", [P, NW]) for b in range(2)]
        mix_loaded, mixed, mix_hi, mix_lo = m.sem("mix_loaded"), m.sem("mixed"), m.sem("mix_hi"), m.sem("mix_lo")
        id_loaded = m.sem("id_loaded")
        raw_loaded, gate_loaded = m.sems("raw_loaded", 2), m.sems("gate_loaded", 2)
        w_hi_done, w_lo_done = m.sem("w_hi_done"), m.sem("w_lo_done")
        attn_done, pool_done, gated, added = m.sem("attn_done"), m.sem("pool_done"), m.sem("gated"), m.sem("added")
        transposed, hi_done, lo_done = m.sem("transposed"), m.sem("hi_done"), m.sem("lo_done")
        rows = [w[0].rearrange("(k p) n -> p k n", p=P) for w in (w_attn_out, w_pool_out)]
        block = ctx.enter_context(nc.Block())

        @block.sync
        def _(sp):
            sp.dma_start(mix[:], w_pool_mix[0].rearrange("g c d -> c g d")).then_inc(mix_loaded, 16)

            def weights(c, quarters):
                for q in quarters:
                    wait(sp, w_lo_done, c * QT + q - 1)
                    sp.dma_start(raw[:, q % 2], rows[q // 2][:, (q % 2) * SL:(q % 2 + 1) * SL, c * NW:(c + 1) * NW]
                                 ).then_inc(raw_loaded[q % 2], 16)

            def gates(n):
                c, t = divmod(n, TT)
                wait(sp, added, n - 1)
                for s in range(2):
                    col = s * D + c * NW
                    sp.dma_start(gate[:, n % 2, s, :], gates_dram[t * P:(t + 1) * P, col:col + NW]
                                 ).then_inc(gate_loaded[n % 2], 16)

            weights(0, range(2))
            for g in range(PG):
                sp.dma_start(pscale[:, g:g + 1], pool_scale[0, g * P:(g + 1) * P].unsqueeze(1)).then_inc(mix_loaded, 16)
            sp.dma_start(ident[:], consts[:, C_ID:C_ID + P]).then_inc(id_loaded, 16)
            weights(0, range(2, QT))
            for n in range(2 * TT):
                gates(n)
                if n == 3:
                    weights(1, range(QT // 2))
                if n == TT:
                    weights(1, range(QT // 2, QT))

        @block.scalar
        def _(act):
            def w_upper(c, q):
                act.wait_ge(raw_loaded[q % 2], 16 * (c * 2 + q // 2 + 1))
                if c:
                    act.wait_ge((attn_done, pool_done)[q // 2], TT)
                nc.scalar.copy(w_hi[:, q * SL:(q + 1) * SL, :], raw[:, q % 2]).then_inc(w_hi_done, 1)

            def mix_upper(n):
                g, half = divmod(n, 2)
                act.wait_ge(mixed, n + 1)
                nc.scalar.activation(pool_hi[:, g, half * NW:(half + 1) * NW], mixed_ps[half][:], ACT.Copy,
                                     scale=pscale[:, g:g + 1]).then_inc(mix_hi, 1)

            def upper(n):
                c, t = divmod(n, TT)
                act.wait_ge(transposed, n + 1)
                nc.scalar.copy(mt_hi[:, c * BK:(c + 1) * BK, t * P:(t + 1) * P], turned[n % 2][:]).then_inc(hi_done, 1)

            for c in range(2):
                for q in range(QT):
                    w_upper(c, q)
                    if c == 0 and q % 2:
                        if q == 1:
                            act.wait_ge(mix_loaded, 16 * (1 + PG))
                        for n in range((q // 2) * PG, (q // 2 + 1) * PG):
                            mix_upper(n)
                for t in range(TT):
                    if c * TT + t >= 1:
                        upper(c * TT + t - 1)
            upper(2 * TT - 1)

        @block.vector
        def _(dve):
            def w_lower(c, q):
                dve.wait_ge(w_hi_done, c * QT + q + 1)
                nc.vector.tensor_tensor(w_lo[:, q * SL:(q + 1) * SL, :], raw[:, q % 2],
                                        w_hi[:, q * SL:(q + 1) * SL, :].bitcast(F32), ALU.subtract
                                        ).then_inc(w_lo_done, 1)

            def mix_lower(n):
                g, half = divmod(n, 2)
                dst = (slice(None), g, slice(half * NW, (half + 1) * NW))
                dve.wait_ge(mix_hi, n + 1)
                nc.vector.scalar_tensor_tensor(out=pool_lo[dst], in0=mixed_ps[half][:], scalar=pscale[:, g:g + 1],
                                               in1=pool_hi[dst].bitcast(F32), op0=ALU.mult,
                                               op1=ALU.subtract).then_inc(mix_lo, 1)

            def combine(n):
                b = n % 2
                dve.wait_ge(gate_loaded[b], 32 * (n // 2 + 1))
                dve.wait_ge(attn_done, n + 1)
                nc.vector.tensor_tensor(part[:, 0, :], acc[b][0][:], gate[:, b, 0, :], ALU.mult).then_inc(gated, 1)
                dve.wait_ge(pool_done, n + 1)
                nc.vector.tensor_tensor(part[:, 1, :], acc[b][1][:], gate[:, b, 1, :], ALU.mult).then_inc(gated, 1)
                dve.wait_ge(gated, 2 * n + 2)
                wait(dve, transposed, n - 1)
                nc.vector.tensor_tensor(merged[:, b, :], part[:, 0, :], part[:, 1, :], ALU.add).then_inc(added, 1)
                dve.wait_ge(added, n + 1)

            def lower(n):
                c, t = divmod(n, TT)
                dve.wait_ge(hi_done, n + 1)
                at = (slice(None), slice(c * BK, (c + 1) * BK), slice(t * P, (t + 1) * P))
                nc.vector.tensor_tensor(mt_lo[at], turned[n % 2][:], mt_hi[at].bitcast(F32),
                                        ALU.subtract).then_inc(lo_done, 1)

            for c in range(2):
                for q in range(QT):
                    w_lower(c, q)
                    if c == 0 and q % 2:
                        for n in range((q // 2) * PG, (q // 2 + 1) * PG):
                            mix_lower(n)
                for t in range(TT):
                    n = c * TT + t
                    combine(n)
                    if n >= 1:
                        lower(n - 1)
            lower(2 * TT - 1)

        @block.tensor
        def _(pe):
            def branch(n, s, hi, lo, done):
                c, t = divmod(n, TT)
                toks = slice(t * P, (t + 1) * P)
                for k in range(BK):
                    q = (s * BK + k) // SL
                    if t == 0 and k % SL == 0:
                        pe.wait_ge(w_lo_done, c * QT + q + 1)
                    last = three_passes(nc, acc[n % 2][s][:], hi[:, k, toks], lo[:, k, toks],
                                        w_hi[:, s * BK + k, :], w_lo[:, s * BK + k, :], k == 0, k == BK - 1)
                last.then_inc(done, 1)
                return last

            def turn(n):
                pe.wait_ge(added, n + 1)
                wait(pe, lo_done, n - 1)
                for j in range(BK):
                    last = nc.tensor.transpose(turned[n % 2][:, j, :], merged[:, n % 2, j * P:(j + 1) * P], ident[:])
                last.then_inc(transposed, 1)

            pe.wait_ge(mix_loaded, 16 * (1 + PG))
            for n in range(2 * PG):
                g, half = divmod(n, 2)
                wait(pe, mix_lo, n - 1)
                nc.tensor.matmul(mixed_ps[half][:], mix[:, g, :], pooled[:, g, half * NW:(half + 1) * NW],
                                 start=True, stop=True).then_inc(mixed, 1)
            pe.wait_ge(id_loaded, 16)
            for n in range(2 * TT):
                wait(pe, added, n - 1)
                if n == 0:
                    pe.wait_ge(mix_lo, 2 * PG)
                branch(n, 0, attn_hi, attn_lo, attn_done)
                branch(n, 1, pool_hi, pool_lo, pool_done)
                if n >= 1:
                    turn(n - 1)
            turn(2 * TT - 1)


def output_and_norm(nc, consts, x, w_o, norm2_g, w_rg, w_re, mt_hi, mt_lo, logits_t, x1_dram, h2_dram):
    with ExitStack() as ctx:
        m = Scope(nc, ctx, "out")
        QT, SL = 4, KC // 4
        ident = m.sb("ident", [P, P])
        raw = m.sb("raw", [P, 2, SL, NW])
        w_hi = m.sb("w_hi", [P, 2, KC, NW], F32R)
        w_lo = m.sb("w_lo", [P, 2, KC, NW], F32R)
        xin = m.sb("xin", [P, 2, NW])
        x1 = m.sb("x1", [P, TT, D])
        g = m.sb("g", [P, D])
        squares = m.sb("squares", [P, D])
        ssq, var = m.sb("ssq", [P, TT]), m.sb("var", [P, TT])
        dev, rstd = m.sb("dev", [P, TT]), m.sb("rstd", [P, TT])
        h2 = m.sb("h2", [P, 2, D])
        h2t = m.sb("h2t", [P, 2, KC, P])
        router = m.sb("router", [P, KC, NR])
        acc = [m.ps(f"acc{b}", [P, NW]) for b in range(4)]
        turned = m.ps("turned", [P, KC, P])
        logit = m.ps("logit", [NR, NW])
        c_loaded, r_loaded = m.sem("c_loaded"), m.sem("r_loaded")
        raw_loaded, x_loaded = m.sems("raw_loaded", 2), m.sems("x_loaded", 2)
        w_hi_done, w_lo_done = m.sem("w_hi_done"), m.sem("w_lo_done")
        projected, added, squared = m.sem("projected"), m.sem("added"), m.sem("squared")
        var_done, dev_done, rstd_done, normed = m.sem("var_done"), m.sem("dev_done"), m.sem("rstd_done"), m.sem("normed")
        x1_stored, h2_stored = m.sem("x1_stored"), m.sems("h2_stored", 2)
        transposed, t_copied, routed, l_copied = m.sem("transposed"), m.sem("t_copied"), m.sem("routed"), m.sem("l_copied")
        rows = w_o[0].rearrange("(k p) n -> p k n", p=P)
        block = ctx.enter_context(nc.Block())

        @block.sync
        def _(sp):
            def weights(c, quarters):
                for q in quarters:
                    wait(sp, w_lo_done, c * QT + q - 1)
                    sp.dma_start(raw[:, q % 2], rows[:, q * SL:(q + 1) * SL, c * NW:(c + 1) * NW]
                                 ).then_inc(raw_loaded[q % 2], 16)

            def store(t):
                sp.wait_ge(added, TT + t + 1)
                sp.dma_start(x1_dram[t * P:(t + 1) * P, :], x1[:, t, :]).then_inc(x1_stored, 16)
                sp.wait_ge(normed, t + 1)
                sp.dma_start(h2_dram[t * P:(t + 1) * P, :], h2[:, t % 2, :]).then_inc(h2_stored[t % 2], 16)

            weights(0, range(QT))
            for n in range(2 * TT):
                c, t = divmod(n, TT)
                wait(sp, added, n - 1)
                sp.dma_start(xin[:, n % 2, :], x[0, t * P:(t + 1) * P, c * NW:(c + 1) * NW]
                             ).then_inc(x_loaded[n % 2], 16)
                if n == 0:
                    sp.dma_start(ident[:], consts[:, C_ID:C_ID + P]).then_inc(c_loaded, 16)
                    sp.dma_start(g[:], norm2_g[0:1, :].to_broadcast([P, D])).then_inc(c_loaded, 16)
                    sp.dma_start(router[:, :, 0:NG], w_rg[0].rearrange("(p c) e -> p c e", c=KC)).then_inc(r_loaded, 16)
                    for e in range(NG):
                        sp.dma_start(router[:, :, NG + e * NE:NG + (e + 1) * NE],
                                     w_re[0, e].rearrange("(p c) e -> p c e", c=KC)).then_inc(r_loaded, 16)
                if n % 2 and n < TT:
                    weights(1, (n // 2,))
                if c == 1 and t >= 3:
                    store(t - 3)
            for t in range(TT - 3, TT):
                store(t)
            sp.wait_ge(x1_stored, 16 * TT)
            for b in range(2):
                sp.wait_ge(h2_stored[b], 16 * TT // 2)

        @block.scalar
        def _(act):
            def square(t):
                act.wait_ge(added, TT + t + 1)
                wait(act, squared, t)
                nc.scalar.activation(squares[:], x1[:, t, :], ACT.Square, accum_out=ssq[:, t:t + 1]).then_inc(squared, 1)

            def root(t):
                act.wait_ge(var_done, t + 1)
                nc.scalar.activation(dev[:, t:t + 1], var[:, t:t + 1], ACT.Sqrt).then_inc(dev_done, 1)

            def copy_turned(t):
                act.wait_ge(transposed, t + 1)
                wait(act, routed, t - 1)
                nc.scalar.copy(h2t[:, t % 2], turned[:]).then_inc(t_copied, 1)

            def copy_logits(t):
                act.wait_ge(routed, t + 1)
                nc.scalar.copy(logits_t[0:NR, t * P:(t + 1) * P], logit[:, 0:P]).then_inc(l_copied, 1)

            for c in range(2):
                for q in range(QT):
                    act.wait_ge(raw_loaded[q % 2], 16 * (c * 2 + q // 2 + 1))
                    nc.scalar.copy(w_hi[:, c, q * SL:(q + 1) * SL, :], raw[:, q % 2]).then_inc(w_hi_done, 1)
            for t in range(TT + 3):
                if t < TT:
                    square(t)
                if 1 <= t <= TT:
                    root(t - 1)
                if 2 <= t < TT + 2:
                    copy_turned(t - 2)
                if t >= 3:
                    copy_logits(t - 3)

        @block.vector
        def _(dve):
            def w_lower(c, q):
                dve.wait_ge(w_hi_done, c * QT + q + 1)
                nc.vector.tensor_tensor(w_lo[:, c, q * SL:(q + 1) * SL, :], raw[:, q % 2],
                                        w_hi[:, c, q * SL:(q + 1) * SL, :].bitcast(F32), ALU.subtract
                                        ).then_inc(w_lo_done, 1)

            def add(n):
                c, t = divmod(n, TT)
                dve.wait_ge(x_loaded[n % 2], 16 * (n // 2 + 1))
                dve.wait_ge(projected, n + 1)
                nc.vector.tensor_tensor(x1[:, t, c * NW:(c + 1) * NW], acc[n % 4][:], xin[:, n % 2, :],
                                        ALU.add).then_inc(added, 1)

            def norm(t):
                at = slice(t, t + 1)
                dve.wait_ge(squared, t + 1)
                nc.vector.tensor_scalar(var[:, at], ssq[:, at], 1.0 / D, EPS, ALU.mult, ALU.add).then_inc(var_done, 1)
                dve.wait_ge(dev_done, t + 1)
                nc.vector.reciprocal(rstd[:, at], dev[:, at]).then_inc(rstd_done, 1)
                dve.wait_ge(rstd_done, t + 1)
                wait(dve, transposed, t - 1)
                wait(dve, h2_stored[t % 2], 16 * (t // 2))
                nc.vector.scalar_tensor_tensor(
                    out=h2[:, t % 2, :].rearrange("q (c p) -> q p c", c=KC), in0=x1[:, t, :].rearrange("q (p c) -> q p c", c=KC),
                    scalar=rstd[:, at], in1=g[:].rearrange("q (p c) -> q p c", c=KC), op0=ALU.mult, op1=ALU.mult
                ).then_inc(normed, 1)

            for q in range(QT):
                w_lower(0, q)
            dve.wait_ge(c_loaded, 32)
            for n in range(2 * TT):
                add(n)
                if n % 2 and n < TT:
                    w_lower(1, n // 2)
                if n > TT:
                    norm(n - TT - 1)
            norm(TT - 1)

        @block.tensor
        def _(pe):
            def products(n):
                c, t = divmod(n, TT)
                toks = slice(t * P, (t + 1) * P)
                wait(pe, added, n - 3)
                for k in range(KC):
                    if t == 0 and k % SL == 0:
                        pe.wait_ge(w_lo_done, c * QT + k // SL + 1)
                    last = three_passes(nc, acc[n % 4][:], mt_hi[:, k, toks], mt_lo[:, k, toks],
                                        w_hi[:, c, k, :], w_lo[:, c, k, :], k == 0, k == KC - 1)
                last.then_inc(projected, 1)

            def turn(t):
                pe.wait_ge(normed, t + 1)
                wait(pe, t_copied, t)
                for k in range(KC):
                    last = nc.tensor.transpose(turned[:, k, :], h2[:, t % 2, k * P:(k + 1) * P], ident[:])
                last.then_inc(transposed, 1)

            def route(t):
                pe.wait_ge(t_copied, t + 1)
                wait(pe, l_copied, t)
                for k in range(KC):
                    last = nc.tensor.matmul(logit[:, 0:P], router[:, k, :], h2t[:, t % 2, k, :],
                                            start=(k == 0), stop=(k == KC - 1))
                last.then_inc(routed, 1)

            for n in range(2 * TT + 3):
                t = n - TT
                if n < 2 * TT:
                    products(n)
                if n == TT:
                    pe.wait_ge(c_loaded, 32)
                    pe.wait_ge(r_loaded, 16 * (1 + NG))
                if 2 <= t < TT + 2:
                    turn(t - 2)
                if t >= 3:
                    route(t - 3)


class ExpertBlocks:

    HALF = D * FH // P // 2

    def __init__(self, nc, m, soft, w_gate, w_up, w_down, h2_dram, y_dram, row_idx, y_idx, ident, slots, first, psum):
        self.first = first
        self.nc, self.slots, self.row_idx, self.y_idx, self.ident = nc, slots, row_idx, y_idx, ident
        self.h2_dram, self.y_dram = h2_dram, y_dram
        self.w = (w_gate, w_up, w_down)
        self.raw = m.sb("raw", [P, 6, self.HALF])
        self.w_hi = m.sb("w_hi", [P, 6, self.HALF], F32R)
        self.w_lo = m.sb("w_lo", [P, 6, self.HALF], F32R)
        self.rows = m.sb("rows", [P, slots, D])
        self.row_of = [m.sb(f"row_of{b}", [P, 1], U32) for b in range(slots)]
        self.y_row_of = [m.sb(f"y_row_of{b}", [P, 1], U32) for b in range(slots)]
        self.xt_hi = m.sb("xt_hi", [P, slots, KC, P], F32R)
        self.xt_lo = m.sb("xt_lo", [P, slots, KC, P], F32R)
        self.act = m.sb("act", [P, FH])
        self.hid = m.sb("hid", [P, FH])
        self.ht_hi = m.sb("ht_hi", [P, FC, P], F32R)
        self.ht_lo = m.sb("ht_lo", [P, FC, P], F32R)
        self.y = m.sb("y", [P, slots, D])
        self.xt_ps, self.gate_ps, self.up_ps, self.ht_ps, self.y_ps = psum
        self.loaded = m.sems("loaded", 6)
        self.w_hi_done = m.sems("w_hi_done", 6)
        self.w_lo_done = m.sems("w_lo_done", 6)
        self.used = m.sems("used", 6)
        self.rows_cleared, self.row_ready, self.y_row_ready = m.sem("rows_cleared"), m.sem("row_ready"), m.sem("y_row_ready")
        self.gathered = soft.sems(f"{m.stage}_gathered", slots)
        self.stored = soft.sems(f"{m.stage}_stored", slots)
        self.x_turned, self.x_hi_done, self.x_lo_done = m.sem("x_turned"), m.sem("x_hi_done"), m.sem("x_lo_done")
        self.act_done, self.hid_done = m.sem("act_done"), m.sem("hid_done")
        self.h_turned, self.h_hi_done, self.h_lo_done = m.sem("h_turned"), m.sem("h_hi_done"), m.sem("h_lo_done")
        self.y_copied = m.sem("y_copied")

    def counts_of_blocks(self):
        return [*self.w_hi_done, *self.w_lo_done, *self.used, self.row_ready, self.y_row_ready, self.x_turned, self.x_hi_done,
                self.x_lo_done, self.act_done, self.hid_done, self.h_turned, self.h_hi_done, self.h_lo_done,
                self.y_copied]


    def load(self, sp, i, expert, mats):
        for h in [2 * w + j for w in mats for j in range(2)]:
            src = self.w[h // 2][0, expert].rearrange("(p c) n -> p (c n)", p=P)
            wait(sp, self.w_lo_done[h], i)
            sp.dma_start(self.raw[:, h, :], src[:, (h % 2) * self.HALF:(h % 2 + 1) * self.HALF]
                         ).then_inc(self.loaded[h], 16)

    def clear_rows(self, pool):
        self.nc.gpsimd.memset(self.rows[:], 0.0).then_inc(self.rows_cleared, 1)

    def gather(self, pool, i, b, column):
        wait(pool, self.x_turned, i + 1 - self.slots if not isinstance(i, int) or i >= self.slots else 0)
        self.nc.gpsimd.tensor_copy(self.row_of[b][:], self.row_idx[:, bass.ds(column, 1)]).then_inc(self.row_ready, 1)
        rows_due = held_value(pool, i + 1)
        pool.wait_ge(self.rows_cleared, 1)
        pool.wait_ge(self.row_ready, rows_due)
        pool.indirect_dma_start(out=self.rows[:, b, :], out_offset=None, in_=self.h2_dram,
                                in_offset=bass.IndirectOffsetOnAxis(ap=self.row_of[b][:, 0:1], axis=0),
                                bounds_check=S - 1, oob_is_err=False).then_inc(self.gathered[b], 16)

    def store_y(self, pool, i, b, n, column):
        if n is not None:
            wait(pool, self.stored[b], n * 16)
        self.nc.gpsimd.tensor_copy(self.y_row_of[b][:], self.y_idx[:, bass.ds(column, 1)]).then_inc(self.y_row_ready, 1)
        rows_due, copies_due = held_value(pool, i + 1), held_value(pool, i + 1)
        pool.wait_ge(self.rows_cleared, 1)
        pool.wait_ge(self.y_row_ready, rows_due)
        pool.wait_ge(self.y_copied, copies_due)
        pool.indirect_dma_start(out=self.y_dram,
                                out_offset=bass.IndirectOffsetOnAxis(ap=self.y_row_of[b][:, 0:1], axis=0),
                                in_=self.y[:, b, :], in_offset=None, bounds_check=2 * S - 1, oob_is_err=False
                                ).then_inc(self.stored[b], 16)

    def turn_x(self, pe, i, b, n):
        pe.wait_ge(self.gathered[b], n * 16 + 16)
        wait(pe, self.x_lo_done, i)
        for k in range(KC):
            last = self.nc.tensor.transpose(self.xt_ps[:, k, :], self.rows[:, b, k * P:(k + 1) * P], self.ident[:])
        last.then_inc(self.x_turned, 1)

    def x_upper(self, act, i, b):
        act.wait_ge(self.x_turned, i + 1)
        wait(act, self.used[3], i + 1 - self.slots if not isinstance(i, int) or i >= self.slots else 0)
        self.nc.scalar.copy(self.xt_hi[:, b], self.xt_ps[:]).then_inc(self.x_hi_done, 1)

    def x_lower(self, dve, i, b):
        dve.wait_ge(self.x_hi_done, i + 1)
        self.nc.vector.tensor_tensor(self.xt_lo[:, b], self.xt_ps[:], self.xt_hi[:, b].bitcast(F32),
                                     ALU.subtract).then_inc(self.x_lo_done, 1)

    def w_upper(self, act, i, h):
        act.wait_ge(self.loaded[h], (i - self.first) * 16 + 16)
        wait(act, self.used[h], i)
        self.nc.scalar.copy(self.w_hi[:, h, :], self.raw[:, h, :]).then_inc(self.w_hi_done[h], 1)

    def w_lower(self, dve, i, h):
        dve.wait_ge(self.w_hi_done[h], i + 1)
        self.nc.vector.tensor_tensor(self.w_lo[:, h, :], self.raw[:, h, :], self.w_hi[:, h, :].bitcast(F32),
                                     ALU.subtract).then_inc(self.w_lo_done[h], 1)

    def into_hidden(self, pe, i, b, mat, half):
        if half == 0:
            if mat == 0:
                pe.wait_ge(self.x_lo_done, i + 1)
            wait(pe, (self.act_done, self.hid_done)[mat], i)
        h = 2 * mat + half
        pe.wait_ge(self.w_lo_done[h], i + 1)
        for j in range(KC // 2):
            k = half * (KC // 2) + j
            cols = slice(j * FH, (j + 1) * FH)
            last = three_passes(self.nc, (self.gate_ps, self.up_ps)[mat][:], self.xt_hi[:, b, k], self.xt_lo[:, b, k],
                                self.w_hi[:, h, cols], self.w_lo[:, h, cols], k == 0, k == KC - 1)
        last.then_inc(self.used[h], 1)

    def silu(self, act, i):
        act.wait_ge(self.used[1], i + 1)
        wait(act, self.hid_done, i)
        self.nc.scalar.activation(self.act[:], self.gate_ps[:], ACT.Silu).then_inc(self.act_done, 1)

    def hidden(self, dve, i):
        dve.wait_ge(self.act_done, i + 1)
        dve.wait_ge(self.used[3], i + 1)
        wait(dve, self.h_turned, i)
        self.nc.vector.tensor_tensor(self.hid[:].rearrange("q (c p) -> q p c", c=FC),
                                     self.up_ps[:].rearrange("q (p c) -> q p c", c=FC),
                                     self.act[:].rearrange("q (p c) -> q p c", c=FC), ALU.mult
                                     ).then_inc(self.hid_done, 1)

    def turn_h(self, pe, i):
        pe.wait_ge(self.hid_done, i + 1)
        wait(pe, self.h_lo_done, i)
        for k in range(FC):
            last = self.nc.tensor.transpose(self.ht_ps[:, k, :], self.hid[:, k * P:(k + 1) * P], self.ident[:])
        last.then_inc(self.h_turned, 1)

    def h_upper(self, act, i):
        act.wait_ge(self.h_turned, i + 1)
        wait(act, self.used[5], i)
        self.nc.scalar.copy(self.ht_hi[:], self.ht_ps[:]).then_inc(self.h_hi_done, 1)

    def h_lower(self, dve, i):
        dve.wait_ge(self.h_hi_done, i + 1)
        self.nc.vector.tensor_tensor(self.ht_lo[:], self.ht_ps[:], self.ht_hi[:].bitcast(F32),
                                     ALU.subtract).then_inc(self.h_lo_done, 1)

    def down(self, pe, i):
        pe.wait_ge(self.h_lo_done, i + 1)
        wait(pe, self.y_copied, i)
        for half in range(2):
            h = 4 + half
            pe.wait_ge(self.w_lo_done[h], i + 1)
            for j in range(FC // 2):
                k = half * (FC // 2) + j
                for c in range(D // NW):
                    cols = slice(j * D + c * NW, j * D + (c + 1) * NW)
                    last = three_passes(self.nc, self.y_ps[:, c, :], self.ht_hi[:, k], self.ht_lo[:, k],
                                        self.w_hi[:, h, cols], self.w_lo[:, h, cols], k == 0, k == FC - 1)
            last.then_inc(self.used[h], 1)

    def copy_y(self, act, i, b, n):
        act.wait_ge(self.used[5], i + 1)
        if n is not None:
            wait(act, self.stored[b], n * 16)
        self.nc.scalar.copy(self.y[:, b, :], self.y_ps[:].rearrange("p c n -> p (c n)")).then_inc(self.y_copied, 1)


def psum_of_experts(m):
    return (m.ps("xt", [P, KC, P]), m.ps("gate", [P, FH]), m.ps("up", [P, FH]), m.ps("ht", [P, FC, P]),
            m.ps("y", [P, D // NW, NW]))


def route_and_experts(nc, soft, consts, b_rg, b_re, w_gate, w_up, w_down, logits_t, row_idx, y_idx, gates, over,
                      h2_dram, y_dram):
    with ExitStack() as ctx:
        m = Scope(nc, ctx, "moe")
        ident, tri, ones = m.sb("ident", [P, P]), m.sb("tri", [P, P]), m.sb("ones", [P, P])
        small = m.sb("small", [P, C_LOG - C_D4])
        iota = m.sb("iota", [P, P])
        bias = m.sb("bias", [P, NR])
        logits = m.sb("logits", [P, TT, NR])
        g_max, g_sum, g_gate, g_key = (m.sb(n, [P, TT]) for n in ("g_max", "g_sum", "g_gate", "g_key"))
        g_one, g_exp = m.sb("g_one", [P, TT, NG]), m.sb("g_exp", [P, TT, NG])
        e_all = m.sb("e_all", [P, TT, NG, NE])
        e_logit = m.sb("e_logit", [P, 2, TT, NE])
        e_max, e_key = m.sb("e_max", [P, 2, TT]), m.sb("e_key", [P, 2, TT])
        e_one = m.sb("e_one", [P, 2, TT, NE])
        ratio, total = m.sb("ratio", [P, TT]), m.sb("total", [P, TT])
        chosen = m.sb("chosen", [P, 2, TT, E])
        both = m.sb("both", [P, E, TT])
        same_expert = m.sb("same_expert", [P, E, TT])
        block_row = logits_t[:, 0:2 * TT * NB].rearrange("p (k t b) -> p k t b", k=2, t=TT)
        up_to = logits_t[:, 2 * TT * NB:2 * TT * NB + E * TT].rearrange("p (e t) -> p e t", e=E)
        before = m.sb("before", [P, E, TT])
        rank_all = m.sb("rank_all", [P, TT, E])
        pick = m.sb("pick", [P, 2, TT, E])
        rank, eid, base, beyond, many = (m.sb(n, [P, 2, TT]) for n in ("rank", "eid", "base", "beyond", "many"))
        column = m.sb("column", [P, 2, TT])
        further = m.sb("further", [P, 2, TT, TT - 1])
        more_than = m.sb("more_than", [P, E, TT - 1])
        to_row = m.sb("to_row", [P, 2, TT])
        vacant, y_row, is_second = (m.sb(n, [P, NB]) for n in ("vacant", "y_row", "is_second"))
        count, more, end, begin = (m.sb(n, [P, E]) for n in ("count", "more", "end", "begin"))
        ended = m.sb("ended", [P, MOST, E])
        over_f = m.sb("over_f", [P, 1 + MOST])
        psum = psum_of_experts(m)
        by_token = psum[3][:].rearrange("p a b -> p (a b)").rearrange("p (t e) -> p t e", t=TT)
        rank_ps = psum[1][:, 0:TT * E].rearrange("p (e t) -> p t e", t=TT)
        count_ps = psum[2][:, 0:E]
        table_ps = psum[4][:, 0, 0:NB]
        c_loaded, b_loaded = m.sem("c_loaded"), m.sem("b_loaded")
        l_turned, near, exp_done = m.sem("l_turned"), m.sem("near"), m.sem("exp_done")
        link_sem, chosen_done, ranked = m.sem("link"), m.sem("chosen_done"), m.sem("ranked")
        hot_done, tabled, idx_ready = m.sem("hot_done"), m.sem("tabled"), m.sem("idx_ready")
        x = ExpertBlocks(nc, m, soft, w_gate, w_up, w_down, h2_dram, y_dram, row_idx, y_idx, ident, 2, 0, psum)
        slot_hot = x.y[:].rearrange("p k (t s) -> p k t s", t=TT)
        o = -C_D4
        d4, d8 = small[:, C_D4 + o:C_D8 + o], small[:, C_D8 + o:C_EID + o]
        eids, th, toks = small[:, C_EID + o:C_TH + o], small[:, C_TH + o:C_TOK + o], small[:, C_TOK + o:C_LOG + o]
        block = ctx.enter_context(nc.Block())

        @block.sync
        def _(sp):
            x.load(sp, 0, 0, (0, 1))
            sp.dma_start(ident[:], consts[:, C_ID:C_ID + P]).then_inc(c_loaded, 16)
            sp.dma_start(tri[:], consts[:, C_TRI:C_TRI + P]).then_inc(c_loaded, 16)
            sp.dma_start(ones[:], consts[:, C_ONE:C_ONE + P]).then_inc(c_loaded, 16)
            sp.dma_start(small[:], consts[:, C_D4:C_LOG]).then_inc(c_loaded, 16)
            sp.dma_start(iota[:], consts[:, C_IOTA:C_ALL]).then_inc(c_loaded, 16)
            sp.dma_start(bias[:, 0:NG], b_rg[0:1, :].to_broadcast([P, NG])).then_inc(b_loaded, 16)
            sp.dma_start(bias[:, NG:NR], b_re.rearrange("a g e -> a (g e)").to_broadcast([P, E])).then_inc(b_loaded, 16)
            def further(i):
                x.load(sp, i, i, (0,))
                x.load(sp, i - 1, i - 1, (2,))
                x.load(sp, i, i, (1,))

            further(1)
            with sp.Fori(2, E) as i:
                further(i)
            x.load(sp, E - 1, E - 1, (2,))

        @block.gpsimd
        def _(pool):
            x.clear_rows(pool)
            pool.wait_ge(idx_ready, 1)
            x.gather(pool, 0, 0, 0)
            x.gather(pool, 1, 1, 1)
            x.gather(pool, 2, 0, 2)
            x.gather(pool, 3, 1, 3)
            x.store_y(pool, 0, 0, 0, 0)
            x.gather(pool, 4, 0, 4)
            x.store_y(pool, 1, 1, 0, 1)
            x.gather(pool, 5, 1, 5)
            with pool.Fori(1, E // 2 - 2) as j:
                x.store_y(pool, j * 2, 0, j, j * 2)
                x.gather(pool, j * 2 + 4, 0, j * 2 + 4)
                x.store_y(pool, j * 2 + 1, 1, j, j * 2 + 1)
                x.gather(pool, j * 2 + 5, 1, j * 2 + 5)
            for i in range(E - 4, E):
                x.store_y(pool, i, i % 2, i // 2, i)
            for b in range(2):
                pool.wait_ge(x.stored[b], 16 * E // 2)

        @block.scalar
        def _(act):
            def step(i, b, n, first=False, last=False):
                before_1 = n if b else n - 1
                if not first:
                    x.w_upper(act, i - 1, 4)
                    x.h_upper(act, i - 1)
                    x.w_upper(act, i - 1, 5)
                x.w_upper(act, i, 2)
                x.silu(act, i)
                x.w_upper(act, i, 3)
                if not last:
                    x.w_upper(act, i + 1, 0)
                if not first:
                    x.copy_y(act, i - 1, 1 - b, before_1)
                if not last:
                    x.x_upper(act, i + 1, 1 - b)
                    x.w_upper(act, i + 1, 1)

            act.wait_ge(near, 1)
            nc.scalar.activation(g_exp[:], g_exp[:], ACT.Exp).then_inc(exp_done, 1)
            act.wait_ge(near, 2)
            nc.scalar.activation(ratio[:], ratio[:], ACT.Exp).then_inc(exp_done, 1)
            x.w_upper(act, 0, 0)
            x.w_upper(act, 0, 1)
            x.x_upper(act, 0, 0)
            step(0, 0, 0, first=True)
            step(1, 1, 0)
            step(2, 0, 1)
            with act.Fori(1, E // 2 - 1) as j:
                step(j * 2 + 1, 1, j)
                step(j * 2 + 2, 0, j + 1)
            step(E - 1, 1, E // 2 - 1, last=True)
            x.w_upper(act, E - 1, 4)
            x.h_upper(act, E - 1)
            x.w_upper(act, E - 1, 5)
            x.copy_y(act, E - 1, 1, E // 2 - 1)

        @block.vector
        def _(dve):
            v = nc.vector
            link = Chain(dve, link_sem)

            def wide(a, n):
                return a.unsqueeze(len(a.shape)).to_broadcast([*a.shape, n])

            def rows(a, *shape):
                for _ in range(len(shape) - 1):
                    a = a.unsqueeze(1)
                return a.to_broadcast([P, *shape])

            def first_of(values, most, key, one, order):
                n = values.shape[-1]
                link(v.tensor_reduce(most, values, AX_X, ALU.max))
                link(v.tensor_tensor(one, values, wide(most, n), ALU.is_equal))
                link(v.tensor_tensor(one, one, rows(order, TT, n), ALU.mult))
                link(v.tensor_reduce(key, one, AX_X, ALU.max))
                link(v.tensor_tensor(one, one, wide(key, n), ALU.is_equal))

            dve.wait_ge(c_loaded, 80)
            dve.wait_ge(b_loaded, 32)
            link(v.memset(same_expert[:], 1.0))
            link(v.memset(same_expert[:, :, 0:1], 0.0))
            dve.wait_ge(l_turned, 1)
            link(v.tensor_tensor(logits[:], by_token[:, :, 0:NR], rows(bias[:], TT, NR), ALU.add))
            gl = logits[:, :, 0:NG]
            first_of(gl, g_max[:], g_key[:], g_one[:], d4)
            v.tensor_tensor(g_exp[:], gl, wide(g_max[:], NG), ALU.subtract).then_inc(near, 1)
            link(v.tensor_tensor(e_all[:], logits[:, :, NG:NR].rearrange("p t (g e) -> p t g e", g=NG),
                                 wide(g_one[:], NE), ALU.mult))
            link(v.tensor_reduce(e_logit[:, 0], e_all[:].rearrange("p t g e -> p t e g"), AX_X, ALU.add))
            first_of(e_logit[:, 0], e_max[:, 0], e_key[:, 0], e_one[:, 0], d8)
            link(v.scalar_tensor_tensor(out=e_logit[:, 1], in0=e_one[:, 0], scalar=-3e38, in1=e_logit[:, 0],
                                        op0=ALU.mult, op1=ALU.add))
            first_of(e_logit[:, 1], e_max[:, 1], e_key[:, 1], e_one[:, 1], d8)
            v.tensor_tensor(ratio[:], e_max[:, 1], e_max[:, 0], ALU.subtract).then_inc(near, 1)
            for k in range(2):
                for g in range(NG):
                    ins = v.tensor_tensor(chosen[:, k, :, g * NE:(g + 1) * NE], e_one[:, k],
                                          wide(g_one[:, :, g], NE), ALU.mult)
                    if (k, g) == (1, NG - 1):
                        link(ins)
            link(v.tensor_tensor(both[:].rearrange("p e t -> p t e"), chosen[:, 0], chosen[:, 1], ALU.add))
            link(v.tensor_tensor_scan(up_to.rearrange("p e t -> p (e t)"),
                                      same_expert[:].rearrange("p e t -> p (e t)"),
                                      both[:].rearrange("p e t -> p (e t)"), 0.0, ALU.mult, ALU.add))
            v.tensor_tensor(before[:], up_to, both[:], ALU.subtract).then_inc(chosen_done, 1)
            for k in range(2):
                link(v.tensor_scalar(to_row[:, k, :], toks, float(k * S + 1), None, ALU.add))
            link(v.tensor_tensor(pick[:], chosen[:], rows(eids, 2, TT, E), ALU.mult))
            link(v.tensor_reduce(eid[:], pick[:], AX_X, ALU.add))
            dve.wait_ge(ranked, 1)
            link(v.tensor_copy(count[:], count_ps))
            link(v.tensor_copy(rank_all[:], rank_ps))
            link(v.scalar_tensor_tensor(out=more_than[:], in0=wide(count[:], TT - 1), scalar=1.0 / P,
                                        in1=rows(th[:, 1:TT], E, TT - 1), op0=ALU.mult, op1=ALU.is_gt))
            link(v.tensor_reduce(more[:], more_than[:], AX_X, ALU.add))
            link(v.tensor_tensor_scan(end[:], ones[:, 0:E], more[:], 0.0, ALU.mult, ALU.add))
            link(v.tensor_tensor(begin[:], end[:], more[:], ALU.subtract))
            for values, result in ((rank_all[:], rank), (rows(begin[:], TT, E), base)):
                for k in range(2):
                    link(v.tensor_tensor(pick[:, k], chosen[:, k], values, ALU.mult))
                link(v.tensor_reduce(result[:], pick[:], AX_X, ALU.add))
            link(v.scalar_tensor_tensor(out=further[:].rearrange("p k t n -> p (k t) n"),
                                        in0=wide(rank[:].rearrange("p k t -> p (k t)"), TT - 1), scalar=1.0 / P,
                                        in1=rows(th[:, 1:TT], 2 * TT, TT - 1), op0=ALU.mult, op1=ALU.is_ge))
            link(v.tensor_reduce(beyond[:], further[:], AX_X, ALU.add))
            link(v.tensor_scalar(many[:], beyond[:], 1.0, None, ALU.min))
            link(v.scalar_tensor_tensor(out=column[:], in0=base[:], scalar=float(E - 1), in1=beyond[:],
                                        op0=ALU.add, op1=ALU.add))
            link(v.tensor_tensor(column[:], column[:], eid[:], ALU.subtract))
            link(v.tensor_tensor(column[:], column[:], many[:], ALU.mult))
            link(v.tensor_tensor(column[:], column[:], eid[:], ALU.add))
            link(v.scalar_tensor_tensor(out=rank[:], in0=beyond[:], scalar=-float(P), in1=rank[:],
                                        op0=ALU.mult, op1=ALU.add))
            for k in range(2):
                v.tensor_tensor(slot_hot[:, k], rows(iota[:], TT, P), wide(rank[:, k], P), ALU.is_equal)
                link(v.tensor_tensor(block_row[:, k], rows(iota[:, 0:NB], TT, NB),
                                     wide(column[:, k], NB), ALU.is_equal))
                v.tensor_tensor(block_row[:, k], block_row[:, k], wide(to_row[:, k], NB),
                                ALU.mult).then_inc(hot_done, 1)
            dve.wait_ge(tabled, 1)
            link(v.tensor_scalar(vacant[:], table_ps, 0.0, float(4 * S), ALU.is_equal, ALU.mult))
            link(v.scalar_tensor_tensor(out=y_row[:], in0=table_ps, scalar=-1.0, in1=vacant[:],
                                        op0=ALU.add, op1=ALU.add))
            link(v.tensor_scalar(is_second[:], y_row[:], float(S), float(-S), ALU.is_ge, ALU.mult))
            link(v.tensor_tensor(row_idx[:], y_row[:], is_second[:], ALU.add))
            v.tensor_copy(y_idx[:], y_row[:]).then_inc(idx_ready, 1)
            dve.wait_ge(exp_done, 2)
            link(v.tensor_reduce(g_sum[:], g_exp[:], AX_X, ALU.add))
            link(v.reciprocal(g_gate[:], g_sum[:]))
            link(v.tensor_scalar(total[:], ratio[:], 1.0, None, ALU.add))
            link(v.reciprocal(total[:], total[:]))
            link(v.tensor_tensor(gates[:, 0, :], g_gate[:], total[:], ALU.mult))
            link(v.tensor_tensor(gates[:, 1, :], gates[:, 0, :], ratio[:], ALU.mult))
            link(v.tensor_tensor(ended[:], rows(end[:], MOST, E), wide(th, E), ALU.is_le))
            link(v.tensor_copy(over_f[:, 0:1], end[:, E - 1:E]))
            link(v.tensor_reduce(over_f[:, 1:], ended[:], AX_X, ALU.add))
            link(v.tensor_scalar(over_f[:, 1:], over_f[:, 1:], float(E - 1), None, ALU.min))
            link(v.tensor_copy(over[:], over_f[:]))

            def step(i, first=False, last=False):
                b = None
                if not first:
                    x.hidden(dve, i - 1)
                    x.w_lower(dve, i - 1, 4)
                    x.h_lower(dve, i - 1)
                    x.w_lower(dve, i - 1, 5)
                x.w_lower(dve, i, 2)
                x.w_lower(dve, i, 3)

            def ahead(i, b):
                x.w_lower(dve, i, 0)
                x.x_lower(dve, i, b)
                x.w_lower(dve, i, 1)

            x.w_lower(dve, 0, 0)
            x.w_lower(dve, 0, 1)
            x.x_lower(dve, 0, 0)
            step(0, first=True)
            ahead(1, 1)
            step(1)
            ahead(2, 0)
            step(2)
            ahead(3, 1)
            with dve.Fori(1, E // 2 - 1) as j:
                step(j * 2 + 1)
                ahead(j * 2 + 2, 0)
                step(j * 2 + 2)
                ahead(j * 2 + 3, 1)
            step(E - 1)
            x.hidden(dve, E - 1)
            x.w_lower(dve, E - 1, 4)
            x.h_lower(dve, E - 1)
            x.w_lower(dve, E - 1, 5)

        @block.tensor
        def _(pe):
            pe.wait_ge(c_loaded, 80)
            for t in range(TT):
                last = nc.tensor.transpose(by_token[:, t, 0:NR], logits_t[0:NR, t * P:(t + 1) * P],
                                           ident[0:NR, 0:NR])
            last.then_inc(l_turned, 1)
            pe.wait_ge(chosen_done, 1)
            nc.tensor.matmul(psum[1][:, 0:TT * E], tri[:], both[:].rearrange("p e t -> p (e t)"), start=True, stop=False)
            nc.tensor.matmul(psum[1][:, 0:TT * E], ones[:], before[:].rearrange("p e t -> p (e t)"),
                             start=False, stop=True)
            nc.tensor.matmul(count_ps, ones[:], up_to[:, :, TT - 1], start=True, stop=True).then_inc(ranked, 1)
            for k in range(2):
                pe.wait_ge(hot_done, k + 1)
                for t in range(TT):
                    last = nc.tensor.matmul(table_ps, slot_hot[:, k, t, :], block_row[:, k, t, :],
                                            start=(k == 0 and t == 0), stop=(k == 1 and t == TT - 1))
            last.then_inc(tabled, 1)

            def step(i, b, n, first=False, last=False):
                x.into_hidden(pe, i, b, 0, 0)
                if not first:
                    x.turn_h(pe, i - 1)
                x.into_hidden(pe, i, b, 0, 1)
                if not first:
                    x.down(pe, i - 1)
                if not last:
                    x.turn_x(pe, i + 1, 1 - b, n + 1 if b else n)
                x.into_hidden(pe, i, b, 1, 0)
                x.into_hidden(pe, i, b, 1, 1)

            x.turn_x(pe, 0, 0, 0)
            pe.wait_ge(idx_ready, 1)
            step(0, 0, 0, first=True)
            step(1, 1, 0)
            step(2, 0, 1)
            with pe.Fori(1, E // 2 - 1) as j:
                step(j * 2 + 1, 1, j)
                step(j * 2 + 2, 0, j + 1)
            step(E - 1, 1, E // 2 - 1, last=True)
            x.turn_h(pe, E - 1)
            x.down(pe, E - 1)


def blocks_beyond(nc, soft, consts, w_gate, w_up, w_down, row_idx, y_idx, over, h2_dram, y_dram):
    with ExitStack() as ctx:
        m = Scope(nc, ctx, "beyond")
        ident = m.sb("ident", [P, P])
        id_loaded, started = m.sem("id_loaded"), m.sem("started")
        x = ExpertBlocks(nc, m, soft, w_gate, w_up, w_down, h2_dram, y_dram, row_idx, y_idx, ident, 1, 1,
                         psum_of_experts(m))
        block = ctx.enter_context(nc.Block())

        def each(eng, body):
            n = eng.value_load(over[0:1, 0:1], min_val=0, max_val=MOST - 1)
            with eng.If(n > 0):
                if eng is nc.gpsimd:
                    for s in x.counts_of_blocks():
                        eng.sem_inc(s, 1)
                    eng.sem_inc(started, 1)
                eng.wait_ge(started, 1)
                with eng.Fori(1, n + 1) as i:
                    body(i)

        @block.sync
        def _(sp):
            sp.dma_start(ident[:], consts[:, C_ID:C_ID + P]).then_inc(id_loaded, 16)

            def body(i):
                expert = sp.value_load(over[0:1, bass.ds(i, 1)], min_val=0, max_val=E - 1)
                x.load(sp, i, expert, (0, 1, 2))

            each(sp, body)

        @block.gpsimd
        def _(pool):
            x.clear_rows(pool)

            def body(i):
                x.gather(pool, i, 0, i + E - 1)
                x.store_y(pool, i, 0, None, i + E - 1)
                pool.wait_ge(x.stored[0], i * 16)

            each(pool, body)

        @block.scalar
        def _(act):
            def body(i):
                x.x_upper(act, i, 0)
                for h in range(4):
                    x.w_upper(act, i, h)
                x.silu(act, i)
                x.w_upper(act, i, 4)
                x.w_upper(act, i, 5)
                x.h_upper(act, i)
                x.copy_y(act, i, 0, None)

            each(act, body)

        @block.vector
        def _(dve):
            def body(i):
                x.x_lower(dve, i, 0)
                for h in range(4):
                    x.w_lower(dve, i, h)
                x.w_lower(dve, i, 4)
                x.w_lower(dve, i, 5)
                x.hidden(dve, i)
                x.h_lower(dve, i)

            each(dve, body)

        @block.tensor
        def _(pe):
            pe.wait_ge(id_loaded, 16)

            def body(i):
                x.turn_x(pe, i, 0, i - 1)
                for mat in range(2):
                    for half in range(2):
                        x.into_hidden(pe, i, 0, mat, half)
                x.turn_h(pe, i)
                x.down(pe, i)

            each(pe, body)


def clear_released_semaphores(nc):
    ids = sorted(nc.released_uncleared_semaphores)
    first = [i for i in ids if i - 1 not in ids]
    last = [i for i in ids if i + 1 not in ids]
    with nc.Block() as block:
        @block.gpsimd
        def _(pool):
            for a, b in zip(first, last):
                pool.sem_clear(range(a, b + 1))


def combine(nc, gates, x1_dram, y_dram, out):
    with ExitStack() as ctx:
        m = Scope(nc, ctx, "sum")
        x1 = m.sb("x1", [P, TT, D])
        y = m.sb("y", [P, TT, 2, D])
        x_loaded, y_loaded = m.sems("x_loaded", TT), m.sems("y_loaded", TT)
        first, added, stored = m.sem("first"), m.sem("added"), m.sem("stored")
        block = ctx.enter_context(nc.Block())

        @block.sync
        def _(sp):
            y_rows = y_dram.rearrange("(k t p) d -> t p k d", k=2, p=P)
            for t in range(TT):
                sp.dma_start(x1[:, t, :], x1_dram[t * P:(t + 1) * P, :]).then_inc(x_loaded[t], 16)
                sp.dma_start(y[:, t], y_rows[t]).then_inc(y_loaded[t], 16)

        @block.vector
        def _(dve):
            for t in range(TT):
                dve.wait_ge(x_loaded[t], 16)
                dve.wait_ge(y_loaded[t], 16)
                for k, done in ((0, first), (1, added)):
                    nc.vector.scalar_tensor_tensor(out=x1[:, t, :], in0=y[:, t, k, :], scalar=gates[:, k, t:t + 1],
                                                   in1=x1[:, t, :], op0=ALU.mult, op1=ALU.add).then_inc(done, 1)
                    if k == 0:
                        dve.wait_ge(first, t + 1)

        @block.scalar
        def _(act):
            for t in range(TT):
                act.wait_ge(added, t + 1)
                act.dma_start(out[0, t * P:(t + 1) * P, :], x1[:, t, :]).then_inc(stored, 16)
            act.wait_ge(stored, 16 * TT)


def decoder_layer(nc, x, norm1_g, w_in, q_norm_g, k_norm_g, w_attn_out, w_pool_mix, pool_scale, w_pool_out, w_o,
                  norm2_g, w_rg, b_rg, w_re, b_re, w_gate, w_up, w_down, consts, out):
    def dram(name, shape, dt=F32):
        return nc.dram_tensor(name, shape, dt).ap()

    u_dram = dram("u_scratch", [PG, P, S])
    gates_dram = dram("gates_scratch", [S, 2 * D])
    x1_dram = dram("x1_scratch", [S, D])
    h2_dram = dram("h2_scratch", [S, D])
    y_dram = dram("y_scratch", [2 * S, D])

    def held(ctx, side, *tensors):
        return [ctx.enter_context(nc.sbuf_tensor(n, s, d, side=side)) for n, s, d in tensors]

    heads, merged, branches, qkv_held = ExitStack(), ExitStack(), ExitStack(), ExitStack()
    with ExitStack() as small:
        soft = Scope(nc, small, "soft")
        h_hi, h_lo = held(heads, "left", ("h_hi", [P, KC, S], F32R), ("h_lo", [P, KC, S], F32R))
        norm_and_transpose(nc, x, norm1_g, consts, h_hi, h_lo)
        qkv, rqk = held(qkv_held, "right", ("qkv", [P, 3, TT, AW], F32), ("rqk", [P, 2, TT, NH], F32))
        project(nc, w_in, h_hi, h_lo, qkv, rqk, u_dram, gates_dram)
        heads.close()
        attn_hi, attn_lo, pooled = held(branches, "left", ("attn_hi", [P, AW // P, S], F32R),
                                        ("attn_lo", [P, AW // P, S], F32R), ("pooled", [P, PG, S], F32))
        attend(nc, consts, q_norm_g, k_norm_g, u_dram, qkv, rqk, attn_hi, attn_lo, pooled)
        qkv_held.close()
        pool_hi, pool_lo = held(branches, "left", *((n, [P, PG, S], F32R) for n in ("pool_hi", "pool_lo")))
        mt_hi, mt_lo = held(merged, "right", ("mt_hi", [P, KC, S], F32R), ("mt_lo", [P, KC, S], F32R))
        merge(nc, consts, gates_dram, w_attn_out, w_pool_mix, pool_scale, w_pool_out, attn_hi, attn_lo, pooled,
              pool_hi, pool_lo, mt_hi, mt_lo)
        branches.close()
        logits_t, row_idx, y_idx, gates, over = held(
            small, "left", ("logits_t", [P, S], F32), ("row_idx", [P, NB], U32), ("y_idx", [P, NB], U32),
            ("gates", [P, 2, TT], F32), ("over", [P, 1 + MOST], I32))
        output_and_norm(nc, consts, x, w_o, norm2_g, w_rg, w_re, mt_hi, mt_lo, logits_t, x1_dram, h2_dram)
        merged.close()
        route_and_experts(nc, soft, consts, b_rg, b_re, w_gate, w_up, w_down, logits_t, row_idx, y_idx, gates,
                          over, h2_dram, y_dram)
        clear_released_semaphores(nc)
        blocks_beyond(nc, soft, consts, w_gate, w_up, w_down, row_idx, y_idx, over, h2_dram, y_dram)
        combine(nc, gates, x1_dram, y_dram, out)


_INS = ["x", "norm1_g", "w_in", "q_norm_g", "k_norm_g", "w_attn_out", "w_pool_mix", "pool_scale", "w_pool_out", "w_o",
        "norm2_g", "w_router_group", "b_router_group", "w_router_expert", "b_router_expert", "w_exp_gate",
        "w_exp_up", "w_exp_down"]
_OUTS = [((1, S, D), "float32")]


def kernel(**inputs):
    import numpy as _np
    import concourse.bacc as _bacc
    from concourse import mybir as _mybir
    from concourse.bass_utils import run_bass_kernel_spmd as _run

    nc = _bacc.Bacc("TRN2", target_bir_lowering=False, num_devices=1)
    arrays, args = {}, []
    for name, a in [(n, _np.ascontiguousarray(inputs[n])) for n in _INS] + [("shape_constants", shape_constants())]:
        arrays[f"in_{name}_dram"] = a
        args.append(nc.dram_tensor(f"in_{name}_dram", a.shape, _mybir.dt.from_np(a.dtype), kind="ExternalInput").ap())
    for i, (shape, dtype) in enumerate(_OUTS):
        dt = _mybir.dt.from_np(_np.dtype(dtype))
        args.append(nc.dram_tensor(f"out_{i}_dram", shape, dt, kind="ExternalOutput").ap())
    decoder_layer(nc, *args)
    r = _run(nc, [arrays], core_ids=[0])
    return r.results[0]["out_0_dram"]
```

```python
from contextlib import ExitStack

import numpy as np

import concourse.bass as bass
from concourse import mybir

P = 128
ALU = mybir.AluOpType
ACT = mybir.ActivationFunctionType
AX_X = mybir.AxisListType.X
F32 = mybir.dt.float32
F32R = mybir.dt.float32r
I32 = mybir.dt.int32
U32 = mybir.dt.uint32
F16 = mybir.dt.float16

D = 1024
S = 1024
KC = D // P
TT = S // P
HD = 64
NH = 8
AW = NH * HD
PG = 4
WIN = (2, 4, 8, 16)
NW = 512
DILATED = ((128, 1), (512, 4), (2048, 16))
NG, NE = 4, 8
E = NG * NE
FH = 512
FC = FH // P
NR = NG + E
EPS = 1e-6
MASKED = -1e30
MOST = 16
NB = E + MOST
PAD = max(WIN)

C_ID, C_TRI, C_ONE = 0, P, 2 * P
C_CNT = 3 * P
C_D4 = C_CNT + PG * PAD
C_D8 = C_D4 + NG
C_EID = C_D8 + NE
C_TH = C_EID + E
C_TOK = C_TH + MOST
C_LOG = C_TOK + TT
C_IOTA = C_LOG + S
C_ALL = C_IOTA + P


def shape_constants():
    c = np.zeros((P, C_ALL), np.float32)
    r = np.arange(P)
    c[:, C_ID:C_ID + P] = np.eye(P)
    c[:, C_TRI:C_TRI + P] = r[:, None] < r[None, :]
    c[:, C_ONE:C_ONE + P] = 1
    for g, w in enumerate(WIN):
        c[:, C_CNT + g * PAD:C_CNT + (g + 1) * PAD] = w / np.minimum(np.arange(PAD) + 1, w)
    c[:, C_D4:C_D4 + NG] = NG - np.arange(NG)
    c[:, C_D8:C_D8 + NE] = NE - np.arange(NE)
    c[:, C_EID:C_EID + E] = np.arange(E)
    c[:, C_TH:C_TH + MOST] = np.arange(MOST)
    c[:, C_TOK:C_TOK + TT] = np.arange(TT)[None, :] * P + r[:, None]
    dist = r[:, None] + (S - P) - np.arange(S)[None, :]
    held = sum(((dist >= 0) & (dist <= w) & (dist % d == 0)).astype(np.int64) for w, d in DILATED)
    c[:, C_IOTA:C_ALL] = np.arange(P)
    c[:, C_LOG:C_LOG + S] = np.where(held > 0, np.log(np.maximum(held, 1)), MASKED)
    return c


def wait(eng, sem, value):
    if not isinstance(value, int) or value > 0:
        eng.wait_ge(sem, value)


def held_value(eng, value):
    return value if isinstance(value, int) else eng.to_reg(value)


class Chain:

    def __init__(self, eng, sem, base=0):
        self.eng, self.sem, self.n = eng, sem, base

    def __call__(self, ins):
        self.n = self.n + 1
        ins.then_inc(self.sem, 1)
        self.eng.wait_ge(self.sem, self.n)


def three_passes(nc, out, a_hi, a_lo, b_hi, b_lo, first, last):
    nc.tensor.matmul(out, a_hi, b_hi, start=first, stop=False)
    nc.tensor.matmul(out, a_lo, b_hi, start=False, stop=False)
    return nc.tensor.matmul(out, a_hi, b_lo, start=False, stop=last)


class Scope:

    def __init__(self, nc, ctx, stage):
        self.nc, self.ctx, self.stage = nc, ctx, stage

    def sb(self, name, shape, dt=F32):
        return self.ctx.enter_context(self.nc.sbuf_tensor(f"{self.stage}_{name}", shape, dt))

    def ps(self, name, shape, dt=F32):
        return self.ctx.enter_context(self.nc.psum_tensor(f"{self.stage}_{name}_ps", shape, dt))

    def sem(self, name):
        return self.ctx.enter_context(self.nc.semaphore(f"{self.stage}_{name}"))

    def sems(self, name, n):
        return [self.sem(f"{name}{i}") for i in range(n)]


class SplitWeights:

    def __init__(self, nc, ctx, w_in):
        m = Scope(nc, ctx, "w_in")
        self.nc = nc
        self.QT, self.SL = 4, KC // 4
        self.raw = m.sb("raw", [P, 2, self.SL, NW])
        self.hi = m.sb("hi", [P, 2, KC, NW], F32R)
        self.lo = m.sb("lo", [P, 2, KC, NW], F32R)
        self.loaded = m.sems("loaded", 2)
        self.hi_done, self.lo_done = m.sem("hi_done"), m.sem("lo_done")
        self.rows = w_in[0].rearrange("(k p) n -> p k n", p=P)

    def load(self, sp, c, q, col):
        wait(sp, self.lo_done, c * self.QT + q - 1)
        sp.dma_start(self.raw[:, q % 2], self.rows[:, q * self.SL:(q + 1) * self.SL, bass.ds(col, NW)]
                     ).then_inc(self.loaded[q % 2], 16)

    def upper(self, act, c, q):
        act.wait_ge(self.loaded[q % 2], c * 32 + 16 * (q // 2 + 1))
        self.nc.scalar.copy(self.hi[:, c % 2, q * self.SL:(q + 1) * self.SL, :], self.raw[:, q % 2]
                            ).then_inc(self.hi_done, 1)

    def lower(self, eng, c, q):
        eng.wait_ge(self.hi_done, c * self.QT + q + 1)
        eng.tensor_tensor(self.lo[:, c % 2, q * self.SL:(q + 1) * self.SL, :], self.raw[:, q % 2],
                          self.hi[:, c % 2, q * self.SL:(q + 1) * self.SL, :].bitcast(F32),
                          ALU.subtract).then_inc(self.lo_done, 1)


def norm_and_first_chunk(nc, x, norm1_g, consts, w, h_hi, h_lo, gates_dram):
    with ExitStack() as ctx:
        m = Scope(nc, ctx, "norm")
        xs = m.sb("x", [P, TT, D])
        g = m.sb("g", [P, D])
        ident = m.sb("ident", [P, P])
        squares = m.sb("squares", [P, D])
        ssq = m.sb("ssq", [P, TT])
        var = m.sb("var", [P, TT])
        dev = m.sb("dev", [P, TT])
        rstd = m.sb("rstd", [P, TT])
        h = m.sb("h", [P, 2, D])
        turned = [m.ps(f"turned{b}", [P, KC, P]) for b in range(2)]
        acc = [m.ps(f"acc{b}", [P, NW]) for b in range(4)]
        staged = m.sb("staged", [P, 2, NW])
        projected, evacuated, stored = m.sem("projected"), m.sem("evacuated"), m.sems("stored", 2)
        x_loaded = m.sems("x_loaded", TT)
        g_loaded, id_loaded = m.sem("g_loaded"), m.sem("id_loaded")
        summed, var_done, dev_done = m.sem("summed"), m.sem("var_done"), m.sem("dev_done")
        rstd_done, scaled = m.sem("rstd_done"), m.sem("scaled")
        transposed, hi_done, lo_done = m.sem("transposed"), m.sem("hi_done"), m.sem("lo_done")
        groups = (0, 2), (2, TT)
        block = ctx.enter_context(nc.Block())

        @block.sync
        def _(sp):
            for t in range(TT):
                sp.dma_start(xs[:, t, :], x[0, t * P:(t + 1) * P, :]).then_inc(x_loaded[t], 16)
                if t == 0:
                    sp.dma_start(ident[:], consts[:, C_ID:C_ID + P]).then_inc(id_loaded, 16)
                    sp.dma_start(g[:], norm1_g[0:1, :].to_broadcast([P, D])).then_inc(g_loaded, 16)
                if t in (1, 3):
                    for q in (t - 1, t):
                        w.load(sp, 0, q, 4 * AW + 3 * NW)
            for q in range(w.QT):
                w.load(sp, 1, q, 3 * AW)

        @block.gpsimd
        def _(pool):
            for q in range(w.QT):
                w.lower(pool, 1, q)

        @block.scalar
        def _(act):
            def sums(b):
                for t in range(*groups[b]):
                    act.wait_ge(x_loaded[t], 16)
                    wait(act, summed, t)
                    nc.scalar.activation(squares[:], xs[:, t, :], ACT.Square,
                                         accum_out=ssq[:, t:t + 1]).then_inc(summed, 1)

            def root(b):
                act.wait_ge(var_done, b + 1)
                r = slice(*groups[b])
                nc.scalar.activation(dev[:, r], var[:, r], ACT.Sqrt).then_inc(dev_done, 1)

            def upper(t):
                act.wait_ge(transposed, t + 1)
                nc.scalar.copy(h_hi[:, :, t * P:(t + 1) * P], turned[t % 2][:]).then_inc(hi_done, 1)

            sums(0)
            root(0)
            def gates(t):
                act.wait_ge(projected, t + 1)
                wait(act, stored[t % 2], 16 * (t // 2))
                nc.scalar.activation(staged[:, t % 2, :], acc[t % 4][:], ACT.Sigmoid).then_inc(evacuated, 1)
                act.wait_ge(evacuated, t + 1)
                act.dma_start(gates_dram[t * P:(t + 1) * P, 3 * NW:4 * NW], staged[:, t % 2, :]
                              ).then_inc(stored[t % 2], 16)

            for t in range(TT):
                if t < 2:
                    w.upper(act, 0, 2 * t)
                    if t == 0:
                        w.upper(act, 0, 1)
                upper(t)
                if t == 1:
                    w.upper(act, 0, 3)
                    sums(1)
                    root(1)
                if 2 <= t < 6:
                    w.upper(act, 1, t - 2)
                if t >= 2:
                    gates(t - 2)
            gates(TT - 2)
            gates(TT - 1)
            for b in range(2):
                act.wait_ge(stored[b], 16 * TT // 2)

        @block.vector
        def _(dve):
            def scale(b):
                r = slice(*groups[b])
                dve.wait_ge(summed, groups[b][1])
                nc.vector.tensor_scalar(var[:, r], ssq[:, r], 1.0 / D, EPS, ALU.mult, ALU.add).then_inc(var_done, 1)
                dve.wait_ge(dev_done, b + 1)
                nc.vector.reciprocal(rstd[:, r], dev[:, r]).then_inc(rstd_done, 1)
                dve.wait_ge(rstd_done, b + 1)

            def apply(t):
                wait(dve, transposed, t - 1)
                nc.vector.scalar_tensor_tensor(out=h[:, t % 2, :], in0=xs[:, t, :], scalar=rstd[:, t:t + 1],
                                               in1=g[:], op0=ALU.mult, op1=ALU.mult).then_inc(scaled, 1)

            def lower(t):
                dve.wait_ge(hi_done, t + 1)
                nc.vector.tensor_tensor(h_lo[:, :, t * P:(t + 1) * P], turned[t % 2][:],
                                        h_hi[:, :, t * P:(t + 1) * P].bitcast(F32),
                                        ALU.subtract).then_inc(lo_done, 1)

            scale(0)
            dve.wait_ge(g_loaded, 16)
            for t in range(TT):
                if t == 2:
                    scale(1)
                apply(t)
                if t >= 1:
                    lower(t - 1)
                if t < 2:
                    w.lower(dve, 0, 2 * t)
                    w.lower(dve, 0, 2 * t + 1)
            lower(TT - 1)

        @block.tensor
        def _(pe):
            def products(t):
                pe.wait_ge(lo_done, t + 1)
                wait(pe, evacuated, t - 3)
                toks = slice(t * P, (t + 1) * P)
                for k in range(KC):
                    if t == 0 and k % w.SL == 0:
                        pe.wait_ge(w.lo_done, k // w.SL + 1)
                    last = three_passes(nc, acc[t % 4][:], h_hi[:, k, toks], h_lo[:, k, toks],
                                        w.hi[:, 0, k, :], w.lo[:, 0, k, :], k == 0, k == KC - 1)
                last.then_inc(projected, 1)

            pe.wait_ge(id_loaded, 16)
            for t in range(TT):
                pe.wait_ge(scaled, t + 1)
                wait(pe, lo_done, t - 1)
                for k in range(KC):
                    last = nc.tensor.transpose(turned[t % 2][:, k, :], h[:, t % 2, k * P:(k + 1) * P], ident[:])
                last.then_inc(transposed, 1)
                if t >= 1:
                    products(t - 1)
            products(TT - 1)


def project(nc, w, h_hi, h_lo, qkv, rqk, u_dram, gates_dram):
    with ExitStack() as ctx:
        m = Scope(nc, ctx, "proj")
        CH = 7
        QT, SL, w_hi, w_lo = w.QT, w.SL, w.hi, w.lo
        staged = m.sb("staged", [P, 2, NW])
        sq = m.sb("sq", [P, 4 * AW])
        ssq = m.sb("ssq", [P, 2 * TT * NH])
        var = m.sb("var", [P, 2 * TT * NH])
        dev = m.sb("dev", [P, 2 * TT * NH])
        acc = [m.ps(f"acc{b}", [P, NW]) for b in range(4)]
        projected, evacuated = m.sem("projected"), m.sem("evacuated")
        stored = m.sems("stored", 2)
        var_done, dev_done, chain = m.sem("var_done"), m.sem("dev_done"), m.sem("chain")
        block = ctx.enter_context(nc.Block())

        @block.sync
        def _(sp):
            def load(c, col):
                for q in range(QT):
                    w.load(sp, c + 1, q, col)

            with sp.Fori(1, 4) as c:
                load(c, c * NW - NW)
            with sp.Fori(4, CH) as c:
                load(c, c * NW)

        @block.scalar
        def _(act):
            def upper(c, q):
                if not isinstance(c, int) or c >= 2:
                    act.wait_ge(projected, c * 8 - 8)
                w.upper(act, c + 1, q)

            def to_dram(c, t, dst, func, n):
                act.wait_ge(projected, c * 8 + t + 1)
                wait(act, stored[t % 2], n * 16)
                nc.scalar.activation(staged[:, t % 2, :], acc[t % 4][:], func).then_inc(evacuated, 1)
                act.wait_ge(evacuated, c * 8 + t + 1)
                act.dma_start(dst, staged[:, t % 2, :]).then_inc(stored[t % 2], 16)

            def split_next(c, t):
                if t % 2:
                    upper(c + 1, t // 2)

            def gate_chunk(c, more):
                for t in range(TT):
                    to_dram(c, t, gates_dram[t * P:(t + 1) * P, bass.ds(c * NW - 4 * NW, NW)],
                            ACT.Sigmoid, c * 4 - 12 + t // 2)
                    if more:
                        split_next(c, t)

            for t in range(TT):
                g, half = divmod(t, 2)
                to_dram(0, t, u_dram[g, :, half * NW:(half + 1) * NW], ACT.Copy, t // 2)
                if t % 2:
                    upper(1, t // 2)
            with act.Fori(1, 4) as c:
                for t in range(TT):
                    act.wait_ge(projected, c * 8 + t + 1)
                    nc.scalar.copy(qkv[:, c - 1, t, :], acc[t % 4][:]).then_inc(evacuated, 1)
                    split_next(c, t)
            with act.Fori(4, CH - 1) as c:
                gate_chunk(c, True)
            act.wait_ge(var_done, 1)
            nc.scalar.activation(dev[:], var[:], ACT.Sqrt).then_inc(dev_done, 1)
            gate_chunk(CH - 1, False)
            for b in range(2):
                act.wait_ge(stored[b], 16 * TT // 2 * (CH - 3))

        @block.vector
        def _(dve):
            link = Chain(dve, chain)

            with dve.Fori(1, 5) as c:
                for q in range(QT):
                    w.lower(dve, c + 1, q)
            dve.wait_ge(evacuated, 8 * 3)
            for s in range(2):
                for b in range(2):
                    half = qkv[:, s, b * 4:(b + 1) * 4, :].rearrange("p t n -> p (t n)")
                    link(nc.vector.tensor_tensor(sq[:], half, half, ALU.mult))
                    at = (s * 2 + b) * 4 * NH
                    link(nc.vector.tensor_reduce(ssq[:, at:at + 4 * NH], sq[:].rearrange("p (a e) -> p a e", e=HD),
                                                 AX_X, ALU.add))
            nc.vector.tensor_scalar(var[:], ssq[:], 1.0 / HD, EPS, ALU.mult, ALU.add).then_inc(var_done, 1)
            with dve.Fori(5, CH) as c:
                for q in range(QT):
                    w.lower(dve, c + 1, q)
            dve.wait_ge(dev_done, 1)
            link(nc.vector.reciprocal(rqk[:].rearrange("p a b c -> p (a b c)"), dev[:]))

        @block.tensor
        def _(pe):
            def columns_first():
                for t in range(8):
                    g, half = divmod(t, 2)
                    wait(pe, evacuated, t - 3)
                    for k in range(KC):
                        if t == 0 and k % SL == 0:
                            pe.wait_ge(w.lo_done, QT + k // SL + 1)
                        cols, toks = slice(g * P, (g + 1) * P), slice(half * NW, (half + 1) * NW)
                        last = three_passes(nc, acc[t % 4][:], w_hi[:, 1, k, cols], w_lo[:, 1, k, cols],
                                            h_hi[:, k, toks], h_lo[:, k, toks], k == 0, k == KC - 1)
                    last.then_inc(projected, 1)

            def tokens_first(c):
                for t in range(TT):
                    pe.wait_ge(evacuated, c * 8 + t - 3)
                    toks = slice(t * P, (t + 1) * P)
                    for k in range(KC):
                        if t == 0 and k % SL == 0:
                            pe.wait_ge(w.lo_done, c * QT + QT + k // SL + 1)
                        last = three_passes(nc, acc[t % 4][:], h_hi[:, k, toks], h_lo[:, k, toks],
                                            w_hi[:, (c + 1) % 2, k, :], w_lo[:, (c + 1) % 2, k, :], k == 0, k == KC - 1)
                    last.then_inc(projected, 1)

            columns_first()
            with pe.Fori(1, CH) as c:
                tokens_first(c)


def attend(nc, consts, quarters, q_norm_g, k_norm_g, u_dram, qkv, rqk, attn_hi, attn_lo, pooled):
    with ExitStack() as ctx:
        m = Scope(nc, ctx, "attn")
        PAIRS, IT = NH // 2, 2 * TT
        ORDER = (0, 6, 1, 5, 2, 4, 3, 7)
        TURNS = {IT: [(0, 0)], IT + 1: [(0, 1), (1, 0)], IT + 2: [(1, 1)]}
        ident = m.sb("ident", [P, P])
        log_held = m.sb("log_held", [P, S])
        ratio = m.sb("ratio", [P, PG, PAD])
        norm_g = m.sb("norm_g", [P, 2])
        scale_g = m.sb("scale_g", [P, 2])
        qk_st = m.sb("qk_st", [P, 2, TT, 2, 2, HD])
        v_st = m.sb("v_st", [P, TT, P])
        q_split = m.sb("q_split", [P, 2, S], F32R)
        k_hi = m.sb("k_hi", [P, 2, S], F32R)
        k_lo = m.sb("k_lo", [P, 2, S], F32R)
        masked = m.sb("masked", [P, 2, S])
        negmax = m.sb("negmax", [P, 2])
        prob = m.sb("prob", [P, 2, S])
        den = m.sb("den", [P, 2, 2])
        rden = m.sb("rden", [P, 2, 2])
        heads_out = m.sb("heads_out", [P, 2, P])
        prob_t = m.sb("prob_t", [P, 2, TT, P])
        u = m.sb("u", [P, PG, PAD + S])
        run = m.sb("run", [P, 2, PAD + S])
        score = [m.ps(f"score{b}", [P, S]) for b in range(2)]
        turned = m.ps("turned", [P, TT, P])
        out = [m.ps(f"out{b}", [P, 2, NW // 2]) for b in range(2)]
        c_loaded, g_loaded, u_loaded = m.sem("c_loaded"), m.sem("g_loaded"), m.sem("u_loaded")
        g_scaled, qk_staged, v_staged = m.sem("g_scaled"), m.sem("qk_staged"), m.sem("v_staged")
        qk_turned, qk_hi_done, qk_lo_done = m.sem("qk_turned"), m.sem("qk_hi_done"), m.sem("qk_lo_done")
        scored, maxed, exped = m.sem("scored"), m.sem("maxed"), m.sem("exped")
        p_turned, p_copied = m.sem("p_turned"), m.sem("p_copied")
        rden_done, normed, out_turned = m.sem("rden_done"), m.sem("normed"), m.sem("out_turned")
        summed, hi_done, lo_done = m.sem("summed"), m.sem("hi_done"), m.sem("lo_done")
        padded, pool_chain, windows_done = m.sem("padded"), m.sem("pool_chain"), m.sem("windows_done")
        averaged = m.sem("averaged")
        block = ctx.enter_context(nc.Block())

        @block.sync
        def _(sp):
            sp.dma_start(ident[:], consts[:, C_ID:C_ID + P]).then_inc(c_loaded, 16)
            sp.dma_start(log_held[:], consts[:, C_LOG:C_LOG + S]).then_inc(c_loaded, 16)
            sp.dma_start(ratio[:].rearrange("p g w -> p (g w)"), consts[:, C_CNT:C_CNT + PG * PAD]
                         ).then_inc(c_loaded, 16)
            for i, g in enumerate((q_norm_g, k_norm_g)):
                for a in range(2):
                    sp.dma_start(norm_g[a * HD:(a + 1) * HD, i:i + 1], g[0].unsqueeze(1)).then_inc(g_loaded, 16)
            sp.wait_ge(padded, 1)
            sp.dma_start(u[:, :, PAD:], u_dram.rearrange("g p s -> p g s")).then_inc(u_loaded, 16)
            for q in (0, 1):
                quarters.load(sp, q)

        @block.gpsimd
        def _(pool):
            link = Chain(pool, pool_chain)
            nc.gpsimd.memset(u[:], 0.0).then_inc(padded, 1)
            link(nc.gpsimd.memset(run[:], 0.0))

            def stage_v(hp):
                wait(pool, summed, hp * IT)
                nc.gpsimd.tensor_copy(v_st[:], qkv[:, 2, :, bass.ds(hp * P, P)]).then_inc(v_staged, 1)

            stage_v(0)
            pool.wait_ge(u_loaded, 16)
            for g, w in enumerate(WIN):
                src = u[:, g]
                for step in range(g + 1):
                    s = 1 << step
                    dst = pooled[:, g] if step == g else run[:, step % 2, PAD:]
                    link(nc.gpsimd.tensor_tensor(dst, src[:, PAD:], src[:, PAD - s:PAD + S - s], ALU.add))
                    src = run[:, step % 2]
                ins = nc.gpsimd.tensor_tensor(pooled[:, g, 0:PAD], pooled[:, g, 0:PAD], ratio[:, g], ALU.mult)
                ins.then_inc(windows_done, 1)
            with pool.Fori(1, PAIRS) as hp:
                stage_v(hp)

        @block.vector
        def _(dve):
            def scale_norms():
                dve.wait_ge(g_loaded, 64)
                nc.vector.tensor_scalar(scale_g[:, 0:1], norm_g[:, 0:1], HD ** -0.5, None, ALU.mult).then_inc(g_scaled, 1)
                nc.vector.tensor_copy(scale_g[:, 1:2], norm_g[:, 1:2]).then_inc(g_scaled, 1)

            def stage_qk(hp, s, twice):
                wait(dve, qk_turned, hp * 8)
                nc.vector.tensor_tensor(
                    qk_st[:, s, :, :, twice],
                    qkv[:, s, :, bass.ds(hp * P, P)].rearrange("p t (a e) -> p t a e", a=2),
                    rqk[:, s, :, bass.ds(hp * 2, 2)].unsqueeze(3).to_broadcast([P, TT, 2, HD]),
                    ALU.mult).then_inc(qk_staged, 1)

            def qk_lower(hp, a, s):
                low = slice(HD, P) if s == 0 else slice(0, P)
                hi, lo = (q_split, q_split) if s == 0 else (k_hi, k_lo)
                for half in range(2):
                    cols = slice(half * NW, (half + 1) * NW)
                    dve.wait_ge(qk_hi_done, hp * 8 + a * 4 + s * 2 + half + 1)
                    nc.vector.scalar_tensor_tensor(
                        out=lo[low, a, cols], in0=score[s][low, cols], scalar=scale_g[low, s:s + 1],
                        in1=hi[low, a, cols].bitcast(F32), op0=ALU.mult, op1=ALU.subtract).then_inc(qk_lo_done, 1)

            def mask_and_max(hp, i):
                b, n = i % 2, (ORDER[i // 2] + 1) * P
                scores_due, exps_due = held_value(dve, hp * IT + i + 1), held_value(dve, hp * IT + max(i - 1, 0))
                dve.wait_ge(c_loaded, 48)
                dve.wait_ge(scored, scores_due)
                wait(dve, exped, exps_due)
                nc.vector.tensor_tensor_reduce(
                    out=masked[:, b, 0:n], in0=score[b][:, 0:n], in1=log_held[:, S - n:S], scale=-1.0,
                    scalar=3e38, op0=ALU.add, op1=ALU.min, accum_out=negmax[:, b:b + 1]).then_inc(maxed, 1)

            def invert(hp, t):
                dve.wait_ge(exped, hp * IT + 2 * t + 2)
                wait(dve, normed, hp * TT + max(t - 1, 0))
                nc.vector.reciprocal(rden[:, t % 2], den[:, t % 2]).then_inc(rden_done, 1)

            def normalise(hp, t):
                dve.wait_ge(rden_done, hp * TT + t + 1)
                dve.wait_ge(summed, hp * IT + 2 * t + 2)
                wait(dve, out_turned, hp * TT + max(t - 1, 0))
                nc.vector.tensor_tensor(
                    heads_out[:, t % 2, :].rearrange("p (a e) -> p a e", a=2),
                    out[t % 2][:, 0, 0:P].rearrange("p (a e) -> p a e", a=2),
                    rden[:, t % 2].unsqueeze(2).to_broadcast([P, 2, HD]), ALU.mult).then_inc(normed, 1)

            def lower(hp, t):
                dve.wait_ge(hi_done, hp * TT + t + 1)
                at = (slice(None), hp, slice(ORDER[t] * P, (ORDER[t] + 1) * P))
                nc.vector.tensor_tensor(attn_lo[at], out[t % 2][:, 1, 0:P], attn_hi[at].bitcast(F32),
                                        ALU.subtract).then_inc(lo_done, 1)

            def average(g):
                dve.wait_ge(windows_done, g + 1)
                nc.vector.scalar_tensor_tensor(out=pooled[:, g], in0=pooled[:, g], scalar=1.0 / WIN[g],
                                               in1=u[:, g, PAD:], op0=ALU.mult, op1=ALU.subtract).then_inc(averaged, 1)

            def pair(hp, more):
                for i in range(IT + 3):
                    if i < IT:
                        mask_and_max(hp, i)
                    if i % 2 == 0 and 2 <= i <= IT:
                        invert(hp, i // 2 - 1)
                    if i % 2 == 0 and i >= 6:
                        lower(hp, i // 2 - 3)
                    if i % 2 == 0 and i >= 4:
                        normalise(hp, i // 2 - 2)
                    if more and i in (7, 9, 11, 13):
                        stage_qk(hp + 1, (i - 7) // 4, (i - 7) // 2 % 2)
                    if not more and i in (7, 9, 11, 13):
                        average((i - 7) // 2)
                    if more:
                        for a, s in TURNS.get(i, []):
                            qk_lower(hp + 1, a, s)
                lower(hp, TT - 1)

            for s in range(2):
                for twice in range(2):
                    stage_qk(0, s, twice)
            scale_norms()
            dve.wait_ge(g_scaled, 2)
            dve.wait_ge(c_loaded, 48)
            for a in range(2):
                for s in range(2):
                    qk_lower(0, a, s)
            pair(0, True)
            with dve.Fori(1, PAIRS - 1) as hp:
                pair(hp, True)
            pair(PAIRS - 1, False)

        @block.scalar
        def _(act):
            def qk_upper(hp, a, s):
                for half in range(2):
                    cols = slice(half * NW, (half + 1) * NW)
                    act.wait_ge(qk_turned, hp * 8 + a * 4 + s * 2 + half + 1)
                    nc.scalar.activation((q_split, k_hi)[s][:, a, cols], score[s][:, cols], ACT.Copy,
                                         scale=scale_g[:, s:s + 1]).then_inc(qk_hi_done, 1)

            def exponent(hp, i):
                b, n = i % 2, (ORDER[i // 2] + 1) * P
                act.wait_ge(maxed, hp * IT + i + 1)
                wait(act, p_turned, hp * IT + max(i - 1, 0))
                nc.scalar.activation(prob[:, b, 0:n], masked[:, b, 0:n], ACT.Exp, bias=negmax[:, b:b + 1], scale=-1.0,
                                     accum_out=den[:, i // 2 % 2, b:b + 1]).then_inc(exped, 1)

            def copy_prob(hp, i):
                b, j = i % 2, ORDER[i // 2] + 1
                act.wait_ge(p_turned, hp * IT + i + 1)
                wait(act, summed, hp * IT + max(i - 1, 0))
                nc.scalar.copy(prob_t[:, b, 0:j, :], turned[:, 0:j, :]).then_inc(p_copied, 1)

            def upper(hp, t):
                act.wait_ge(out_turned, hp * TT + t + 1)
                nc.scalar.copy(attn_hi[:, hp, ORDER[t] * P:(ORDER[t] + 1) * P], out[t % 2][:, 1, 0:P]
                               ).then_inc(hi_done, 1)

            def pair(hp, more):
                for i in range(IT + 3):
                    if i < IT:
                        exponent(hp, i)
                    if i % 2 and i >= 5:
                        upper(hp, (i - 5) // 2)
                    if 1 <= i <= IT:
                        copy_prob(hp, i - 1)
                    if more:
                        for a, s in TURNS.get(i, []):
                            qk_upper(hp + 1, a, s)
                upper(hp, TT - 1)

            act.wait_ge(g_scaled, 2)
            for a in range(2):
                for s in range(2):
                    qk_upper(0, a, s)
            pair(0, True)
            with act.Fori(1, PAIRS - 1) as hp:
                pair(hp, True)
            pair(PAIRS - 1, False)

        @block.tensor
        def _(pe):
            def turn_qk(hp, a, s):
                pe.wait_ge(qk_staged, hp * 4 + s * 2 + 2)
                if not a:
                    wait(pe, maxed, hp * IT - 1 + s if not isinstance(hp, int) or hp else 0)
                for t in range(TT):
                    half = t // (TT // 2)
                    if a and t % (TT // 2) == 0:
                        pe.wait_ge(qk_lo_done, hp * 8 + s * 2 + half + 1)
                    last = nc.tensor.transpose(score[s][:, t * P:(t + 1) * P],
                                               qk_st[:, s, t, a].rearrange("p two e -> p (two e)"), ident[:])
                    if t % (TT // 2) == TT // 2 - 1:
                        last.then_inc(qk_turned, 1)

            def scores(hp, i):
                t, a = ORDER[i // 2], i % 2
                n = (t + 1) * P
                if i < 2:
                    pe.wait_ge(qk_lo_done, hp * 8 + 2 * i + 6)
                else:
                    pe.wait_ge(maxed, hp * IT + i - 1)
                for c in range(0, n, NW):
                    w = min(NW, n - c)
                    for k, first in ((k_hi, True), (k_lo, False)):
                        last = nc.tensor.matmul(score[i % 2][:, c:c + w], q_split[:, a, t * P:(t + 1) * P],
                                                k[:, a, c:c + w], start=first, stop=not first)
                last.then_inc(scored, 1)

            def turn_prob(hp, i):
                pe.wait_ge(exped, hp * IT + i + 1)
                wait(pe, p_copied, hp * IT + i)
                for j in range(ORDER[i // 2] + 1):
                    last = nc.tensor.transpose(turned[:, j, :], prob[:, i % 2, j * P:(j + 1) * P], ident[:])
                last.then_inc(p_turned, 1)

            def weigh(hp, i):
                t, a = divmod(i, 2)
                h = slice(a * HD, (a + 1) * HD)
                pe.wait_ge(p_copied, hp * IT + i + 1)
                if a == 0:
                    wait(pe, lo_done, hp * TT + max(t - 1, 0))
                if i == 0:
                    pe.wait_ge(v_staged, hp + 1)
                for j in range(ORDER[t] + 1):
                    last = nc.tensor.matmul(out[t % 2][:, 0, h], prob_t[:, i % 2, j, :], v_st[:, j, h],
                                            start=(j == 0), stop=(j == ORDER[t]))
                last.then_inc(summed, 1)

            def turn_out(hp, t):
                pe.wait_ge(normed, hp * TT + t + 1)
                nc.tensor.transpose(out[t % 2][:, 1, 0:P], heads_out[:, t % 2, :], ident[:]).then_inc(out_turned, 1)

            def pair(hp, more):
                for i in range(IT + 3):
                    if i < IT:
                        scores(hp, i)
                    if 2 <= i < IT + 2:
                        turn_prob(hp, i - 2)
                    if i % 2 and i >= 5:
                        turn_out(hp, (i - 5) // 2)
                    if i >= 3:
                        weigh(hp, i - 3)
                    if more:
                        for a, s in TURNS.get(i, []):
                            turn_qk(hp + 1, a, s)
                turn_out(hp, TT - 1)

            pe.wait_ge(c_loaded, 48)
            for a in range(2):
                for s in range(2):
                    turn_qk(0, a, s)
            pair(0, True)
            with pe.Fori(1, PAIRS - 1) as hp:
                pair(hp, True)
            pair(PAIRS - 1, False)


class Quarters:

    SL = 2

    def __init__(self, nc, ctx, w_attn_out, w_pool_out, w_o):
        m = Scope(nc, ctx, "quarters")
        self.nc = nc
        self.raw = ctx.enter_context(nc.sbuf_tensor("quarters_raw", [P, 2, self.SL, NW], F32, side="right"))
        self.loaded = m.sems("loaded", 2)
        self.hi_done, self.lo_done = m.sem("hi_done"), m.sem("lo_done")
        a, p, o = (w[0].rearrange("(q k p) (c n) -> c q p k n", p=P, k=self.SL, n=NW)
                   for w in (w_attn_out, w_pool_out, w_o))
        self.sources = [src for c in range(2) for src in (a[c, 0], a[c, 1], p[c, 0], p[c, 1])]
        self.sources += [o[c, q] for c in range(2) for q in range(4)]

    def load(self, sp, n):
        wait(sp, self.lo_done, n - 1)
        sp.dma_start(self.raw[:, n % 2], self.sources[n]).then_inc(self.loaded[n % 2], 16)

    def upper(self, act, n, w_hi):
        act.wait_ge(self.loaded[n % 2], 16 * (n // 2 + 1))
        self.nc.scalar.copy(w_hi, self.raw[:, n % 2]).then_inc(self.hi_done, 1)

    def lower(self, dve, n, w_hi, w_lo):
        dve.wait_ge(self.hi_done, n + 1)
        self.nc.vector.tensor_tensor(w_lo, self.raw[:, n % 2], w_hi.bitcast(F32), ALU.subtract
                                     ).then_inc(self.lo_done, 1)


def merge(nc, consts, quarters, gates_dram, w_pool_mix, pool_scale, attn_hi, attn_lo, pooled,
          pool_hi, pool_lo, mt_hi, mt_lo):
    with ExitStack() as ctx:
        m = Scope(nc, ctx, "merge")
        QT, SL, BK = 4, 2, AW // P
        ident = m.sb("ident", [P, P])
        w_hi = m.sb("w_hi", [P, 2 * BK, NW], F32R)
        w_lo = m.sb("w_lo", [P, 2 * BK, NW], F32R)
        gate = m.sb("gate", [P, 2, 2, NW])
        part = m.sb("part", [P, 2, NW])
        merged = m.sb("merged", [P, 2, NW])
        acc = [[m.ps(f"acc{b}{s}", [P, NW]) for s in range(2)] for b in range(2)]
        turned = [m.ps(f"turned{b}", [P, NW // P, P]) for b in range(2)]
        mix = m.sb("mix", [P, PG, P])
        pscale = m.sb("pscale", [P, PG])
        mixed_ps = [*(m.ps(f"mixed{b}", [P, NW]) for b in range(2)), *acc[1]]
        mix_loaded, mixed, mix_hi, mix_lo = m.sem("mix_loaded"), m.sem("mixed"), m.sem("mix_hi"), m.sem("mix_lo")
        id_loaded = m.sem("id_loaded")
        gate_loaded = m.sems("gate_loaded", 2)
        attn_done, pool_done, gated, added = m.sem("attn_done"), m.sem("pool_done"), m.sem("gated"), m.sem("added")
        transposed, hi_done, lo_done = m.sem("transposed"), m.sem("hi_done"), m.sem("lo_done")
        block = ctx.enter_context(nc.Block())

        @block.sync
        def _(sp):
            sp.dma_start(mix[:], w_pool_mix[0].rearrange("g c d -> c g d")).then_inc(mix_loaded, 16)

            def gates(n):
                c, t = divmod(n, TT)
                wait(sp, added, n - 1)
                for s in range(2):
                    col = s * D + c * NW
                    sp.dma_start(gate[:, n % 2, s, :], gates_dram[t * P:(t + 1) * P, col:col + NW]
                                 ).then_inc(gate_loaded[n % 2], 16)

            for g in range(PG):
                sp.dma_start(pscale[:, g:g + 1], pool_scale[0, g * P:(g + 1) * P].unsqueeze(1)).then_inc(mix_loaded, 16)
            sp.dma_start(ident[:], consts[:, C_ID:C_ID + P]).then_inc(id_loaded, 16)
            for q in (2, 3):
                quarters.load(sp, q)
            for n in range(2 * TT):
                gates(n)
                if n == 3:
                    for q in (4, 5):
                        quarters.load(sp, q)
                if n == TT:
                    for q in (6, 7):
                        quarters.load(sp, q)
            for q in (8, 9):
                quarters.load(sp, q)

        @block.scalar
        def _(act):
            def w_upper(c, q):
                if c:
                    act.wait_ge((attn_done, pool_done)[q // 2], TT)
                quarters.upper(act, c * QT + q, w_hi[:, q * SL:(q + 1) * SL, :])

            def mix_upper(n):
                g, half = divmod(n, 2)
                act.wait_ge(mixed, n + 1)
                nc.scalar.activation(pool_hi[:, g, half * NW:(half + 1) * NW], mixed_ps[n % 4][:], ACT.Copy,
                                     scale=pscale[:, g:g + 1]).then_inc(mix_hi, 1)

            def upper(n):
                c, t = divmod(n, TT)
                act.wait_ge(transposed, n + 1)
                nc.scalar.copy(mt_hi[:, c * BK:(c + 1) * BK, t * P:(t + 1) * P], turned[n % 2][:]).then_inc(hi_done, 1)

            for c in range(2):
                for q in range(QT):
                    w_upper(c, q)
                    if c == 0 and q in (1, 2):
                        if q == 1:
                            act.wait_ge(mix_loaded, 16 * (1 + PG))
                        for n in range((q - 1) * PG, q * PG):
                            mix_upper(n)
                for t in range(TT):
                    if c * TT + t >= 1:
                        upper(c * TT + t - 1)
            upper(2 * TT - 1)

        @block.vector
        def _(dve):
            def w_lower(c, q):
                quarters.lower(dve, c * QT + q, w_hi[:, q * SL:(q + 1) * SL, :], w_lo[:, q * SL:(q + 1) * SL, :])

            def mix_lower(n):
                g, half = divmod(n, 2)
                dst = (slice(None), g, slice(half * NW, (half + 1) * NW))
                dve.wait_ge(mix_hi, n + 1)
                nc.vector.scalar_tensor_tensor(out=pool_lo[dst], in0=mixed_ps[n % 4][:], scalar=pscale[:, g:g + 1],
                                               in1=pool_hi[dst].bitcast(F32), op0=ALU.mult,
                                               op1=ALU.subtract).then_inc(mix_lo, 1)

            def combine(n):
                b = n % 2
                dve.wait_ge(gate_loaded[b], 32 * (n // 2 + 1))
                dve.wait_ge(attn_done, n + 1)
                nc.vector.tensor_tensor(part[:, 0, :], acc[b][0][:], gate[:, b, 0, :], ALU.mult).then_inc(gated, 1)
                dve.wait_ge(pool_done, n + 1)
                nc.vector.tensor_tensor(part[:, 1, :], acc[b][1][:], gate[:, b, 1, :], ALU.mult).then_inc(gated, 1)
                dve.wait_ge(gated, 2 * n + 2)
                wait(dve, transposed, n - 1)
                nc.vector.tensor_tensor(merged[:, b, :], part[:, 0, :], part[:, 1, :], ALU.add).then_inc(added, 1)
                dve.wait_ge(added, n + 1)

            def lower(n):
                c, t = divmod(n, TT)
                dve.wait_ge(hi_done, n + 1)
                at = (slice(None), slice(c * BK, (c + 1) * BK), slice(t * P, (t + 1) * P))
                nc.vector.tensor_tensor(mt_lo[at], turned[n % 2][:], mt_hi[at].bitcast(F32),
                                        ALU.subtract).then_inc(lo_done, 1)

            for c in range(2):
                for q in range(QT):
                    w_lower(c, q)
                    if c == 0 and q in (1, 2):
                        for n in range((q - 1) * PG, q * PG):
                            mix_lower(n)
                for t in range(TT):
                    n = c * TT + t
                    combine(n)
                    if n >= 1:
                        lower(n - 1)
            lower(2 * TT - 1)

        @block.tensor
        def _(pe):
            def branch(n, s, hi, lo, done):
                c, t = divmod(n, TT)
                toks = slice(t * P, (t + 1) * P)
                for k in range(BK):
                    q = (s * BK + k) // SL
                    if t == 0 and k % SL == 0:
                        pe.wait_ge(quarters.lo_done, c * QT + q + 1)
                    last = three_passes(nc, acc[n % 2][s][:], hi[:, k, toks], lo[:, k, toks],
                                        w_hi[:, s * BK + k, :], w_lo[:, s * BK + k, :], k == 0, k == BK - 1)
                last.then_inc(done, 1)
                return last

            def turn(n):
                pe.wait_ge(added, n + 1)
                wait(pe, lo_done, n - 1)
                for j in range(BK):
                    last = nc.tensor.transpose(turned[n % 2][:, j, :], merged[:, n % 2, j * P:(j + 1) * P], ident[:])
                last.then_inc(transposed, 1)

            def mix_pools():
                pe.wait_ge(mix_loaded, 16 * (1 + PG))
                for n in range(2 * PG):
                    g, half = divmod(n, 2)
                    wait(pe, mix_lo, n - 3)
                    nc.tensor.matmul(mixed_ps[n % 4][:], mix[:, g, :], pooled[:, g, half * NW:(half + 1) * NW],
                                     start=True, stop=True).then_inc(mixed, 1)

            for n in range(2 * TT):
                wait(pe, added, n - 1)
                branch(n, 0, attn_hi, attn_lo, attn_done)
                if n == 0:
                    mix_pools()
                    pe.wait_ge(mix_lo, 2 * PG)
                    pe.wait_ge(id_loaded, 16)
                branch(n, 1, pool_hi, pool_lo, pool_done)
                if n >= 1:
                    turn(n - 1)
            turn(2 * TT - 1)


def output_and_norm(nc, consts, quarters, x, norm2_g, w_rg, w_re, mt_hi, mt_lo, logits_t, x1_dram, h2_dram,
                    b_rg, b_re, routing):
    with ExitStack() as ctx:
        m = Scope(nc, ctx, "out")
        QT, SL = 4, KC // 4
        ident, tri, ones, iota, small, bias = routing
        w_hi = m.sb("w_hi", [P, 2, KC, NW], F32R)
        w_lo = m.sb("w_lo", [P, 2, KC, NW], F32R)
        xin = m.sb("xin", [P, 2, NW])
        x1 = m.sb("x1", [P, TT, D])
        g = m.sb("g", [P, D])
        squares = m.sb("squares", [P, D])
        ssq, var = m.sb("ssq", [P, TT]), m.sb("var", [P, TT])
        dev, rstd = m.sb("dev", [P, TT]), m.sb("rstd", [P, TT])
        h2 = m.sb("h2", [P, 2, D])
        h2t = m.sb("h2t", [P, 2, KC, P])
        router = m.sb("router", [P, KC, NR])
        acc = [m.ps(f"acc{b}", [P, NW]) for b in range(4)]
        turned = m.ps("turned", [P, KC, P])
        logit = m.ps("logit", [NR, NW])
        next_loaded = m.sem("next_loaded")
        c_loaded, r_loaded = m.sem("c_loaded"), m.sem("r_loaded")
        x_loaded = m.sems("x_loaded", 2)
        FIRST = 2 * QT
        projected, added, squared = m.sem("projected"), m.sem("added"), m.sem("squared")
        var_done, dev_done, rstd_done, normed = m.sem("var_done"), m.sem("dev_done"), m.sem("rstd_done"), m.sem("normed")
        x1_stored, h2_stored = m.sem("x1_stored"), m.sems("h2_stored", 2)
        transposed, t_copied, routed, l_copied = m.sem("transposed"), m.sem("t_copied"), m.sem("routed"), m.sem("l_copied")
        block = ctx.enter_context(nc.Block())

        @block.sync
        def _(sp):
            def store(t):
                sp.wait_ge(added, TT + t + 1)
                sp.dma_start(x1_dram[t * P:(t + 1) * P, :], x1[:, t, :]).then_inc(x1_stored, 16)
                sp.wait_ge(normed, t + 1)
                sp.dma_start(h2_dram[t * P:(t + 1) * P, :], h2[:, t % 2, :]).then_inc(h2_stored[t % 2], 16)

            for q in (2, 3):
                quarters.load(sp, FIRST + q)
            for n in range(2 * TT):
                c, t = divmod(n, TT)
                wait(sp, added, n - 1)
                sp.dma_start(xin[:, n % 2, :], x[0, t * P:(t + 1) * P, c * NW:(c + 1) * NW]
                             ).then_inc(x_loaded[n % 2], 16)
                if n == 0:
                    sp.dma_start(ident[:], consts[:, C_ID:C_ID + P]).then_inc(c_loaded, 16)
                    sp.dma_start(g[:], norm2_g[0:1, :].to_broadcast([P, D])).then_inc(c_loaded, 16)
                    sp.dma_start(router[:, :, 0:NG], w_rg[0].rearrange("(p c) e -> p c e", c=KC)).then_inc(r_loaded, 16)
                    for e in range(NG):
                        sp.dma_start(router[:, :, NG + e * NE:NG + (e + 1) * NE],
                                     w_re[0, e].rearrange("(p c) e -> p c e", c=KC)).then_inc(r_loaded, 16)
                if n % 2 and n < TT:
                    quarters.load(sp, FIRST + QT + n // 2)
                if n == TT:
                    for dst, col in ((tri, C_TRI), (ones, C_ONE), (iota, C_IOTA)):
                        sp.dma_start(dst[:], consts[:, col:col + P]).then_inc(next_loaded, 16)
                    sp.dma_start(small[:], consts[:, C_D4:C_LOG]).then_inc(next_loaded, 16)
                    sp.dma_start(bias[:, 0:NG], b_rg[0:1, :].to_broadcast([P, NG])).then_inc(next_loaded, 16)
                    sp.dma_start(bias[:, NG:NR], b_re.rearrange("a g e -> a (g e)").to_broadcast([P, E])
                                 ).then_inc(next_loaded, 16)
                if c == 1 and t >= 3:
                    store(t - 3)
            for t in range(TT - 3, TT):
                store(t)
            sp.wait_ge(next_loaded, 16 * 6)
            sp.wait_ge(x1_stored, 16 * TT)
            for b in range(2):
                sp.wait_ge(h2_stored[b], 16 * TT // 2)

        @block.scalar
        def _(act):
            def square(t):
                act.wait_ge(added, TT + t + 1)
                wait(act, squared, t)
                nc.scalar.activation(squares[:], x1[:, t, :], ACT.Square, accum_out=ssq[:, t:t + 1]).then_inc(squared, 1)

            def root(t):
                act.wait_ge(var_done, t + 1)
                nc.scalar.activation(dev[:, t:t + 1], var[:, t:t + 1], ACT.Sqrt).then_inc(dev_done, 1)

            def copy_turned(t):
                act.wait_ge(transposed, t + 1)
                wait(act, routed, t - 1)
                nc.scalar.copy(h2t[:, t % 2], turned[:]).then_inc(t_copied, 1)

            def copy_logits(t):
                act.wait_ge(routed, t + 1)
                nc.scalar.copy(logits_t[0:NR, t * P:(t + 1) * P], logit[:, 0:P]).then_inc(l_copied, 1)

            for c in range(2):
                for q in range(QT):
                    quarters.upper(act, FIRST + c * QT + q, w_hi[:, c, q * SL:(q + 1) * SL, :])
            for t in range(TT + 3):
                if t < TT:
                    square(t)
                if 1 <= t <= TT:
                    root(t - 1)
                if 2 <= t < TT + 2:
                    copy_turned(t - 2)
                if t >= 3:
                    copy_logits(t - 3)

        @block.vector
        def _(dve):
            def w_lower(c, q):
                quarters.lower(dve, FIRST + c * QT + q, w_hi[:, c, q * SL:(q + 1) * SL, :],
                               w_lo[:, c, q * SL:(q + 1) * SL, :])

            def add(n):
                c, t = divmod(n, TT)
                dve.wait_ge(x_loaded[n % 2], 16 * (n // 2 + 1))
                dve.wait_ge(projected, n + 1)
                nc.vector.tensor_tensor(x1[:, t, c * NW:(c + 1) * NW], acc[n % 4][:], xin[:, n % 2, :],
                                        ALU.add).then_inc(added, 1)

            def norm(t):
                at = slice(t, t + 1)
                dve.wait_ge(squared, t + 1)
                nc.vector.tensor_scalar(var[:, at], ssq[:, at], 1.0 / D, EPS, ALU.mult, ALU.add).then_inc(var_done, 1)
                dve.wait_ge(dev_done, t + 1)
                nc.vector.reciprocal(rstd[:, at], dev[:, at]).then_inc(rstd_done, 1)
                dve.wait_ge(rstd_done, t + 1)
                wait(dve, transposed, t - 1)
                wait(dve, h2_stored[t % 2], 16 * (t // 2))
                nc.vector.scalar_tensor_tensor(
                    out=h2[:, t % 2, :].rearrange("q (c p) -> q p c", c=KC), in0=x1[:, t, :].rearrange("q (p c) -> q p c", c=KC),
                    scalar=rstd[:, at], in1=g[:].rearrange("q (p c) -> q p c", c=KC), op0=ALU.mult, op1=ALU.mult
                ).then_inc(normed, 1)

            for q in range(QT):
                w_lower(0, q)
            dve.wait_ge(c_loaded, 32)
            for n in range(2 * TT):
                add(n)
                if n % 2 and n < TT:
                    w_lower(1, n // 2)
                if n > TT:
                    norm(n - TT - 1)
            norm(TT - 1)

        @block.tensor
        def _(pe):
            def products(n):
                c, t = divmod(n, TT)
                toks = slice(t * P, (t + 1) * P)
                wait(pe, added, n - 3)
                for k in range(KC):
                    if t == 0 and k % SL == 0:
                        pe.wait_ge(quarters.lo_done, FIRST + c * QT + k // SL + 1)
                    last = three_passes(nc, acc[n % 4][:], mt_hi[:, k, toks], mt_lo[:, k, toks],
                                        w_hi[:, c, k, :], w_lo[:, c, k, :], k == 0, k == KC - 1)
                last.then_inc(projected, 1)

            def turn(t):
                pe.wait_ge(normed, t + 1)
                wait(pe, t_copied, t)
                for k in range(KC):
                    last = nc.tensor.transpose(turned[:, k, :], h2[:, t % 2, k * P:(k + 1) * P], ident[:])
                last.then_inc(transposed, 1)

            def route(t):
                pe.wait_ge(t_copied, t + 1)
                wait(pe, l_copied, t)
                for k in range(KC):
                    last = nc.tensor.matmul(logit[:, 0:P], router[:, k, :], h2t[:, t % 2, k, :],
                                            start=(k == 0), stop=(k == KC - 1))
                last.then_inc(routed, 1)

            for n in range(2 * TT + 3):
                t = n - TT
                if n < 2 * TT:
                    products(n)
                if n == TT:
                    pe.wait_ge(c_loaded, 32)
                    pe.wait_ge(r_loaded, 16 * (1 + NG))
                if 2 <= t < TT + 2:
                    turn(t - 2)
                if t >= 3:
                    route(t - 3)


class ExpertBlocks:

    HALF = D * FH // P // 2

    def __init__(self, nc, m, soft, w_gate, w_up, w_down, h2_dram, y_dram, row_idx, y_idx, ident, raw, slots, first, psum):
        self.first = first
        self.nc, self.slots, self.row_idx, self.y_idx, self.ident = nc, slots, row_idx, y_idx, ident
        self.h2_dram, self.y_dram = h2_dram, y_dram
        self.w = (w_gate, w_up, w_down)
        self.raw = raw
        self.w_hi = m.sb("w_hi", [P, 6, self.HALF], F32R)
        self.w_lo = m.sb("w_lo", [P, 6, self.HALF], F32R)
        self.rows = m.sb("rows", [P, slots, D])
        self.row_of = [m.sb(f"row_of{b}", [P, 1], U32) for b in range(slots)]
        self.y_row_of = [m.sb(f"y_row_of{b}", [P, 1], U32) for b in range(slots)]
        self.xt_hi = m.sb("xt_hi", [P, slots, KC, P], F32R)
        self.xt_lo = m.sb("xt_lo", [P, slots, KC, P], F32R)
        self.act = m.sb("act", [P, FH])
        self.hid = m.sb("hid", [P, FH])
        self.ht_hi = m.sb("ht_hi", [P, FC, P], F32R)
        self.ht_lo = m.sb("ht_lo", [P, FC, P], F32R)
        self.y = m.sb("y", [P, slots, D])
        self.xt_ps, self.gate_ps, self.up_ps, self.ht_ps, self.y_ps = psum
        self.loaded = m.sems("loaded", 6)
        self.w_hi_done = m.sems("w_hi_done", 6)
        self.w_lo_done = m.sems("w_lo_done", 6)
        self.used = m.sems("used", 6)
        self.rows_cleared, self.row_ready, self.y_row_ready = m.sem("rows_cleared"), m.sem("row_ready"), m.sem("y_row_ready")
        self.gathered = soft.sems(f"{m.stage}_gathered", slots)
        self.stored = soft.sems(f"{m.stage}_stored", slots)
        self.x_turned, self.x_hi_done, self.x_lo_done = m.sem("x_turned"), m.sem("x_hi_done"), m.sem("x_lo_done")
        self.act_done, self.hid_done = m.sem("act_done"), m.sem("hid_done")
        self.h_turned, self.h_hi_done, self.h_lo_done = m.sem("h_turned"), m.sem("h_hi_done"), m.sem("h_lo_done")
        self.y_copied = m.sem("y_copied")

    def counts_of_blocks(self):
        return [*self.w_hi_done, *self.w_lo_done, *self.used, self.row_ready, self.y_row_ready, self.x_turned, self.x_hi_done,
                self.x_lo_done, self.act_done, self.hid_done, self.h_turned, self.h_hi_done, self.h_lo_done,
                self.y_copied]


    def load(self, sp, i, expert, mats):
        for h in [2 * w + j for w in mats for j in range(2)]:
            src = self.w[h // 2][0, expert].rearrange("(p c) n -> p (c n)", p=P)
            wait(sp, self.w_lo_done[h], i)
            sp.dma_start(self.raw[:, h, :], src[:, (h % 2) * self.HALF:(h % 2 + 1) * self.HALF]
                         ).then_inc(self.loaded[h], 16)

    def clear_rows(self, pool):
        self.nc.gpsimd.memset(self.rows[:], 0.0).then_inc(self.rows_cleared, 1)

    def gather(self, pool, i, b, column):
        wait(pool, self.x_turned, i + 1 - self.slots if not isinstance(i, int) or i >= self.slots else 0)
        self.nc.gpsimd.tensor_copy(self.row_of[b][:], self.row_idx[:, bass.ds(column, 1)]).then_inc(self.row_ready, 1)
        rows_due = held_value(pool, i + 1)
        pool.wait_ge(self.rows_cleared, 1)
        pool.wait_ge(self.row_ready, rows_due)
        pool.indirect_dma_start(out=self.rows[:, b, :], out_offset=None, in_=self.h2_dram,
                                in_offset=bass.IndirectOffsetOnAxis(ap=self.row_of[b][:, 0:1], axis=0),
                                bounds_check=S - 1, oob_is_err=False).then_inc(self.gathered[b], 16)

    def store_y(self, pool, i, b, n, column):
        if n is not None:
            wait(pool, self.stored[b], n * 16)
        self.nc.gpsimd.tensor_copy(self.y_row_of[b][:], self.y_idx[:, bass.ds(column, 1)]).then_inc(self.y_row_ready, 1)
        rows_due, copies_due = held_value(pool, i + 1), held_value(pool, i + 1)
        pool.wait_ge(self.rows_cleared, 1)
        pool.wait_ge(self.y_row_ready, rows_due)
        pool.wait_ge(self.y_copied, copies_due)
        pool.indirect_dma_start(out=self.y_dram,
                                out_offset=bass.IndirectOffsetOnAxis(ap=self.y_row_of[b][:, 0:1], axis=0),
                                in_=self.y[:, b, :], in_offset=None, bounds_check=2 * S - 1, oob_is_err=False
                                ).then_inc(self.stored[b], 16)

    def turn_x(self, pe, i, b, n):
        pe.wait_ge(self.gathered[b], n * 16 + 16)
        wait(pe, self.x_lo_done, i)
        for k in range(KC):
            last = self.nc.tensor.transpose(self.xt_ps[:, k, :], self.rows[:, b, k * P:(k + 1) * P], self.ident[:])
        last.then_inc(self.x_turned, 1)

    def x_upper(self, act, i, b):
        act.wait_ge(self.x_turned, i + 1)
        wait(act, self.used[3], i + 1 - self.slots if not isinstance(i, int) or i >= self.slots else 0)
        self.nc.scalar.copy(self.xt_hi[:, b], self.xt_ps[:]).then_inc(self.x_hi_done, 1)

    def x_lower(self, dve, i, b):
        dve.wait_ge(self.x_hi_done, i + 1)
        self.nc.vector.tensor_tensor(self.xt_lo[:, b], self.xt_ps[:], self.xt_hi[:, b].bitcast(F32),
                                     ALU.subtract).then_inc(self.x_lo_done, 1)

    def w_upper(self, act, i, h):
        act.wait_ge(self.loaded[h], (i - self.first) * 16 + 16)
        wait(act, self.used[h], i)
        self.nc.scalar.copy(self.w_hi[:, h, :], self.raw[:, h, :]).then_inc(self.w_hi_done[h], 1)

    def w_lower(self, eng, i, h):
        eng.wait_ge(self.w_hi_done[h], i + 1)
        eng.tensor_tensor(self.w_lo[:, h, :], self.raw[:, h, :], self.w_hi[:, h, :].bitcast(F32),
                                     ALU.subtract).then_inc(self.w_lo_done[h], 1)

    def into_hidden(self, pe, i, b, mat, half):
        if half == 0:
            if mat == 0:
                pe.wait_ge(self.x_lo_done, i + 1)
            wait(pe, (self.act_done, self.hid_done)[mat], i)
        h = 2 * mat + half
        pe.wait_ge(self.w_lo_done[h], i + 1)
        for j in range(KC // 2):
            k = half * (KC // 2) + j
            cols = slice(j * FH, (j + 1) * FH)
            last = three_passes(self.nc, (self.gate_ps, self.up_ps)[mat][:], self.xt_hi[:, b, k], self.xt_lo[:, b, k],
                                self.w_hi[:, h, cols], self.w_lo[:, h, cols], k == 0, k == KC - 1)
        last.then_inc(self.used[h], 1)

    def silu(self, act, i):
        act.wait_ge(self.used[1], i + 1)
        wait(act, self.hid_done, i)
        self.nc.scalar.activation(self.act[:], self.gate_ps[:], ACT.Silu).then_inc(self.act_done, 1)

    def hidden(self, dve, i):
        dve.wait_ge(self.act_done, i + 1)
        dve.wait_ge(self.used[3], i + 1)
        wait(dve, self.h_turned, i)
        self.nc.vector.tensor_tensor(self.hid[:].rearrange("q (c p) -> q p c", c=FC),
                                     self.up_ps[:].rearrange("q (p c) -> q p c", c=FC),
                                     self.act[:].rearrange("q (p c) -> q p c", c=FC), ALU.mult
                                     ).then_inc(self.hid_done, 1)

    def turn_h(self, pe, i):
        pe.wait_ge(self.hid_done, i + 1)
        wait(pe, self.h_lo_done, i)
        for k in range(FC):
            last = self.nc.tensor.transpose(self.ht_ps[:, k, :], self.hid[:, k * P:(k + 1) * P], self.ident[:])
        last.then_inc(self.h_turned, 1)

    def h_upper(self, act, i):
        act.wait_ge(self.h_turned, i + 1)
        wait(act, self.used[5], i)
        self.nc.scalar.copy(self.ht_hi[:], self.ht_ps[:]).then_inc(self.h_hi_done, 1)

    def h_lower(self, dve, i):
        dve.wait_ge(self.h_hi_done, i + 1)
        self.nc.vector.tensor_tensor(self.ht_lo[:], self.ht_ps[:], self.ht_hi[:].bitcast(F32),
                                     ALU.subtract).then_inc(self.h_lo_done, 1)

    def down(self, pe, i):
        pe.wait_ge(self.h_lo_done, i + 1)
        wait(pe, self.y_copied, i)
        for half in range(2):
            h = 4 + half
            pe.wait_ge(self.w_lo_done[h], i + 1)
            for j in range(FC // 2):
                k = half * (FC // 2) + j
                for c in range(D // NW):
                    cols = slice(j * D + c * NW, j * D + (c + 1) * NW)
                    last = three_passes(self.nc, self.y_ps[:, c, :], self.ht_hi[:, k], self.ht_lo[:, k],
                                        self.w_hi[:, h, cols], self.w_lo[:, h, cols], k == 0, k == FC - 1)
            last.then_inc(self.used[h], 1)

    def copy_y(self, act, i, b, n):
        act.wait_ge(self.used[5], i + 1)
        if n is not None:
            wait(act, self.stored[b], n * 16)
        self.nc.scalar.copy(self.y[:, b, :], self.y_ps[:].rearrange("p c n -> p (c n)")).then_inc(self.y_copied, 1)


def x1_into_raw(sp, x, blocks_done, x1_dram, raw, loaded):
    tiles = x1_dram.rearrange("(h t p) d -> h p t d", h=4, p=P)
    for h in range(4):
        sp.wait_ge(x.w_lo_done[h], blocks_done)
        sp.dma_start(raw[:, h, :].rearrange("p (t d) -> p t d", d=D), tiles[h]).then_inc(loaded, 16)
    sp.wait_ge(loaded, 16 * 4)


def psum_of_experts(m):
    return (m.ps("xt", [P, KC, P]), m.ps("gate", [P, FH]), m.ps("up", [P, FH]), m.ps("ht", [P, FC, P]),
            m.ps("y", [P, D // NW, NW]))


def route_and_experts(nc, soft, routing, w_gate, w_up, w_down, logits_t, row_idx, y_idx, gates, over,
                      raw, h2_dram, x1_dram, y_dram):
    with ExitStack() as ctx:
        m = Scope(nc, ctx, "moe")
        ident, tri, ones, iota, small, bias = routing
        logits = m.sb("logits", [P, TT, NR])
        g_max, g_sum, g_gate, g_key = (m.sb(n, [P, TT]) for n in ("g_max", "g_sum", "g_gate", "g_key"))
        g_one, g_exp = m.sb("g_one", [P, TT, NG]), m.sb("g_exp", [P, TT, NG])
        e_all = m.sb("e_all", [P, TT, NG, NE])
        e_logit = m.sb("e_logit", [P, 2, TT, NE])
        e_max, e_key = m.sb("e_max", [P, 2, TT]), m.sb("e_key", [P, 2, TT])
        e_one = m.sb("e_one", [P, 2, TT, NE])
        ratio, total = m.sb("ratio", [P, TT]), m.sb("total", [P, TT])
        chosen = m.sb("chosen", [P, 2, TT, E])
        both = m.sb("both", [P, E, TT])
        same_expert = m.sb("same_expert", [P, E, TT])
        block_row = logits_t[:, 0:TT * NB].bitcast(F16).rearrange("p (k t b) -> p k t b", k=2, t=TT)
        up_to = logits_t[:, TT * NB:TT * NB + E * TT].rearrange("p (e t) -> p e t", e=E)
        before = m.sb("before", [P, E, TT])
        rank_all = m.sb("rank_all", [P, TT, E])
        pick = m.sb("pick", [P, 2, TT, E])
        rank, eid, base, beyond, many = (m.sb(n, [P, 2, TT]) for n in ("rank", "eid", "base", "beyond", "many"))
        column = m.sb("column", [P, 2, TT])
        further = m.sb("further", [P, 2, TT, TT - 1])
        more_than = m.sb("more_than", [P, E, TT - 1])
        to_row = m.sb("to_row", [P, 2, TT])
        vacant, y_row, is_second = (m.sb(n, [P, NB]) for n in ("vacant", "y_row", "is_second"))
        count, more, end, begin = (m.sb(n, [P, E]) for n in ("count", "more", "end", "begin"))
        ended = m.sb("ended", [P, MOST, E])
        over_f = m.sb("over_f", [P, 1 + MOST])
        psum = psum_of_experts(m)
        by_token = psum[3][:].rearrange("p a b -> p (a b)").rearrange("p (t e) -> p t e", t=TT)
        rank_ps = psum[1][:, 0:TT * E].rearrange("p (e t) -> p t e", t=TT)
        count_ps = psum[2][:, 0:E]
        table_ps = psum[4][:, 0, 0:NB]
        l_turned, near, exp_done = m.sem("l_turned"), m.sem("near"), m.sem("exp_done")
        link_sem, chosen_done, ranked = m.sem("link"), m.sem("chosen_done"), m.sem("ranked")
        x1_loaded = m.sem("x1_loaded")
        hot_done, tabled, idx_ready = m.sem("hot_done"), m.sem("tabled"), m.sem("idx_ready")
        x = ExpertBlocks(nc, m, soft, w_gate, w_up, w_down, h2_dram, y_dram, row_idx, y_idx, ident, raw, 2, 0,
                         psum)
        slot_hot = x.y[:, 0, :].bitcast(F16).rearrange("p (k t s) -> p k t s", k=2, t=TT)
        POOL_HALVES = 2
        o = -C_D4
        d4, d8 = small[:, C_D4 + o:C_D8 + o], small[:, C_D8 + o:C_EID + o]
        eids, th, toks = small[:, C_EID + o:C_TH + o], small[:, C_TH + o:C_TOK + o], small[:, C_TOK + o:C_LOG + o]
        block = ctx.enter_context(nc.Block())

        @block.sync
        def _(sp):
            x.load(sp, 0, 0, (0, 1))

            def further(i):
                x.load(sp, i, i, (0,))
                x.load(sp, i - 1, i - 1, (2,))
                x.load(sp, i, i, (1,))

            further(1)
            with sp.Fori(2, E) as i:
                further(i)
            x.load(sp, E - 1, E - 1, (2,))
            x1_into_raw(sp, x, E, x1_dram, raw, x1_loaded)

        @block.gpsimd
        def _(pool):
            x.clear_rows(pool)
            for h in range(POOL_HALVES):
                x.w_lower(pool, 0, h)
            pool.wait_ge(idx_ready, 1)
            x.gather(pool, 0, 0, 0)
            x.gather(pool, 1, 1, 1)
            x.gather(pool, 2, 0, 2)
            x.gather(pool, 3, 1, 3)
            x.store_y(pool, 0, 0, 0, 0)
            x.gather(pool, 4, 0, 4)
            x.store_y(pool, 1, 1, 0, 1)
            x.gather(pool, 5, 1, 5)
            with pool.Fori(1, E // 2 - 2) as j:
                x.store_y(pool, j * 2, 0, j, j * 2)
                x.gather(pool, j * 2 + 4, 0, j * 2 + 4)
                x.store_y(pool, j * 2 + 1, 1, j, j * 2 + 1)
                x.gather(pool, j * 2 + 5, 1, j * 2 + 5)
            for i in range(E - 4, E):
                x.store_y(pool, i, i % 2, i // 2, i)
            for b in range(2):
                pool.wait_ge(x.stored[b], 16 * E // 2)

        @block.scalar
        def _(act):
            def step(i, b, n, first=False, last=False):
                before_1 = n if b else n - 1
                if not first:
                    x.w_upper(act, i - 1, 4)
                    x.h_upper(act, i - 1)
                    x.w_upper(act, i - 1, 5)
                if not first:
                    x.w_upper(act, i, 2)
                x.silu(act, i)
                if not first:
                    x.w_upper(act, i, 3)
                if not last:
                    x.w_upper(act, i + 1, 0)
                if not first:
                    x.copy_y(act, i - 1, 1 - b, before_1)
                if not last:
                    x.x_upper(act, i + 1, 1 - b)
                    x.w_upper(act, i + 1, 1)

            act.wait_ge(near, 1)
            nc.scalar.activation(g_exp[:], g_exp[:], ACT.Exp).then_inc(exp_done, 1)
            act.wait_ge(near, 2)
            nc.scalar.activation(ratio[:], ratio[:], ACT.Exp).then_inc(exp_done, 1)
            for h in range(4):
                x.w_upper(act, 0, h)
            x.x_upper(act, 0, 0)
            step(0, 0, 0, first=True)
            step(1, 1, 0)
            step(2, 0, 1)
            with act.Fori(1, E // 2 - 1) as j:
                step(j * 2 + 1, 1, j)
                step(j * 2 + 2, 0, j + 1)
            step(E - 1, 1, E // 2 - 1, last=True)
            x.w_upper(act, E - 1, 4)
            x.h_upper(act, E - 1)
            x.w_upper(act, E - 1, 5)
            x.copy_y(act, E - 1, 1, E // 2 - 1)

        @block.vector
        def _(dve):
            v = nc.vector
            link = Chain(dve, link_sem)

            def wide(a, n):
                return a.unsqueeze(len(a.shape)).to_broadcast([*a.shape, n])

            def rows(a, *shape):
                for _ in range(len(shape) - 1):
                    a = a.unsqueeze(1)
                return a.to_broadcast([P, *shape])

            def first_of(values, most, key, one, order):
                n = values.shape[-1]
                link(v.tensor_reduce(most, values, AX_X, ALU.max))
                link(v.tensor_tensor(one, values, wide(most, n), ALU.is_equal))
                link(v.tensor_tensor(one, one, rows(order, TT, n), ALU.mult))
                link(v.tensor_reduce(key, one, AX_X, ALU.max))
                link(v.tensor_tensor(one, one, wide(key, n), ALU.is_equal))

            link(v.memset(same_expert[:], 1.0))
            link(v.memset(same_expert[:, :, 0:1], 0.0))
            dve.wait_ge(l_turned, 1)
            link(v.tensor_tensor(logits[:], by_token[:, :, 0:NR], rows(bias[:], TT, NR), ALU.add))
            gl = logits[:, :, 0:NG]
            first_of(gl, g_max[:], g_key[:], g_one[:], d4)
            v.tensor_tensor(g_exp[:], gl, wide(g_max[:], NG), ALU.subtract).then_inc(near, 1)
            link(v.tensor_tensor(e_all[:], logits[:, :, NG:NR].rearrange("p t (g e) -> p t g e", g=NG),
                                 wide(g_one[:], NE), ALU.mult))
            link(v.tensor_reduce(e_logit[:, 0], e_all[:].rearrange("p t g e -> p t e g"), AX_X, ALU.add))
            first_of(e_logit[:, 0], e_max[:, 0], e_key[:, 0], e_one[:, 0], d8)
            link(v.scalar_tensor_tensor(out=e_logit[:, 1], in0=e_one[:, 0], scalar=-3e38, in1=e_logit[:, 0],
                                        op0=ALU.mult, op1=ALU.add))
            first_of(e_logit[:, 1], e_max[:, 1], e_key[:, 1], e_one[:, 1], d8)
            v.tensor_tensor(ratio[:], e_max[:, 1], e_max[:, 0], ALU.subtract).then_inc(near, 1)
            for k in range(2):
                link(v.tensor_tensor(chosen[:, k].rearrange("p t (g e) -> p t g e", g=NG),
                                     e_one[:, k].unsqueeze(2).to_broadcast([P, TT, NG, NE]), wide(g_one[:], NE),
                                     ALU.mult))
            link(v.tensor_tensor(both[:].rearrange("p e t -> p t e"), chosen[:, 0], chosen[:, 1], ALU.add))
            link(v.tensor_tensor_scan(up_to.rearrange("p e t -> p (e t)"),
                                      same_expert[:].rearrange("p e t -> p (e t)"),
                                      both[:].rearrange("p e t -> p (e t)"), 0.0, ALU.mult, ALU.add))
            v.tensor_tensor(before[:], up_to, both[:], ALU.subtract).then_inc(chosen_done, 1)
            for k in range(2):
                link(v.tensor_scalar(to_row[:, k, :], toks, float(k * S + 1), None, ALU.add))
            link(v.tensor_tensor(pick[:], chosen[:], rows(eids, 2, TT, E), ALU.mult))
            link(v.tensor_reduce(eid[:], pick[:], AX_X, ALU.add))
            dve.wait_ge(ranked, 1)
            link(v.tensor_copy(count[:], count_ps))
            link(v.tensor_copy(rank_all[:], rank_ps))
            link(v.scalar_tensor_tensor(out=more_than[:], in0=wide(count[:], TT - 1), scalar=1.0 / P,
                                        in1=rows(th[:, 1:TT], E, TT - 1), op0=ALU.mult, op1=ALU.is_gt))
            link(v.tensor_reduce(more[:], more_than[:], AX_X, ALU.add))
            link(v.tensor_tensor_scan(end[:], ones[:, 0:E], more[:], 0.0, ALU.mult, ALU.add))
            link(v.tensor_tensor(begin[:], end[:], more[:], ALU.subtract))
            for values, result in ((rank_all[:], rank), (rows(begin[:], TT, E), base)):
                for k in range(2):
                    link(v.tensor_tensor(pick[:, k], chosen[:, k], values, ALU.mult))
                link(v.tensor_reduce(result[:], pick[:], AX_X, ALU.add))
            link(v.scalar_tensor_tensor(out=further[:].rearrange("p k t n -> p (k t) n"),
                                        in0=wide(rank[:].rearrange("p k t -> p (k t)"), TT - 1), scalar=1.0 / P,
                                        in1=rows(th[:, 1:TT], 2 * TT, TT - 1), op0=ALU.mult, op1=ALU.is_ge))
            link(v.tensor_reduce(beyond[:], further[:], AX_X, ALU.add))
            link(v.tensor_scalar(many[:], beyond[:], 1.0, None, ALU.min))
            link(v.scalar_tensor_tensor(out=column[:], in0=base[:], scalar=float(E - 1), in1=beyond[:],
                                        op0=ALU.add, op1=ALU.add))
            link(v.tensor_tensor(column[:], column[:], eid[:], ALU.subtract))
            link(v.tensor_tensor(column[:], column[:], many[:], ALU.mult))
            link(v.tensor_tensor(column[:], column[:], eid[:], ALU.add))
            link(v.scalar_tensor_tensor(out=rank[:], in0=beyond[:], scalar=-float(P), in1=rank[:],
                                        op0=ALU.mult, op1=ALU.add))
            for k in range(2):
                v.tensor_tensor(slot_hot[:, k], rows(iota[:], TT, P), wide(rank[:, k], P), ALU.is_equal)
                link(v.tensor_tensor(block_row[:, k], rows(iota[:, 0:NB], TT, NB),
                                     wide(column[:, k], NB), ALU.is_equal))
                v.tensor_tensor(block_row[:, k], block_row[:, k], wide(to_row[:, k], NB),
                                ALU.mult).then_inc(hot_done, 1)
            dve.wait_ge(tabled, 1)
            link(v.tensor_scalar(vacant[:], table_ps, 0.0, float(4 * S), ALU.is_equal, ALU.mult))
            link(v.scalar_tensor_tensor(out=y_row[:], in0=table_ps, scalar=-1.0, in1=vacant[:],
                                        op0=ALU.add, op1=ALU.add))
            link(v.tensor_scalar(is_second[:], y_row[:], float(S), float(-S), ALU.is_ge, ALU.mult))
            link(v.tensor_tensor(row_idx[:], y_row[:], is_second[:], ALU.add))
            v.tensor_copy(y_idx[:], y_row[:]).then_inc(idx_ready, 1)
            dve.wait_ge(exp_done, 2)
            link(v.tensor_reduce(g_sum[:], g_exp[:], AX_X, ALU.add))
            link(v.reciprocal(g_gate[:], g_sum[:]))
            link(v.tensor_scalar(total[:], ratio[:], 1.0, None, ALU.add))
            link(v.reciprocal(total[:], total[:]))
            link(v.tensor_tensor(gates[:, 0, :], g_gate[:], total[:], ALU.mult))
            link(v.tensor_tensor(gates[:, 1, :], gates[:, 0, :], ratio[:], ALU.mult))
            link(v.tensor_tensor(ended[:], rows(end[:], MOST, E), wide(th, E), ALU.is_le))
            link(v.tensor_copy(over_f[:, 0:1], end[:, E - 1:E]))
            link(v.tensor_reduce(over_f[:, 1:], ended[:], AX_X, ALU.add))
            link(v.tensor_scalar(over_f[:, 1:], over_f[:, 1:], float(E - 1), None, ALU.min))
            link(v.tensor_copy(over[:], over_f[:]))

            def step(i, first=False, last=False):
                if not first:
                    x.hidden(dve, i - 1)
                    x.w_lower(dve, i - 1, 4)
                    x.h_lower(dve, i - 1)
                    x.w_lower(dve, i - 1, 5)
                if not first:
                    x.w_lower(dve, i, 2)
                    x.w_lower(dve, i, 3)

            def ahead(i, b):
                x.w_lower(dve, i, 0)
                x.x_lower(dve, i, b)
                x.w_lower(dve, i, 1)

            for h in range(POOL_HALVES, 4):
                x.w_lower(dve, 0, h)
            x.x_lower(dve, 0, 0)
            step(0, first=True)
            ahead(1, 1)
            step(1)
            ahead(2, 0)
            step(2)
            ahead(3, 1)
            with dve.Fori(1, E // 2 - 1) as j:
                step(j * 2 + 1)
                ahead(j * 2 + 2, 0)
                step(j * 2 + 2)
                ahead(j * 2 + 3, 1)
            step(E - 1)
            x.hidden(dve, E - 1)
            x.w_lower(dve, E - 1, 4)
            x.h_lower(dve, E - 1)
            x.w_lower(dve, E - 1, 5)

        @block.tensor
        def _(pe):
            for t in range(TT):
                last = nc.tensor.transpose(by_token[:, t, 0:NR], logits_t[0:NR, t * P:(t + 1) * P],
                                           ident[0:NR, 0:NR])
            last.then_inc(l_turned, 1)
            pe.wait_ge(chosen_done, 1)
            nc.tensor.matmul(psum[1][:, 0:TT * E], tri[:], both[:].rearrange("p e t -> p (e t)"), start=True, stop=False)
            nc.tensor.matmul(psum[1][:, 0:TT * E], ones[:], before[:].rearrange("p e t -> p (e t)"),
                             start=False, stop=True)
            nc.tensor.matmul(count_ps, ones[:], up_to[:, :, TT - 1], start=True, stop=True).then_inc(ranked, 1)
            for k in range(2):
                pe.wait_ge(hot_done, k + 1)
                for t in range(TT):
                    last = nc.tensor.matmul(table_ps, slot_hot[:, k, t, :], block_row[:, k, t, :],
                                            start=(k == 0 and t == 0), stop=(k == 1 and t == TT - 1))
            last.then_inc(tabled, 1)

            def step(i, b, n, first=False, last=False):
                x.into_hidden(pe, i, b, 0, 0)
                if not first:
                    x.turn_h(pe, i - 1)
                x.into_hidden(pe, i, b, 0, 1)
                if not first:
                    x.down(pe, i - 1)
                if not last:
                    x.turn_x(pe, i + 1, 1 - b, n + 1 if b else n)
                x.into_hidden(pe, i, b, 1, 0)
                x.into_hidden(pe, i, b, 1, 1)

            x.turn_x(pe, 0, 0, 0)
            pe.wait_ge(idx_ready, 1)
            step(0, 0, 0, first=True)
            step(1, 1, 0)
            step(2, 0, 1)
            with pe.Fori(1, E // 2 - 1) as j:
                step(j * 2 + 1, 1, j)
                step(j * 2 + 2, 0, j + 1)
            step(E - 1, 1, E // 2 - 1, last=True)
            x.turn_h(pe, E - 1)
            x.down(pe, E - 1)


def blocks_beyond(nc, soft, ident, w_gate, w_up, w_down, row_idx, y_idx, over, raw, h2_dram, x1_dram, y_dram):
    with ExitStack() as ctx:
        m = Scope(nc, ctx, "beyond")
        started = m.sem("started")
        x = ExpertBlocks(nc, m, soft, w_gate, w_up, w_down, h2_dram, y_dram, row_idx, y_idx, ident, raw, 1, 1,
                         psum_of_experts(m))
        x1_loaded = m.sem("x1_loaded")
        block = ctx.enter_context(nc.Block())

        def each(eng, body, after=None):
            n = eng.value_load(over[0:1, 0:1], min_val=0, max_val=MOST - 1)
            with eng.If(n > 0):
                if eng is nc.gpsimd:
                    for s in x.counts_of_blocks():
                        eng.sem_inc(s, 1)
                    eng.sem_inc(started, 1)
                eng.wait_ge(started, 1)
                with eng.Fori(1, n + 1) as i:
                    body(i)
                if after is not None:
                    after(n)

        @block.sync
        def _(sp):
            def body(i):
                expert = sp.value_load(over[0:1, bass.ds(i, 1)], min_val=0, max_val=E - 1)
                x.load(sp, i, expert, (0, 1, 2))

            each(sp, body, lambda n: x1_into_raw(sp, x, n + 1, x1_dram, raw, x1_loaded))

        @block.gpsimd
        def _(pool):
            x.clear_rows(pool)

            def body(i):
                x.gather(pool, i, 0, i + E - 1)
                x.store_y(pool, i, 0, None, i + E - 1)
                pool.wait_ge(x.stored[0], i * 16)

            each(pool, body)

        @block.scalar
        def _(act):
            def body(i):
                x.x_upper(act, i, 0)
                for h in range(4):
                    x.w_upper(act, i, h)
                x.silu(act, i)
                x.w_upper(act, i, 4)
                x.w_upper(act, i, 5)
                x.h_upper(act, i)
                x.copy_y(act, i, 0, None)

            each(act, body)

        @block.vector
        def _(dve):
            def body(i):
                x.x_lower(dve, i, 0)
                for h in range(4):
                    x.w_lower(dve, i, h)
                x.w_lower(dve, i, 4)
                x.w_lower(dve, i, 5)
                x.hidden(dve, i)
                x.h_lower(dve, i)

            each(dve, body)

        @block.tensor
        def _(pe):
            def body(i):
                x.turn_x(pe, i, 0, i - 1)
                for mat in range(2):
                    for half in range(2):
                        x.into_hidden(pe, i, 0, mat, half)
                x.turn_h(pe, i)
                x.down(pe, i)

            each(pe, body)


def clear_released_semaphores(nc):
    ids = sorted(nc.released_uncleared_semaphores)
    first = [i for i in ids if i - 1 not in ids]
    last = [i for i in ids if i + 1 not in ids]
    with nc.Block() as block:
        @block.gpsimd
        def _(pool):
            for a, b in zip(first, last):
                pool.sem_clear(range(a, b + 1))


def combine(nc, gates, raw, y_dram, out):
    with ExitStack() as ctx:
        m = Scope(nc, ctx, "sum")
        x1 = raw[:, 0:4, :].rearrange("p h (t d) -> p (h t) d", d=D)
        y = m.sb("y", [P, TT, 2, D])
        y_loaded = m.sems("y_loaded", TT)
        first, added, stored = m.sem("first"), m.sem("added"), m.sem("stored")
        block = ctx.enter_context(nc.Block())

        @block.sync
        def _(sp):
            y_rows = y_dram.rearrange("(k t p) d -> t p k d", k=2, p=P)
            for t in range(TT):
                sp.dma_start(y[:, t], y_rows[t]).then_inc(y_loaded[t], 16)

        @block.vector
        def _(dve):
            for t in range(TT):
                dve.wait_ge(y_loaded[t], 16)
                for k, done in ((0, first), (1, added)):
                    nc.vector.scalar_tensor_tensor(out=x1[:, t, :], in0=y[:, t, k, :], scalar=gates[:, k, t:t + 1],
                                                   in1=x1[:, t, :], op0=ALU.mult, op1=ALU.add).then_inc(done, 1)
                    if k == 0:
                        dve.wait_ge(first, t + 1)

        @block.scalar
        def _(act):
            for t in range(TT):
                act.wait_ge(added, t + 1)
                act.dma_start(out[0, t * P:(t + 1) * P, :], x1[:, t, :]).then_inc(stored, 16)
            act.wait_ge(stored, 16 * TT)


def decoder_layer(nc, x, norm1_g, w_in, q_norm_g, k_norm_g, w_attn_out, w_pool_mix, pool_scale, w_pool_out, w_o,
                  norm2_g, w_rg, b_rg, w_re, b_re, w_gate, w_up, w_down, consts, out):
    def dram(name, shape, dt=F32):
        return nc.dram_tensor(name, shape, dt).ap()

    u_dram = dram("u_scratch", [PG, P, S])
    gates_dram = dram("gates_scratch", [S, 2 * D])
    x1_dram = dram("x1_scratch", [S, D])
    h2_dram = dram("h2_scratch", [S, D])
    y_dram = dram("y_scratch", [2 * S, D])

    def held(ctx, side, *tensors):
        return [ctx.enter_context(nc.sbuf_tensor(n, s, d, side=side)) for n, s, d in tensors]

    heads, merged, branches, qkv_held, quarters_held = (ExitStack() for _ in range(5))
    with ExitStack() as small:
        soft = Scope(nc, small, "soft")
        h_hi, h_lo = held(heads, "left", ("h_hi", [P, KC, S], F32R), ("h_lo", [P, KC, S], F32R))
        w = SplitWeights(nc, heads, w_in)
        norm_and_first_chunk(nc, x, norm1_g, consts, w, h_hi, h_lo, gates_dram)
        quarters = Quarters(nc, quarters_held, w_attn_out, w_pool_out, w_o)
        qkv, rqk = held(qkv_held, "right", ("qkv", [P, 3, TT, AW], F32), ("rqk", [P, 2, TT, NH], F32))
        project(nc, w, h_hi, h_lo, qkv, rqk, u_dram, gates_dram)
        heads.close()
        attn_hi, attn_lo, pooled = held(branches, "left", ("attn_hi", [P, AW // P, S], F32R),
                                        ("attn_lo", [P, AW // P, S], F32R), ("pooled", [P, PG, S], F32))
        attend(nc, consts, quarters, q_norm_g, k_norm_g, u_dram, qkv, rqk, attn_hi, attn_lo, pooled)
        qkv_held.close()
        pool_hi, pool_lo = held(branches, "left", *((n, [P, PG, S], F32R) for n in ("pool_hi", "pool_lo")))
        mt_hi, mt_lo = held(merged, "right", ("mt_hi", [P, KC, S], F32R), ("mt_lo", [P, KC, S], F32R))
        merge(nc, consts, quarters, gates_dram, w_pool_mix, pool_scale, attn_hi, attn_lo, pooled,
              pool_hi, pool_lo, mt_hi, mt_lo)
        branches.close()
        logits_t, row_idx, y_idx, gates, over = held(
            small, "left", ("logits_t", [P, S], F32), ("row_idx", [P, NB], U32), ("y_idx", [P, NB], U32),
            ("gates", [P, 2, TT], F32), ("over", [P, 1 + MOST], I32))
        routing = held(small, "left", *((n, [P, w], F32) for n, w in (
            ("ident", P), ("tri", P), ("ones", P), ("iota", P), ("small", C_LOG - C_D4), ("bias", NR))))
        output_and_norm(nc, consts, quarters, x, norm2_g, w_rg, w_re, mt_hi, mt_lo, logits_t, x1_dram, h2_dram,
                        b_rg, b_re, routing)
        merged.close()
        quarters_held.close()
        (raw,) = held(small, "left", ("raw", [P, 6, ExpertBlocks.HALF], F32))
        route_and_experts(nc, soft, routing, w_gate, w_up, w_down, logits_t, row_idx, y_idx, gates,
                          over, raw, h2_dram, x1_dram, y_dram)
        clear_released_semaphores(nc)
        blocks_beyond(nc, soft, routing[0], w_gate, w_up, w_down, row_idx, y_idx, over, raw, h2_dram, x1_dram, y_dram)
        combine(nc, gates, raw, y_dram, out)


_INS = ["x", "norm1_g", "w_in", "q_norm_g", "k_norm_g", "w_attn_out", "w_pool_mix", "pool_scale", "w_pool_out", "w_o",
        "norm2_g", "w_router_group", "b_router_group", "w_router_expert", "b_router_expert", "w_exp_gate",
        "w_exp_up", "w_exp_down"]
_OUTS = [((1, S, D), "float32")]


def kernel(**inputs):
    import numpy as _np
    import concourse.bacc as _bacc
    from concourse import mybir as _mybir
    from concourse.bass_utils import run_bass_kernel_spmd as _run

    nc = _bacc.Bacc("TRN2", target_bir_lowering=False, num_devices=1)
    arrays, args = {}, []
    for name, a in [(n, _np.ascontiguousarray(inputs[n])) for n in _INS] + [("shape_constants", shape_constants())]:
        arrays[f"in_{name}_dram"] = a
        args.append(nc.dram_tensor(f"in_{name}_dram", a.shape, _mybir.dt.from_np(a.dtype), kind="ExternalInput").ap())
    for i, (shape, dtype) in enumerate(_OUTS):
        dt = _mybir.dt.from_np(_np.dtype(dtype))
        args.append(nc.dram_tensor(f"out_{i}_dram", shape, dt, kind="ExternalOutput").ap())
    decoder_layer(nc, *args)
    r = _run(nc, [arrays], core_ids=[0])
    return r.results[0]["out_0_dram"]
```
